# Optimizing a Trainium2 kernel written in Bass

```python
import math
import jax, jax.numpy as jnp
from jax import lax
import numpy as np
import math, functools

D_MODEL = 1024
BATCH = 1
SEQ = 256
DEPTH = 1

A_HEADS = 8
A_HEAD_DIM = 64
A_WIDTH = A_HEADS * A_HEAD_DIM
MOBA_BLOCK = 256
MOBA_TOPK = 3
MOBA_Q_CHUNK = 32
B_HEADS = 8
B_NOPE = 64
B_ROPE = 32
B_V = 64
B_WIDTH = B_HEADS * B_V
Q_LORA = 256
KV_LORA = 128
MLA_Q_BLOCK = 128
PEER_HEADS = 8
PEER_NKEYS = 128
PEER_EXPERTS = PEER_NKEYS * PEER_NKEYS
PEER_HALF = 128
PEER_QDIM = 2 * PEER_HALF
PEER_TOPK = 16
PEER_TOKEN_CHUNK = 128
ROPE_THETA = 10000.0
RMS_EPS = 1e-6
IN_WIDTHS = (A_WIDTH, A_WIDTH, A_WIDTH, Q_LORA, KV_LORA, B_ROPE, D_MODEL, D_MODEL)
IN_TOTAL = 3 * A_WIDTH + Q_LORA + KV_LORA + B_ROPE + 2 * D_MODEL


def rms_norm(x, g):
    xf = x.astype(jnp.float32)
    y = xf * lax.rsqrt(jnp.mean(xf * xf, axis=-1, keepdims=True) + RMS_EPS)
    return (y * g.astype(jnp.float32)).astype(x.dtype)

def rope_tables(positions, dim, dtype):
    inv_freq = ROPE_THETA ** (-jnp.arange(0, dim, 2, dtype=jnp.float32) / dim)
    ang = positions.astype(jnp.float32)[..., None] * inv_freq
    return jnp.cos(ang)[:, :, None, :].astype(dtype), jnp.sin(ang)[:, :, None, :].astype(dtype)

def apply_rope(x, cos, sin):
    x1, x2 = jnp.split(x, 2, axis=-1)
    return jnp.concatenate([x1 * cos - x2 * sin, x2 * cos + x1 * sin], axis=-1)

def moba_attention(q, k, v):
    B, S, H, dh = q.shape
    nb = -(-S // MOBA_BLOCK)
    pad = nb * MOBA_BLOCK - S
    k_eff = min(MOBA_TOPK, nb)
    scale = 1.0 / math.sqrt(dh)
    qt = q.transpose(0, 2, 1, 3)
    kt = jnp.pad(k.transpose(0, 2, 1, 3), ((0, 0), (0, 0), (0, pad), (0, 0)))
    vt = jnp.pad(v.transpose(0, 2, 1, 3), ((0, 0), (0, 0), (0, pad), (0, 0)))
    kb = kt.reshape(B, H, nb, MOBA_BLOCK, dh)
    vb = vt.reshape(B, H, nb, MOBA_BLOCK, dh)
    k_mean = jnp.mean(kb.astype(jnp.float32), axis=3)
    b_ix = jnp.arange(B)[:, None, None, None]
    h_ix = jnp.arange(H)[None, :, None, None]
    n_chunks = S // MOBA_Q_CHUNK

    def chunk(ci):
        start = ci * MOBA_Q_CHUNK
        blk = start // MOBA_BLOCK
        qc = lax.dynamic_slice_in_dim(qt, start, MOBA_Q_CHUNK, axis=2)
        gate = jnp.einsum('bhqd,bhnd->bhqn', qc.astype(jnp.float32), k_mean)
        gate = jnp.where(jnp.arange(nb) < blk, gate, -jnp.inf)
        _, sel = lax.top_k(gate, k_eff)
        sel_valid = jnp.arange(k_eff) < blk
        k_sel = kb[b_ix, h_ix, sel]
        v_sel = vb[b_ix, h_ix, sel]
        s_sel = jnp.einsum('bhqd,bhqtkd->bhqtk', qc, k_sel).astype(jnp.float32) * scale
        s_sel = jnp.where(sel_valid[:, None], s_sel, -jnp.inf)
        s_sel = s_sel.reshape(B, H, MOBA_Q_CHUNK, k_eff * MOBA_BLOCK)
        k_own = lax.dynamic_index_in_dim(kb, blk, axis=2, keepdims=False)
        v_own = lax.dynamic_index_in_dim(vb, blk, axis=2, keepdims=False)
        s_own = jnp.einsum('bhqd,bhkd->bhqk', qc, k_own).astype(jnp.float32) * scale
        q_pos = start + jnp.arange(MOBA_Q_CHUNK)
        k_pos = blk * MOBA_BLOCK + jnp.arange(MOBA_BLOCK)
        s_own = jnp.where(k_pos[None, :] <= q_pos[:, None], s_own, -jnp.inf)
        p = jax.nn.softmax(jnp.concatenate([s_sel, s_own], axis=-1), axis=-1).astype(v.dtype)
        p_sel = p[..., :k_eff * MOBA_BLOCK].reshape(B, H, MOBA_Q_CHUNK, k_eff, MOBA_BLOCK)
        p_own = p[..., k_eff * MOBA_BLOCK:]
        return (jnp.einsum('bhqtk,bhqtkd->bhqd', p_sel, v_sel)
                + jnp.einsum('bhqk,bhkd->bhqd', p_own, v_own))

    out = lax.map(chunk, jnp.arange(n_chunks))
    return out.transpose(1, 0, 3, 2, 4).reshape(B, S, H * dh)

def causal_attention_blocks(q, k, v, scale):
    B, H, S, _ = q.shape
    dv = v.shape[-1]
    k_pos = jnp.arange(S)

    def block(bi):
        qb = lax.dynamic_slice_in_dim(q, bi * MLA_Q_BLOCK, MLA_Q_BLOCK, axis=2)
        s = jnp.einsum('bhqd,bhkd->bhqk', qb, k).astype(jnp.float32) * scale
        q_pos = bi * MLA_Q_BLOCK + jnp.arange(MLA_Q_BLOCK)
        s = jnp.where(k_pos[None, :] <= q_pos[:, None], s, -jnp.inf)
        p = jax.nn.softmax(s, axis=-1).astype(v.dtype)
        return jnp.einsum('bhqk,bhkd->bhqd', p, v)

    out = lax.map(block, jnp.arange(S // MLA_Q_BLOCK))
    return out.transpose(1, 0, 3, 2, 4).reshape(B, S, H * dv)

def mla_attention(c_q, c_kv, k_pe, q_norm_g, w_q_up, kv_norm_g, w_kv_up, cos_b, sin_b):
    B, S, _ = c_q.shape
    q = (rms_norm(c_q, q_norm_g) @ w_q_up).reshape(B, S, B_HEADS, B_NOPE + B_ROPE)
    q_nope, q_pe = q[..., :B_NOPE], q[..., B_NOPE:]
    q_pe = apply_rope(q_pe, cos_b, sin_b)
    kv = (rms_norm(c_kv, kv_norm_g) @ w_kv_up).reshape(B, S, B_HEADS, B_NOPE + B_V)
    k_nope, v = kv[..., :B_NOPE], kv[..., B_NOPE:]
    k_pe = apply_rope(k_pe[:, :, None, :], cos_b, sin_b)
    k_pe = jnp.broadcast_to(k_pe, (B, S, B_HEADS, B_ROPE))
    q_full = jnp.concatenate([q_nope, q_pe], axis=-1).transpose(0, 2, 1, 3)
    k_full = jnp.concatenate([k_nope, k_pe], axis=-1).transpose(0, 2, 1, 3)
    v = v.transpose(0, 2, 1, 3)
    return causal_attention_blocks(q_full, k_full, v, 1.0 / math.sqrt(B_NOPE + B_ROPE))

def peer_ffn(h, w_query, sub_keys_1, sub_keys_2, expert_u, expert_v):
    B, S, D = h.shape
    T = B * S
    hc = h.reshape(T // PEER_TOKEN_CHUNK, PEER_TOKEN_CHUNK, D)

    def chunk(xc):
        q = (xc @ w_query).reshape(PEER_TOKEN_CHUNK, PEER_HEADS, 2, PEER_HALF)
        s1 = jnp.einsum('thd,hnd->thn', q[:, :, 0], sub_keys_1).astype(jnp.float32)
        s2 = jnp.einsum('thd,hnd->thn', q[:, :, 1], sub_keys_2).astype(jnp.float32)
        v1, i1 = lax.top_k(s1, PEER_TOPK)
        v2, i2 = lax.top_k(s2, PEER_TOPK)
        cand = (v1[..., :, None] + v2[..., None, :]).reshape(PEER_TOKEN_CHUNK, PEER_HEADS, PEER_TOPK * PEER_TOPK)
        cand_idx = (i1[..., :, None] * PEER_NKEYS + i2[..., None, :]).reshape(PEER_TOKEN_CHUNK, PEER_HEADS, PEER_TOPK * PEER_TOPK)
        best, pos = lax.top_k(cand, PEER_TOPK)
        idx = jnp.take_along_axis(cand_idx, pos, axis=-1)
        g = jax.nn.softmax(best, axis=-1)
        u = expert_u[idx]
        act = jax.nn.gelu(jnp.einsum('td,thkd->thk', xc, u).astype(jnp.float32), approximate=False)
        w = (g * act).astype(h.dtype)
        return jnp.einsum('thk,thkd->td', w, expert_v[idx])

    return lax.map(chunk, hc).reshape(B, S, D)

def first_inputs(seed: int = 0) -> dict:
    key = jax.random.key(seed)
    ks = jax.random.split(key, 20)
    f32 = jnp.float32
    L = DEPTH

    def nrm(k, shape, scale):
        return jax.random.normal(k, shape, f32) * scale

    def gain(k, shape):
        return 1.0 + 0.02 * jax.random.normal(k, shape, f32)

    x = jax.random.normal(ks[0], (BATCH, SEQ, D_MODEL), f32)
    positions = jnp.broadcast_to(jnp.arange(SEQ, dtype=jnp.int32), (BATCH, SEQ))
    return {
        "x": x,
        "positions": positions,
        "mix_norm_g": gain(ks[1], (L, D_MODEL)),
        "w_in": nrm(ks[2], (L, D_MODEL, IN_TOTAL), D_MODEL ** -0.5),
        "q_norm_g": gain(ks[3], (L, Q_LORA)),
        "w_q_up": nrm(ks[4], (L, Q_LORA, B_HEADS * (B_NOPE + B_ROPE)), Q_LORA ** -0.5),
        "kv_norm_g": gain(ks[5], (L, KV_LORA)),
        "w_kv_up": nrm(ks[6], (L, KV_LORA, B_HEADS * (B_NOPE + B_V)), KV_LORA ** -0.5),
        "w_branch_a": nrm(ks[7], (L, A_WIDTH, D_MODEL), A_WIDTH ** -0.5),
        "w_branch_b": nrm(ks[8], (L, B_WIDTH, D_MODEL), B_WIDTH ** -0.5),
        "w_out": nrm(ks[9], (L, D_MODEL, D_MODEL), D_MODEL ** -0.5),
        "ffn_norm_g": gain(ks[10], (L, D_MODEL)),
        "w_peer_query": nrm(ks[11], (L, D_MODEL, PEER_HEADS * PEER_QDIM), D_MODEL ** -0.5),
        "peer_sub_keys_1": nrm(ks[12], (L, PEER_HEADS, PEER_NKEYS, PEER_HALF), PEER_HALF ** -0.5),
        "peer_sub_keys_2": nrm(ks[13], (L, PEER_HEADS, PEER_NKEYS, PEER_HALF), PEER_HALF ** -0.5),
        "peer_expert_u": nrm(ks[14], (L, PEER_EXPERTS, D_MODEL), D_MODEL ** -0.5),
        "peer_expert_v": nrm(ks[15], (L, PEER_EXPERTS, D_MODEL), (PEER_HEADS * PEER_TOPK) ** -0.5),
        "final_norm_g": gain(ks[16], (D_MODEL,)),
    }

def first_block(x, positions, mix_norm_g, w_in, q_norm_g, w_q_up, kv_norm_g, w_kv_up,
              w_branch_a, w_branch_b, w_out, ffn_norm_g, w_peer_query, peer_sub_keys_1,
              peer_sub_keys_2, peer_expert_u, peer_expert_v, final_norm_g):
    B, S, _ = x.shape
    cos_a, sin_a = rope_tables(positions, A_HEAD_DIM, x.dtype)
    cos_b, sin_b = rope_tables(positions, B_ROPE, x.dtype)
    splits = [sum(IN_WIDTHS[:i + 1]) for i in range(len(IN_WIDTHS) - 1)]
    for layer in range(DEPTH):
        h = rms_norm(x, mix_norm_g[layer])
        proj = h @ w_in[layer]
        q_a, k_a, v_a, c_q, c_kv, k_pe, gate_a, gate_b = jnp.split(proj, splits, axis=-1)
        q_a = apply_rope(q_a.reshape(B, S, A_HEADS, A_HEAD_DIM), cos_a, sin_a)
        k_a = apply_rope(k_a.reshape(B, S, A_HEADS, A_HEAD_DIM), cos_a, sin_a)
        v_a = v_a.reshape(B, S, A_HEADS, A_HEAD_DIM)
        y_a = moba_attention(q_a, k_a, v_a)
        y_b = mla_attention(c_q, c_kv, k_pe, q_norm_g[layer], w_q_up[layer],
                            kv_norm_g[layer], w_kv_up[layer], cos_b, sin_b)
        merged = (jax.nn.sigmoid(gate_a) * (y_a @ w_branch_a[layer])
                  + jax.nn.sigmoid(gate_b) * (y_b @ w_branch_b[layer]))
        x = x + merged @ w_out[layer]
        x = x + peer_ffn(rms_norm(x, ffn_norm_g[layer]), w_peer_query[layer],
                         peer_sub_keys_1[layer], peer_sub_keys_2[layer],
                         peer_expert_u[layer], peer_expert_v[layer])
    return rms_norm(x, final_norm_g)


DEPTH_2 = 2

PLE_DIM = 256
N_EVEN = (DEPTH_2 + 1) // 2
N_ODD = DEPTH_2 // 2
A_WIDTH_2 = D_MODEL // 2
A_GROUPS = 4
A_GROUP_DIM = A_WIDTH_2 // A_GROUPS
A_CHUNK = 128
B_HEADS_2 = 4
B_HEAD_DIM = (D_MODEL // 2) // B_HEADS_2
B_WIDTH_2 = B_HEADS_2 * B_HEAD_DIM
B_CONV = 4
B_CHUNK = 64
C_HEADS = 8
C_HEAD_DIM = D_MODEL // (2 * C_HEADS)
C_VALUE_DIM = 2 * C_HEAD_DIM
Q_BLOCK = 128
D_FF = 4 * D_MODEL
EVEN_IN = 2 * A_WIDTH_2 + 4 * B_WIDTH_2 + 2 * B_HEADS_2
NORM_EPS = 1e-6
RES_SCALE = 0.5


def rms_norm_2(x, gain):
    xf = x.astype(jnp.float32)
    y = xf * lax.rsqrt(jnp.mean(xf * xf, axis=-1, keepdims=True) + NORM_EPS)
    return (y * gain.astype(jnp.float32)).astype(x.dtype)

def layer_norm(x, gain):
    xf = x.astype(jnp.float32)
    xc = xf - jnp.mean(xf, axis=-1, keepdims=True)
    y = xc * lax.rsqrt(jnp.mean(xc * xc, axis=-1, keepdims=True) + NORM_EPS)
    return (y * gain.astype(jnp.float32)).astype(x.dtype)

def l2_normalize(x):
    xf = x.astype(jnp.float32)
    return xf * lax.rsqrt(jnp.sum(xf * xf, axis=-1, keepdims=True) + NORM_EPS)

def causal_depthwise_conv(x, w):
    k_len, ch = w.shape
    return lax.conv_general_dilated(
        x, w[:, None, :].astype(x.dtype), window_strides=(1,), padding=[(k_len - 1, 0)],
        dimension_numbers=('NWC', 'WIO', 'NWC'), feature_group_count=ch)

def gmlp_spatial_gate(uv, v_gain, w_s, b_s):
    bsz, seq, _ = uv.shape
    u, v = jnp.split(uv, 2, axis=-1)
    v = v.reshape(bsz, seq // A_CHUNK, A_CHUNK, A_GROUPS, A_GROUP_DIM)
    v = layer_norm(v, v_gain.reshape(A_GROUPS, A_GROUP_DIM))
    causal = jnp.tril(jnp.ones((A_CHUNK, A_CHUNK), dtype=bool))
    w = jnp.where(causal, w_s, 0.0)
    s = jnp.einsum('gts,bnsgc->bntgc', w, v) + b_s.T[None, None, :, :, None]
    return u * s.reshape(bsz, seq, A_WIDTH_2)

def chunk_gated_delta_rule(q, k, v, g, beta):
    bsz, seq, heads, dk = q.shape
    dv = v.shape[-1]
    c = B_CHUNK
    n = seq // c
    f32 = jnp.float32

    def chunks(t):
        t = t.astype(f32).reshape((bsz, n, c, heads) + t.shape[3:])
        return jnp.moveaxis(t, 3, 1)

    q, k, v, g, beta = chunks(q), chunks(k), chunks(v), chunks(g), chunks(beta)
    gc = jnp.cumsum(g, axis=-1)
    causal = jnp.tril(jnp.ones((c, c), dtype=bool))
    strict = jnp.tril(jnp.ones((c, c), dtype=bool), k=-1)
    diff = gc[..., :, None] - gc[..., None, :]
    decay = jnp.where(causal, jnp.exp(jnp.where(causal, diff, 0.0)), 0.0)
    k_beta = k * beta[..., None]
    v_beta = v * beta[..., None]
    a = jnp.where(strict, jnp.einsum('bhnid,bhnjd->bhnij', k_beta, k) * decay, 0.0)
    t_mat = a + jnp.eye(c, dtype=f32)
    solve = functools.partial(lax.linalg.triangular_solve, left_side=True, lower=True,
                              unit_diagonal=True)
    u = solve(t_mat, v_beta)
    w = solve(t_mat, k_beta * jnp.exp(gc)[..., None])
    qk = jnp.einsum('bhnid,bhnjd->bhnij', q, k) * decay
    q_dec = q * jnp.exp(gc)[..., None]
    k_dec = k * jnp.exp(gc[..., -1:] - gc)[..., None]
    g_last = jnp.exp(gc[..., -1])
    xs = tuple(jnp.moveaxis(t, 2, 0) for t in (q_dec, k_dec, u, w, qk, g_last))

    def step(state, inp):
        q_c, k_c, u_c, w_c, qk_c, gl_c = inp
        v_new = u_c - jnp.einsum('bhck,bhkv->bhcv', w_c, state)
        o_c = (jnp.einsum('bhck,bhkv->bhcv', q_c, state)
               + jnp.einsum('bhij,bhjv->bhiv', qk_c, v_new))
        state = state * gl_c[..., None, None] + jnp.einsum('bhck,bhcv->bhkv', k_c, v_new)
        return state, o_c

    state0 = jnp.zeros((bsz, heads, dk, dv), f32)
    _, o = lax.scan(step, state0, xs)
    return jnp.transpose(o, (1, 0, 3, 2, 4)).reshape(bsz, seq, heads, dv)

def gated_deltanet(qkv, z, beta_logit, a_logit, conv_w, a_log, dt_bias, out_gain):
    bsz, seq, _ = qkv.shape
    qkv = jax.nn.silu(causal_depthwise_conv(qkv, conv_w))
    q, k, v = jnp.split(qkv, 3, axis=-1)
    shp = (bsz, seq, B_HEADS_2, B_HEAD_DIM)
    q = l2_normalize(q.reshape(shp)) * (B_HEAD_DIM ** -0.5)
    k = l2_normalize(k.reshape(shp))
    v = v.reshape(shp)
    beta = jax.nn.sigmoid(beta_logit.astype(jnp.float32))
    g = -jnp.exp(a_log.astype(jnp.float32)) * jax.nn.softplus(
        a_logit.astype(jnp.float32) + dt_bias.astype(jnp.float32))
    o = chunk_gated_delta_rule(q, k, v, g, beta).astype(qkv.dtype)
    o = rms_norm_2(o, out_gain) * jax.nn.silu(z.reshape(shp))
    return o.reshape(bsz, seq, B_WIDTH_2)

def alibi_slopes(heads):
    return 2.0 ** (-8.0 * jnp.arange(1, heads + 1, dtype=jnp.float32) / heads)

def diff_attention(qkv, q_gain, k_gain, lam_params, sub_gain, lam_init):
    bsz, seq, _ = qkv.shape
    q, k, v = jnp.split(qkv, 3, axis=-1)
    q = rms_norm_2(q.reshape(bsz, seq, C_HEADS, 2, C_HEAD_DIM), q_gain) * (C_HEAD_DIM ** -0.5)
    k = rms_norm_2(k.reshape(bsz, seq, C_HEADS, 2, C_HEAD_DIM), k_gain)
    v = v.reshape(bsz, seq, C_HEADS, C_VALUE_DIM)
    lp = lam_params.astype(jnp.float32)
    lam = jnp.exp(jnp.sum(lp[0] * lp[1])) - jnp.exp(jnp.sum(lp[2] * lp[3])) + lam_init
    slopes = alibi_slopes(C_HEADS)[None, :, None, None, None]
    nblk = seq // Q_BLOCK
    qb = jnp.moveaxis(q.reshape(bsz, nblk, Q_BLOCK, C_HEADS, 2, C_HEAD_DIM), 1, 0)
    kpos = jnp.arange(seq)

    def attend(args):
        q_blk, blk = args
        qpos = blk * Q_BLOCK + jnp.arange(Q_BLOCK)
        dist = (qpos[:, None] - kpos[None, :]).astype(jnp.float32)
        logits = jnp.einsum('bqhrd,bkhrd->bhrqk', q_blk, k).astype(jnp.float32) - slopes * dist
        logits = jnp.where(dist >= 0, logits, -jnp.inf)
        probs = jax.nn.softmax(logits, axis=-1)
        attn = probs[:, :, 0] - lam * probs[:, :, 1]
        return jnp.einsum('bhqk,bkhe->bqhe', attn.astype(v.dtype), v)

    o = lax.map(attend, (qb, jnp.arange(nblk)))
    o = jnp.moveaxis(o, 0, 1).reshape(bsz, seq, C_HEADS, C_VALUE_DIM)
    o = rms_norm_2(o, sub_gain) * (1.0 - lam_init)
    return o.reshape(bsz, seq, C_HEADS * C_VALUE_DIM)

def second_inputs(seed: int = 0) -> dict:
    key = jax.random.key(seed)
    ks = jax.random.split(key, 32)
    f32 = jnp.float32

    def normal(k, shape, scale):
        return jax.random.normal(k, shape, f32) * scale

    def gain(k, shape):
        return 1.0 + 0.1 * jax.random.normal(k, shape, f32)

    dt = jnp.exp(jax.random.uniform(ks[9], (N_EVEN, B_HEADS_2), f32,
                                    minval=math.log(1e-3), maxval=math.log(1e-1)))
    return {
        'x': normal(ks[0], (BATCH, SEQ, D_MODEL), 1.0),
        'p': normal(ks[1], (DEPTH_2, BATCH, SEQ, PLE_DIM), 1.0),
        'ln_mix_e': gain(ks[2], (N_EVEN, D_MODEL)),
        'w_in_e': normal(ks[3], (N_EVEN, D_MODEL, EVEN_IN), D_MODEL ** -0.5),
        'gmlp_v_gain': gain(ks[4], (N_EVEN, A_WIDTH_2)),
        'gmlp_ws': normal(ks[5], (N_EVEN, A_GROUPS, A_CHUNK, A_CHUNK), A_CHUNK ** -0.5),
        'gmlp_bs': gain(ks[6], (N_EVEN, A_GROUPS, A_CHUNK)),
        'gdn_conv': normal(ks[7], (N_EVEN, B_CONV, 3 * B_WIDTH_2), B_CONV ** -0.5),
        'gdn_a_log': jnp.log(jax.random.uniform(ks[8], (N_EVEN, B_HEADS_2), f32, minval=1.0, maxval=16.0)),
        'gdn_dt_bias': dt + jnp.log(-jnp.expm1(-dt)),
        'gdn_out_gain': gain(ks[10], (N_EVEN, B_HEAD_DIM)),
        'w_out_e': normal(ks[11], (N_EVEN, A_WIDTH_2 + B_WIDTH_2, D_MODEL), (A_WIDTH_2 + B_WIDTH_2) ** -0.5 * RES_SCALE),
        'ln_mix_o': gain(ks[12], (N_ODD, D_MODEL)),
        'w_qkv_o': normal(ks[13], (N_ODD, D_MODEL, 3 * C_HEADS * C_VALUE_DIM), D_MODEL ** -0.5),
        'attn_q_gain': gain(ks[14], (N_ODD, C_HEAD_DIM)),
        'attn_k_gain': gain(ks[15], (N_ODD, C_HEAD_DIM)),
        'diff_lambda': normal(ks[16], (N_ODD, 4, C_HEAD_DIM), 0.1),
        'attn_sub_gain': gain(ks[17], (N_ODD, C_VALUE_DIM)),
        'w_out_o': normal(ks[18], (N_ODD, C_HEADS * C_VALUE_DIM, D_MODEL), (C_HEADS * C_VALUE_DIM) ** -0.5 * RES_SCALE),
        'ln_mlp': gain(ks[19], (DEPTH_2, D_MODEL)),
        'w_mlp1': normal(ks[20], (DEPTH_2, D_MODEL, D_FF), D_MODEL ** -0.5),
        'w_mlp2': normal(ks[21], (DEPTH_2, D_FF, D_MODEL), D_FF ** -0.5 * RES_SCALE),
        'ln_ple': gain(ks[22], (DEPTH_2, D_MODEL)),
        'w_ple_gate': normal(ks[23], (DEPTH_2, D_MODEL, D_MODEL), D_MODEL ** -0.5),
        'w_ple_proj': normal(ks[24], (DEPTH_2, PLE_DIM, D_MODEL), PLE_DIM ** -0.5 * RES_SCALE),
    }

def second_block(x, p, ln_mix_e, w_in_e, gmlp_v_gain, gmlp_ws, gmlp_bs, gdn_conv, gdn_a_log,
              gdn_dt_bias, gdn_out_gain, w_out_e, ln_mix_o, w_qkv_o, attn_q_gain, attn_k_gain,
              diff_lambda, attn_sub_gain, w_out_o, ln_mlp, w_mlp1, w_mlp2, ln_ple, w_ple_gate,
              w_ple_proj):
    split_at = [2 * A_WIDTH_2, 2 * A_WIDTH_2 + 3 * B_WIDTH_2, 2 * A_WIDTH_2 + 4 * B_WIDTH_2,
                2 * A_WIDTH_2 + 4 * B_WIDTH_2 + B_HEADS_2]
    h = x
    for layer in range(DEPTH_2):
        i = layer // 2
        if layer % 2 == 0:
            hn = rms_norm_2(h, ln_mix_e[i])
            proj = hn @ w_in_e[i]
            a_uv, b_qkv, b_z, b_beta, b_a = jnp.split(proj, split_at, axis=-1)
            a_out = gmlp_spatial_gate(jax.nn.gelu(a_uv), gmlp_v_gain[i], gmlp_ws[i], gmlp_bs[i])
            b_out = gated_deltanet(b_qkv, b_z, b_beta, b_a, gdn_conv[i], gdn_a_log[i],
                                   gdn_dt_bias[i], gdn_out_gain[i])
            h = h + jnp.concatenate([a_out, b_out], axis=-1) @ w_out_e[i]
        else:
            hn = rms_norm_2(h, ln_mix_o[i])
            lam_init = 0.8 - 0.6 * math.exp(-0.3 * layer)
            o = diff_attention(hn @ w_qkv_o[i], attn_q_gain[i], attn_k_gain[i], diff_lambda[i],
                               attn_sub_gain[i], lam_init)
            h = h + o @ w_out_o[i]
        hn = rms_norm_2(h, ln_mlp[layer])
        h = h + jnp.square(jax.nn.relu(hn @ w_mlp1[layer])) @ w_mlp2[layer]
        gate = jax.nn.sigmoid(rms_norm_2(h, ln_ple[layer]) @ w_ple_gate[layer])
        h = h + (p[layer] @ w_ple_proj[layer]) * gate
    return h


def setup_inputs(seed=0):
    out = dict(first_inputs(seed))
    for name, value in second_inputs(seed + 1).items():
        if name != "x":
            out[name + "_2"] = value
    return out


def reference(
    x, positions, mix_norm_g, w_in, q_norm_g, w_q_up, kv_norm_g, w_kv_up, w_branch_a,
    w_branch_b, w_out, ffn_norm_g, w_peer_query, peer_sub_keys_1, peer_sub_keys_2,
    peer_expert_u, peer_expert_v, final_norm_g, p_2, ln_mix_e_2, w_in_e_2, gmlp_v_gain_2,
    gmlp_ws_2, gmlp_bs_2, gdn_conv_2, gdn_a_log_2, gdn_dt_bias_2, gdn_out_gain_2, w_out_e_2,
    ln_mix_o_2, w_qkv_o_2, attn_q_gain_2, attn_k_gain_2, diff_lambda_2, attn_sub_gain_2,
    w_out_o_2, ln_mlp_2, w_mlp1_2, w_mlp2_2, ln_ple_2, w_ple_gate_2, w_ple_proj_2,
):
    x = first_block(
        x, positions, mix_norm_g, w_in, q_norm_g, w_q_up, kv_norm_g, w_kv_up, w_branch_a,
        w_branch_b, w_out, ffn_norm_g, w_peer_query, peer_sub_keys_1, peer_sub_keys_2,
        peer_expert_u, peer_expert_v, final_norm_g,
    )
    return second_block(
        x, p_2, ln_mix_e_2, w_in_e_2, gmlp_v_gain_2, gmlp_ws_2, gmlp_bs_2, gdn_conv_2,
        gdn_a_log_2, gdn_dt_bias_2, gdn_out_gain_2, w_out_e_2, ln_mix_o_2, w_qkv_o_2,
        attn_q_gain_2, attn_k_gain_2, diff_lambda_2, attn_sub_gain_2, w_out_o_2, ln_mlp_2,
        w_mlp1_2, w_mlp2_2, ln_ple_2, w_ple_gate_2, w_ple_proj_2,
    )


_drawn_inputs = setup_inputs


def setup_inputs(seed=0):
    import zlib

    import numpy as np

    out = dict(_drawn_inputs(seed))
    spreads = {}
    factors = {'mix_norm_g': 7.725,
     'q_norm_g': 8.0,
     'kv_norm_g': 8.0,
     'ffn_norm_g': 26.08,
     'gmlp_v_gain_2': 3.643,
     'gdn_a_log_2': 3.092,
     'attn_q_gain_2': 2.991,
     'attn_k_gain_2': 3.301,
     'diff_lambda_2': 5.582,
     'ln_ple_2': 5.002}
    for name, (base, spread) in spreads.items():
        noise = np.random.default_rng([zlib.crc32(name.encode()), seed]).standard_normal(out[name].shape)
        drawn = base * np.exp(spread * noise) if base else spread * noise
        out[name] = __import__('jax').numpy.asarray(drawn.astype(out[name].dtype))
    for name, factor in factors.items():
        out[name] = (out[name] * factor).astype(out[name].dtype)
    return out
```

```python
from contextlib import ExitStack
import math

import numpy as np
import concourse.bass as bass
from concourse import mybir

F32 = mybir.dt.float32
F32R = mybir.dt.float32r
U32 = mybir.dt.uint32
I32 = mybir.dt.int32
ACT = mybir.ActivationFunctionType
ALU = mybir.AluOpType
AX_X = mybir.AxisListType.X

P = 128
SEQ, D = 256, 1024
NT = SEQ // P
KD = D // P
NEG = -1e30
LOWEST = -3.0e38
EPS = 1e-6

A_H, A_DH = 8, 64
B_H, B_NOPE, B_ROPE, B_V = 8, 64, 32, 64
B_DK = B_NOPE + B_ROPE
Q_LORA, KV_LORA = 256, 128
VC_W = 512 + Q_LORA + KV_LORA + B_ROPE
PE_H, NKEYS, TOPK = 8, 128, 16
G_H, G_DK, G_CH = 4, 128, 64
M_G = 4
C_H, C_DH = 8, 64
ROUND = 1.5 * 2.0 ** 23
TURN = [6.28125, 0.00193500518798828125, 2 * math.pi - 6.28125 - 0.00193500518798828125]
D_FF = 4 * D
PLE = 256
LAM_INIT = 0.8 - 0.6 * math.exp(-0.3)

RING = 4
AHEAD = 3

GAINS = ["mix", "ffn", "ln_e", "mlp0", "ple0", "ln_o", "mlp1", "ple1"]
C_QN = 8 * len(GAINS)
C_KVN = C_QN + 2
C_CONV = C_KVN + 1
C_BS = C_CONV + 48
C_ALL = C_BS + 4
R_FINAL = 0
R_VG = R_FINAL + D
R_OG = R_VG + 512
R_QG = R_OG + 128
R_KG = R_QG + 64
R_SG = R_KG + 64
R_LAM = R_SG + 128
R_ALOG = R_LAM + 256
R_DT = R_ALOG + 4
R_ALL = R_DT + 4
N_FREQ = A_DH // 2 + B_ROPE // 2
ROWS_OVER = -(-R_ALL // SEQ)


def chunk_plan():
    plan, first = [], {}

    def rows(name, src, blocks, c0, width):
        first[name] = len(plan)
        plan.extend((src, "row", k, c0, width) for k in blocks)

    def cols(name, src, blocks):
        first[name] = len(plan)
        plan.extend((src, "col", n, 0, D) for n in blocks)

    rows("qk", "w_in", range(KD), 0, 1024)
    rows("vc", "w_in", range(KD), 1024, VC_W)
    rows("ga", "w_in", range(KD), 1024 + VC_W, 1024)
    rows("gb", "w_in", range(KD), 2048 + VC_W, 1024)
    rows("qup", "w_q_up", range(2), 0, B_H * B_DK)
    rows("kvup", "w_kv_up", range(1), 0, B_H * (B_NOPE + B_V))
    rows("br_a", "w_branch_a", range(4), 0, D)
    rows("br_b", "w_branch_b", range(4), 0, D)
    rows("wout", "w_out", range(KD), 0, D)
    cols("query", "w_query", range(16))
    cols("u", "expert_u", range(NKEYS))
    rows("v", "expert_v", range(NKEYS), 0, D)
    cols("qkv_e", "w_qkv_e", range(12))
    rows("zba", "w_in_e", range(KD), 2560, 520)
    rows("uv", "w_in_e", range(KD), 0, 1024)
    rows("out_e", "w_out_e", range(KD), 0, D)
    for layer in range(2):
        if layer:
            for n, name in enumerate(("q1", "k1", "v1")):
                rows(name, "w_qkv_o", range(KD), n * D, D)
            rows("out_o", "w_out_o", range(KD), 0, D)
        first[f"mlp{layer}"] = len(plan)
        for f in range(D_FF // P + 1):
            if f < D_FF // P:
                plan.append((f"w_mlp1_{layer}", "col", f, 0, D))
            if f:
                plan.append((f"w_mlp2_{layer}", "row", f - 1, 0, D))
        rows(f"gate{layer}", f"w_gate_{layer}", range(KD), 0, D)
        rows(f"ple{layer}", f"w_ple_{layer}", range(PLE // P), 0, D)
    return plan, first


PLAN, FIRST = chunk_plan()
GROUPS = ["qk", "vc", "ga", "gb", "qup", "kvup", "br_a", "br_b", "wout", "v", "zba", "uv", "out_e",
          "mlp0", "gate0", "ple0", "q1", "k1", "v1", "out_o", "mlp1", "gate1", "ple1"]
U0, V0 = FIRST["u"], FIRST["v"]
HALF = NKEYS // 2

MLP_SKIP = 3
MLP_ROUNDS = (D_FF // P - 2) // 2
LOOPS = {U0: NKEYS // 4, V0: NKEYS // 4}
LOOPS.update({FIRST[f"mlp{n}"] + MLP_SKIP: MLP_ROUNDS for n in range(2)})


SOLVE = [
    ("a", "kbT", "kT", -1), ("aT", "kT", "kbT", -1),
    ("N2", "N1T", "N1", 1), ("N2T", "N1", "N1T", 1),
    ("Y+", "YT", "N2", 2), ("YT+", "N2", "YT", 2),
    ("N4", "N2T", "N2", 3), ("N4T", "N2", "N2T", 3),
    ("Y+", "YT", "N4", 6), ("YT+", "N4", "YT", 6),
    ("N8", "N4T", "N4", 7),
    ("Y+", "YT", "N8", 10), ("YT+", "N8", "YT", 10),
    ("P1", "L1T", "Y", 11),
    ("Y-", "YT", "P1", 13), ("YT-", "P1", "YT", 13),
    ("P2", "L2T", "Y", 14),
    ("YT-", "P2", "YT", 16),
    ("u", "YT", "VB", 17), ("wT", "KBE", "YT", 17), ("qkT", "kT", "qT", -1),
]


def share(semaphore, signals):
    base, shared = 0, {}
    for name, count in signals:
        shared[name] = (semaphore, base)
        base += count
    return shared


SHARED = {
    **share("acc_read_dve", [("ev_" + g, 4) for g in (
        "qk", "vc", "qup", "kvup", "br_a", "br_b", "wout", "v", "out_e", "mlp0", "ple0", "q1", "k1",
        "v1", "out_o", "mlp1", "ple1")]),
    **share("acc_read_act", [("ev_" + g, 4) for g in ("ga", "gb", "zba", "uv", "gate0", "gate1")]),
    **share("filled", [("c_T", 2), ("qa_T", 4), ("qb_T", 8), ("pT", 16), ("y_T", 4), ("m_T", 4),
                       ("pk_T", 2), ("tok_T", 6), ("fT_T", 8), ("oc_T", 4), ("qk1_T", 8), ("aT", 8),
                       ("o1_T", 4)]),
    **share("fill_read_dve", [("qa_E", 4), ("qb_E", 8), ("y_E", 4), ("m_E", 4), ("pk_E", 2),
                              ("tok_E", 6), ("fT_E", 8), ("oc_E", 4), ("qk1_E", 8), ("o1_E", 4)]),
    **share("fill_read_act", [("pT_E", 16), ("aT_E", 8)]),
    **share("small_act", [("trig", 1), ("crms", 2), ("best_exp", 1), ("beta", 2), ("sp_exp", 1),
                          ("sp_ln", 1), ("l2_root", 1), ("egc", 1), ("o_root", 1), ("v_root", 1),
                          ("lam_exp", 1), ("qk_root", 2), ("o1_root", 1)]),
    **share("small_dve", [("angles", 1), ("cn", 1), ("rope_a", 1), ("cT", 3), ("rope_q", 1),
                          ("rope_k", 1), ("rope_b", 2), ("y", 4), ("best", 1), ("picks", 1),
                          ("x_final", 4), ("sp", 2), ("g_ready", 1), ("l2", 1), ("tokmaps", 1),
                          ("o_ss", 1), ("v_ss", 1), ("gv", 1), ("oc", 1), ("lam_dots", 2),
                          ("o1_ss", 1), ("o1", 1)]),
    **share("small_pe", [("gcT", 2), ("gcrow", 2), ("mix", 2)]),
}


def program(nc, ins, out):
    ctx = ExitStack()
    with ctx:
        base = -(-nc.sbuf_base // 32) * 32

        def at(name, offset, shape, dtype=F32):
            return nc.alloc_sbuf_tensor_at(name, shape, dtype, offset=base + offset)

        sems = {}

        def sem(name):
            name = SHARED.get(name, (name, 0))[0]
            if name not in sems:
                sems[name] = ctx.enter_context(nc.semaphore(name))
            return sems[name]

        def upto(name, value):
            return value + SHARED.get(name, (name, 0))[1]

        KB = 1024
        BIG, HT, MISC = 48 * KB, 176 * KB, 192 * KB
        w_raw = at("w_raw", 0, [P, RING, 1024])
        w_hi = at("w_hi", 16 * KB, [P, RING, 1024], F32R)
        w_lo = at("w_lo", 32 * KB, [P, RING, 1024], F32R)
        hT_hi = at("hT_hi", HT, [P, KD, SEQ], F32R)
        hT_lo = at("hT_lo", HT + 8 * KB, [P, KD, SEQ], F32R)
        misc_at = [MISC]

        def small(name, shape, dtype=F32):
            size = 4 * int(np.prod(shape[1:]))
            t = at(name, misc_at[0], shape, dtype)
            misc_at[0] += -(-size // 32) * 32
            return t

        ident = small("ident", [P, P])
        iota_row = small("iota_row", [P, P])
        cols = small("cols", [P, C_ALL])
        GT_AT = misc_at[0]
        g_hi = small("g_hi", [P, SEQ], F32R)
        g_lo = small("g_lo", [P, SEQ], F32R)
        i1T = small("i1T", [P, SEQ])
        i2T = small("i2T", [P, SEQ])
        HOT2 = misc_at[0]
        hot2 = small("hot2", [P, 2, 4, NKEYS], F32R)
        IS1 = misc_at[0]
        is1 = small("is1", [P, 4, HALF])
        hot_hi = small("hot_hi", [P, 2, 4, HALF], F32R)
        hot_lo = small("hot_lo", [P, 2, 4, HALF], F32R)
        causal = at("causal", GT_AT, [P, 3 * P])
        causal1 = at("causal1", HOT2 + 2 * KB, [P, 3 * P])
        WST = at("WST", HOT2, [P, M_G, P])
        masks = at("masks", GT_AT, [P, 6, P])
        ones = at("ones", GT_AT + 3 * KB, [P, P])
        dist = at("dist", IS1, [P, 3 * P])
        ss = small("ss", [P, 2, 2])
        ms = small("ms", [P, 2])
        rstd = small("rstd", [P, 2])
        minus_half = small("minus_half", [P, 2])
        epsc = small("epsc", [P, 1])
        rows_f = small("rows_f", [P, N_FREQ])
        pos_i = small("pos_i", [P, 2], I32)
        pos_f = small("pos_f", [P, 2])
        stat = small("stat", [P, 64])
        sq16 = small("sq16", [P, 16])
        sq32 = small("sq32", [P, 32])
        gc = small("gc", [P, 8])
        egc = small("egc", [P, 8])
        gl = small("gl", [P, 16])
        mx1 = small("mx1", [P, 16, 2])
        sum1 = small("sum1", [P, 16, 2])
        assert base + misc_at[0] <= nc.sbuf_usable_end, misc_at[0]

        def big(name, kb, shape, dtype=F32):
            assert kb * KB + 4 * int(np.prod(shape[1:])) <= 128 * KB, name
            return at(name, BIG + int(kb * KB), shape, dtype)

        X = big("X", 120, [P, NT, D])
        XN = big("XN", 98, [P, NT, D])
        junk = big("junk", 106, [P, NT, D])
        QK = big("QK", 0, [P, NT, 16, 64])
        VC = big("VC", 8, [P, NT, VC_W])
        GA = big("GA", 16, [P, NT, D])
        GB = big("GB", 24, [P, NT, D])
        QR = big("QR", 32, [P, NT, 16, 64])
        QTA = big("QTA", 40, [P, 8, SEQ])
        QB = big("QB", 48, [P, NT, B_H, B_DK])
        KF = big("KF", 54, [P, NT, B_H, B_DK])
        VB = big("VB", 60, [P, NT, B_H, B_V])
        QTB = big("QTB", 64, [P, 2 * B_H, SEQ])
        Sm = big("Sm", 80, [P, 2, 3 * P])
        Pr = big("Pr", 83, [P, 2, 3 * P])
        PT = big("PT", 86, [P, 2, 3 * P])
        Y = big("Y", 90, [P, 2, NT, 8, 64])
        rope_t = big("rope_t", 114, [P, NT, 16, 32])
        rope_u = big("rope_u", 109, [P, NT, 16, 32])
        ang = big("ang", 118, [P, NT, 2, N_FREQ])
        ang_k = big("ang_k", 118.75, [P, NT, 2, N_FREQ])
        CN = big("CN", 106, [P, NT, 384])
        mx = big("mx", 119.5, [P, 16, 2])
        sums = big("sums", 119.625, [P, 16, 2])
        M = big("M", 0, [P, NT, D])
        M2 = big("M2", 32, [P, NT, D])
        cT_hi = big("cT_hi", 40, [P, 3, SEQ], F32R)
        cT_lo = big("cT_lo", 43, [P, 3, SEQ], F32R)
        act_e = big("act_e", 0, [P, NKEYS, SEQ])
        QPT = big("QPT", 64, [P, 16, SEQ])
        KST = big("KST", 80, [P, 16, NKEYS])
        SC = big("SC", 88, [P, NT, 16, NKEYS])
        tk_s2 = big("tk_s2", 104, [P, 256])
        tk_v = big("tk_v", 105, [P, NT, 16, TOPK])
        tk_i = big("tk_i", 107, [P, NT, 16, TOPK], U32)
        tk_if = big("tk_if", 109, [P, NT, 16, TOPK])
        tk_bv = big("tk_bv", 111, [P, NT, PE_H, TOPK])
        tk_bp = big("tk_bp", 112, [P, NT, PE_H, TOPK], U32)
        tk_pa = big("tk_pa", 113, [P, 2, NT, PE_H, TOPK], U32)
        tk_pf = big("tk_pf", 115, [P, 2, NT, PE_H, TOPK])
        tk_c = big("tk_c", 117, [P, 256])
        tk_sel = big("tk_sel", 118, [P, 2, NT, PE_H, TOPK])
        tk_e = big("tk_e", 96, [P, PE_H, TOPK, TOPK])
        W_hi = at("W_hi", HT, [P, 2, SEQ], F32R)
        W_lo = at("W_lo", HT + 2 * KB, [P, 2, SEQ], F32R)
        XB = at("XB", HT + 4 * KB, [P, NT, D])
        rows = big("rows", 0, [P, R_ALL])

        QKVF = big("QKVF", 9, [P, 12, SEQ])
        UV = big("UV", 21, [P, NT, D])
        Z = big("Z", 29, [P, NT, 512])
        Qt = big("Qt", 33, [P, NT, G_H, P])
        Kt = big("Kt", 37, [P, NT, G_H, P])
        Vt = big("Vt", 41, [P, NT, G_H, P])
        KBt = big("KBt", 45, [P, NT, G_H, P])
        KBE = big("KBE", 49, [P, NT, G_H, P])
        VBt = big("VBt", 53, [P, NT, G_H, P])
        QDt = big("QDt", 57, [P, NT, G_H, P])
        KDt = big("KDt", 61, [P, NT, G_H, P])
        fT = big("fT", 65, [P, 4, NT, G_H, P])
        decA = big("decA", 81, [P, NT, G_H, P])
        decAT = big("decAT", 85, [P, NT, G_H, P])
        decQ = big("decQ", 89, [P, NT, G_H, P])
        D0 = big("D0", 93, [P, NT, G_H, P])
        aM = big("aM", 97, [P, NT, G_H, P])
        aT = big("aT", 101, [P, NT, G_H, P])
        N1 = big("N1", 45, [P, NT, G_H, P])
        N1T = big("N1T", 57, [P, NT, G_H, P])
        N2 = big("N2", 105, [P, NT, G_H, P])
        N2T = big("N2T", 109, [P, NT, G_H, P])
        N4 = big("N4", 113, [P, NT, G_H, P])
        N4T = big("N4T", 9, [P, NT, G_H, P])
        N8 = big("N8", 13, [P, NT, G_H, P])
        YI = big("YI", 17, [P, NT, G_H, P])
        YIT = big("YIT", 93, [P, NT, G_H, P])
        L1T = big("L1T", 105, [P, NT, G_H, P])
        P1 = big("P1", 109, [P, NT, G_H, P])
        L2T = big("L2T", 113, [P, NT, G_H, P])
        P2 = big("P2", 9, [P, NT, G_H, P])
        Ut = big("Ut", 45, [P, NT, G_H, P])
        wT = big("wT", 57, [P, NT, G_H, P])
        qkT = big("qkT", 13, [P, NT, G_H, P])
        Vn = big("Vn", 113, [P, NT, G_H, P])
        St = big("St", 117, [P, G_H, P])
        Ot = big("Ot", 17, [P, NT, G_H, P])
        DG = big("DG", 105, [P, NT, G_H, P])
        OC = big("OC", 65, [P, NT, D])
        Q1 = big("Q1", 9, [P, NT, D])
        K1 = big("K1", 17, [P, NT, D])
        V1 = big("V1", 25, [P, NT, D])
        QKT = big("QKT", 33, [P, 16, SEQ])
        ALIBI = big("ALIBI", 49, [P, C_H, 3 * P])
        S1 = big("S1", 61, [P, 2, 3 * P])
        PR1 = big("PR1", 64, [P, 4, 3 * P])
        PT1 = big("PT1", 70, [P, 2, 3 * P])
        O1 = big("O1", 73, [P, NT, D])
        SQ = big("SQ", 81, [P, NT, D])
        H_hi = big("H_hi", 33, [P, 2, SEQ], F32R)
        H_lo = big("H_lo", 35, [P, 2, SEQ], F32R)
        H_r = big("H_r", 37, [P, 2, SEQ])
        H_q = big("H_q", 39, [P, 2, SEQ])
        p_raw = big("p_raw", 41, [P, 2, SEQ])
        p_hi = big("p_hi", 43, [P, 2, SEQ], F32R)
        p_lo = big("p_lo", 45, [P, 2, SEQ], F32R)
        GT = big("GT", 89, [P, NT, D])
        G2 = big("G2", 81, [P, NT, D])

        x_dram = ins["x"].rearrange("(t p) d -> p t d", p=P)
        out_dram = out.rearrange("(t p) d -> p t d", p=P)
        x_spill = nc.dram_tensor("x_spill", [P, NT * D], F32).ap()

        acc = [ctx.enter_context(nc.psum_tensor(f"acc{i}", [P, 512], F32)) for i in range(4)]
        col = [ctx.enter_context(nc.psum_tensor(f"col{i}", [P, 512], F32)) for i in range(2)]
        mb = [ctx.enter_context(nc.psum_tensor(f"mb{i}", [P, 512], F32)) for i in range(2)]

        norm_banks = [col[0], col[1], mb[0], mb[1]]

        block = ctx.enter_context(nc.Block())

        def src_of(j):
            name, kind, b, c0, width = PLAN[j]
            if kind == "col":
                return ins[name][b]
            return ins[name][b * P:(b + 1) * P, c0:c0 + width]

        def splits_of(j):
            width = PLAN[j][4]
            if width == VC_W:
                return [(0, 512), (512, VC_W)]
            if width == 520:
                return [(0, 512), (512, 520)]
            return [(0, width // 2), (width // 2, width)]

        last_of = {g: FIRST[g] - 1 for g in GROUPS}
        for g in GROUPS:
            if g.startswith("mlp"):
                last_of[g] = FIRST[g] + 2 * D_FF // P - 1
            else:
                last_of[g] = FIRST[g]
                while last_of[g] + 1 < len(PLAN) and last_of[g] + 1 not in FIRST.values():
                    last_of[g] += 1

        def acc_full(eng, g, bank):
            if bank < 3:
                eng.wait_ge(sem("acc_full"), 3 * GROUPS.index(g) + bank + 1)
            else:
                used(eng, last_of[g])

        def used(eng, j, i=0):
            eng.wait_ge(sem(f"used{j % RING}"), upto(f"used{j % RING}", j // RING + i + 1))

        @block.sync
        def _(sp):
            sp.dma_start(X[:, 0, :], x_dram[:, 0, :]).then_inc(sem("x0_in"), 16)
            sp.dma_start(cols[:, :], ins["cols"]).then_inc(sem("cols_in"), 16)

            def load(j, src=None, i=0):
                s = j % RING
                use = j // RING + i
                if j >= RING:
                    sp.wait_ge(sem(f"hi{s}"), upto(f"hi{s}", use))
                    sp.wait_ge(sem(f"lo{s}"), upto(f"lo{s}", use))
                width = PLAN[j][4]
                sp.dma_start(w_raw[:, s, 0:width], src_of(j) if src is None else src).then_inc(
                    sem(f"raw{s}"), 16)

            j = 0
            while j < len(PLAN):
                if j == RING:
                    sp.dma_start(pos_i[:, :], ins["positions"]).then_inc(sem("pos_in"), 16)
                    sp.dma_start(rows_f[:, :], ins["freqs"].to_broadcast([P, N_FREQ])).then_inc(
                        sem("freq_in"), 16)
                if j == FIRST["query"] + 8:
                    sp.wait_ge(sem("ev_wout"), upto("ev_wout", 4))
                    sp.dma_start(x_spill, X[:, :, :]).then_inc(sem("x_spilled"), 16)
                    sp.dma_start(KST[:, :, :], ins["sub_keys"]).then_inc(sem("keys_in"), 16)
                if j == FIRST["qkv_e"]:
                    used(sp, V0 - 1)
                    sp.wait_ge(sem("x_spilled"), 16)
                    sp.dma_start(XB[:, :, :], x_spill).then_inc(sem("x_back"), 16)
                    sp.wait_ge(sem("gate"), NKEYS)
                    sp.dma_start(WST[:, :, :], ins["gmlp_w"]).then_inc(sem("wst_in"), 16)
                    sp.wait_ge(sem("W_lo"), ROWS_OVER)
                    sp.dma_start(rows[:, :], ins["rows"].to_broadcast([P, R_ALL])).then_inc(
                        sem("rows_in"), 16)
                for layer in range(2):
                    if j == FIRST[f"gate{layer}"]:
                        sp.dma_start(p_raw[:, :, :], ins["p"][layer]).then_inc(sem("p_in"), 16)
                if j in LOOPS:
                    with sp.Fori(0, LOOPS[j]) as i:
                        for q in range(4):
                            name, kind, b = PLAN[j + q][:3]
                            n = i * (PLAN[j + 4 + q][2] - b) + b
                            src = ins[name][n] if kind == "col" else ins[name][bass.ds(n * P, P), :]
                            load(j + q, src, i)
                    j += 4 * LOOPS[j]
                    continue
                load(j)
                j += 1
            sp.wait_ge(sem("ev_ple1"), upto("ev_ple1", 4))
            sp.dma_start(out_dram, X[:, :, :]).then_inc(sem("stored"), 16)
            sp.wait_ge(sem("stored"), 16)
            sp.wait_ge(sem("x_spilled"), 16)

        @block.tensor
        def _(pe):
            mm = nc.tensor.matmul

            def chunk_in(j, i=0):
                pe.wait_ge(sem(f"hi{j % RING}"), upto(f"hi{j % RING}", j // RING + i + 1))
                pe.wait_ge(sem(f"lo{j % RING}"), upto(f"lo{j % RING}", j // RING + i + 1))

            def row_chunk(j, i, hi, lo, first, last, freed=None):
                s = j % RING
                chunk_in(j, i)
                for t in range(NT):
                    for n, (a, b) in enumerate(splits_of(j)):
                        o = acc[2 * t + n][:, 0:b - a]
                        if first and freed:
                            pe.wait_ge(sem(freed), upto(freed, 2 * t + n + 1))
                        mm(o, hi(t), w_hi[:, s, a:b], start=first, stop=False)
                        mm(o, hi(t), w_lo[:, s, a:b], start=False, stop=False)
                        m = mm(o, lo(t), w_hi[:, s, a:b], start=False, stop=last)
                        if last and 2 * t + n < 3:
                            m.then_inc(sem("acc_full"), 1)
                m.then_inc(sem(f"used{s}"), 1)

            def row_group(g, freed, hi=None, lo=None, blocks=None, norm=None):
                j0 = FIRST[g]
                hi = hi or (lambda k: lambda t: hT_hi[:, k, t * P:(t + 1) * P])
                lo = lo or (lambda k: lambda t: hT_lo[:, k, t * P:(t + 1) * P])
                count = last_of[g] - j0 + 1
                for k in range(count):
                    b = k if blocks is None else blocks[k]
                    if norm is not None:
                        block_in(norm, k)
                    row_chunk(j0 + k, 0, hi(b), lo(b), k == 0, k == count - 1, freed)

            def col_chunk(j, i, bank, norm=None):
                s = j % RING
                chunk_in(j, i)
                wh = w_hi[:, s, :].rearrange("p (k n) -> p k n", k=KD)
                wl = w_lo[:, s, :].rearrange("p (k n) -> p k n", k=KD)
                o = col[bank][:, 0:SEQ]
                for k in range(KD):
                    if norm is not None:
                        block_in(norm, k)
                    mm(o, wh[:, k, :], hT_hi[:, k, :], start=k == 0, stop=False)
                    mm(o, wh[:, k, :], hT_lo[:, k, :], start=False, stop=False)
                    m = mm(o, wl[:, k, :], hT_hi[:, k, :], start=False, stop=k == KD - 1)
                m.then_inc(sem(f"used{s}"), 1)

            def norm_T(n):
                for t in range(NT):
                    pe.wait_ge(sem("xn1" if t else "xn0"), n + 1)
                    for b, bank in enumerate(norm_banks):
                        for kk in range(2):
                            k = 2 * b + kk
                            m = pe.transpose(bank[:, kk * SEQ + t * P:kk * SEQ + (t + 1) * P],
                                             XN[:, t, k * P:(k + 1) * P], ident[:, :])
                        if t == NT - 1:
                            m.then_inc(sem("xnT"), 1)

            def block_in(norm, k):
                pe.wait_ge(sem("hT"), KD * norm + max(k, 3) + 1)

            def fills(name, banks, n0=0):
                for b, parts in enumerate(banks):
                    if b + n0 >= 2:
                        pe.wait_ge(sem(name + "_E"), upto(name + "_E", b + n0 - 1))
                    for c, src in parts:
                        rows_, n = src.shape[1], src.shape[0]
                        m = pe.transpose(mb[b % 2][0:rows_, c:c + n], src, ident[:, :])
                    m.then_inc(sem(name + "_T"), 1)

            pe.wait_ge(sem("ident"), 2)
            norm_T(0)
            row_group("qk", None, norm=0)
            row_group("vc", "ev_qk")
            row_group("ga", "ev_vc")
            pe.wait_ge(sem("cn"), upto("cn", 1))
            fills("c", [[(kk * SEQ + t * P, CN[:, t, k * P:(k + 1) * P])
                         for kk, k in enumerate(ks) for t in range(NT)] for ks in ((0, 1), (2,))])
            row_group("gb", "ev_ga")
            pe.wait_ge(sem("cT"), upto("cT", 3))
            for g, base, freed in (("qup", 0, "ev_gb"), ("kvup", 2, "ev_qup")):
                row_group(g, freed,
                          lambda k, base=base: lambda t: cT_hi[:, base + k, t * P:(t + 1) * P],
                          lambda k, base=base: lambda t: cT_lo[:, base + k, t * P:(t + 1) * P])

            pe.wait_ge(sem("rope_a"), upto("rope_a", 1))
            fills("qa", [[(kk * SEQ + t * P, QR[:, t, 2 * (2 * b + kk):2 * (2 * b + kk) + 2, :]
                           .rearrange("p h d -> p (h d)")) for kk in range(2) for t in range(NT)]
                         for b in range(4)])
            pe.wait_ge(sem("qa_E"), upto("qa_E", 4))
            pe.wait_ge(sem("rope_b"), upto("rope_b", 2))
            fills("qb", [[(kk * SEQ + t * P, (QB if b < 4 else KF)[:, t, 2 * (b % 4) + kk, :])
                          for kk in range(2) for t in range(NT)] for b in range(8)])
            pe.wait_ge(sem("qb_E"), upto("qb_E", 8))

            def qk_of(u):
                if u < A_H:
                    r = slice(64 * (u % 2), 64 * (u % 2) + 64)
                    return QTA[r, u // 2, :], QTA[r, 4 + u // 2, :]
                return QTB[0:B_DK, u - A_H, :], QTB[0:B_DK, u, :]

            def scores(u):
                if u >= 2:
                    pe.wait_ge(sem("masked"), u - 1)
                q, k = qk_of(u)
                mm(col[u % 2][:, 0:P], q[:, 0:P], k[:, 0:P], start=True, stop=True)
                mm(col[u % 2][:, P:3 * P], q[:, P:2 * P], k, start=True, stop=True).then_inc(
                    sem("scores"), 1)

            def causal_fills(u, probs, done, freed):
                if u >= 2:
                    pe.wait_ge(sem(freed), upto(freed, u - 1))
                for c in range(3):
                    m = pe.transpose(mb[u % 2][:, c * P:(c + 1) * P], probs[:, c * P:(c + 1) * P],
                                     ident[:, :])
                m.then_inc(sem(done), 1)

            def values(u, pt, v, o, done):
                mm(o(0), pt[:, 0:P], v(0), start=True, stop=True)
                mm(o(1), pt[:, P:2 * P], v(0), start=True, stop=False)
                mm(o(1), pt[:, 2 * P:3 * P], v(1), start=False, stop=True).then_inc(sem(done), 1)

            scores(0)
            scores(1)
            for u in range(A_H + B_H):
                pe.wait_ge(sem("exp"), u + 1)
                causal_fills(u, Pr[:, u % 2, :], "pT", "pT_E")
                if u + 2 < A_H + B_H:
                    scores(u + 2)
                pe.wait_ge(sem("pT_E"), upto("pT_E", u + 1))
                if u == 0:
                    pe.wait_ge(sem("ev_kvup"), upto("ev_kvup", 4))
                h = u % 8
                if u < A_H:
                    v = lambda kt, h=h: VC[:, kt, h * 64:(h + 1) * 64]
                else:
                    v = lambda kt, h=h: VB[:, kt, h, :]
                values(u, PT[:, u % 2, :], v,
                       lambda t, u=u, h=h: acc[2 * (u // 8) + t][:, h * 64:(h + 1) * 64], "pv")

            pe.wait_ge(sem("y"), upto("y", 4))
            fills("y", [[(kk * SEQ + t * P, Y[:, br, t, 2 * (2 * b + kk):2 * (2 * b + kk) + 2, :]
                          .rearrange("p h d -> p (h d)")) for kk in range(2) for t in range(NT)]
                        for br in range(2) for b in range(2)])
            pe.wait_ge(sem("y_E"), upto("y_E", 4))
            row_group("br_a", None)
            row_group("br_b", "ev_br_a", blocks=[4, 5, 6, 7])
            pe.wait_ge(sem("ev_br_b"), upto("ev_br_b", 4))

            def stream_T(name, src):
                fills(name, [[(kk * SEQ + t * P, src[:, t, (2 * b + kk) * P:(2 * b + kk + 1) * P])
                              for kk in range(2) for t in range(NT)] for b in range(4)])
                pe.wait_ge(sem(name + "_E"), upto(name + "_E", 4))

            stream_T("m", M)
            row_group("wout", "ev_br_b")

            norm_T(1)
            for n in range(16):
                if n >= 2:
                    pe.wait_ge(sem("qp"), n - 1)
                col_chunk(FIRST["query"] + n, 0, n % 2, norm=1 if n == 0 else None)
            pe.wait_ge(sem("keys_in"), 16)
            pe.wait_ge(sem("qp"), 16)
            for t in range(NT):
                for b in range(4):
                    f = 4 * t + b
                    if f >= 2:
                        pe.wait_ge(sem("sc"), f - 1)
                    for q in range(4):
                        n = 4 * b + q
                        m = mm(mb[f % 2][:, q * P:(q + 1) * P], QPT[:, n, t * P:(t + 1) * P],
                               KST[:, n, :], start=True, stop=True)
                    m.then_inc(sem("scT"), 1)

            def u_round(r):
                for q in range(4):
                    n = r * 4 + q
                    if not (isinstance(n, int) and n < 2):
                        pe.wait_ge(sem("gelu"), n - 1)
                    col_chunk(U0 + q, r, q % 2)
                    yield q

            def gates(n, q):
                pe.wait_ge(sem("hot"), n + 1)
                if not (isinstance(n, int) and n < 2):
                    pe.wait_ge(sem("gated"), n - 1)
                for t in range(4):
                    o = mb[q % 2][:, t * HALF:(t + 1) * HALF]
                    mm(o, hot2[:, q % 2, t, :], hot_hi[:, q % 2, t, :], start=True, stop=False)
                    m = mm(o, hot2[:, q % 2, t, :], hot_lo[:, q % 2, t, :], start=False, stop=True)
                m.then_inc(sem("gate"), 1)

            def v_round(r, first=False, last=False):
                for q in range(4):
                    n = r * 4 + q
                    pe.wait_ge(sem("W_hi"), n + 1)
                    pe.wait_ge(sem("W_lo"), n + 1)
                    row_chunk(V0 + q, r, lambda t: W_hi[:, q % 2, t * P:(t + 1) * P],
                              lambda t: W_lo[:, q % 2, t * P:(t + 1) * P],
                              first and q == 0, last and q == 3)
                    yield q

            QUARTER = HALF // 4
            for _ in u_round(0):
                pass
            with pe.Fori(1, QUARTER) as r:
                for _ in u_round(r):
                    pass
            pe.wait_ge(sem("sc"), 8)
            pe.wait_ge(sem("picks"), upto("picks", 1))
            pick_maps = [tk_bv[:, :, :, :], tk_sel[:, 0, :, :, :], tk_sel[:, 1, :, :, :]]
            fills("pk", [[((m % 2) * SEQ + t * P, pick_maps[m][:, t].rearrange("p h k -> p (h k)"))
                          for m in ms for t in range(NT)] for ms in ((0, 1), (2,))])
            pe.wait_ge(sem("pk_E"), upto("pk_E", 2))
            for q in u_round(QUARTER):
                gates(q, q)
            with pe.Fori(QUARTER + 1, 2 * QUARTER) as r:
                for q in u_round(r):
                    gates((r - QUARTER) * 4 + q, q)

            for q in v_round(0, first=True):
                gates(HALF + q, q)
            with pe.Fori(1, QUARTER) as r:
                for q in v_round(r):
                    gates(r * 4 + q + HALF, q)
            with pe.Fori(QUARTER, 2 * QUARTER - 1) as r:
                for _ in v_round(r):
                    pass
            for _ in v_round(2 * QUARTER - 1, last=True):
                pass

            norm_T(2)
            for n in range(12):
                if n >= 2:
                    pe.wait_ge(sem("conv"), n - 1)
                col_chunk(FIRST["qkv_e"] + n, 0, n % 2, norm=2 if n == 0 else None)
            row_group("zba", "ev_v")
            row_group("uv", "ev_zba")

            pe.wait_ge(sem("silu"), 12)
            fills("tok", [[(h * P, QKVF[:, 4 * m + h, t * P:(t + 1) * P]) for h in range(G_H)]
                          for m in range(3) for t in range(NT)])
            pe.wait_ge(sem("tok_E"), upto("tok_E", 6))
            pe.wait_ge(sem("ev_uv"), upto("ev_uv", 4))
            for t in range(NT):
                if t == 0:
                    pe.wait_ge(sem("g_ready"), upto("g_ready", 1))
                mm(mb[t][:, 0:G_H], masks[:, 2, :], stat[:, 16 + 4 * t:20 + 4 * t], start=True,
                   stop=True).then_inc(sem("gcT"), 1)
            for t in range(NT):
                if t == 0:
                    pe.wait_ge(sem("ones"), 1)
                pe.wait_ge(sem("diag"), t + 1)
                mm(acc[t][:, :], ones[:, :], DG[:, t, :, :].rearrange("p h f -> p (h f)"),
                   start=True, stop=True).then_inc(sem("gcrow"), 1)
            pe.wait_ge(sem("tokmaps"), upto("tokmaps", 1))
            for t in range(NT):
                for m, src in enumerate((Kt, KBt, Qt, QDt)):
                    f = 4 * t + m
                    if f >= 2:
                        pe.wait_ge(sem("fT_E"), upto("fT_E", f - 1))
                    for h in range(G_H):
                        x = pe.transpose(mb[f % 2][:, h * P:(h + 1) * P], src[:, t, h, :], ident[:, :])
                    x.then_inc(sem("fT_T"), 1)
            pe.wait_ge(sem("fT_E"), upto("fT_E", 8))

            maps = {"kT": fT[:, 0], "kbT": fT[:, 1], "qT": fT[:, 2], "N1": N1, "N1T": N1T,
                    "N2": N2, "N2T": N2T, "N4": N4, "N4T": N4T, "N8": N8, "Y": YI, "YT": YIT,
                    "L1T": L1T, "P1": P1, "L2T": L2T, "P2": P2, "VB": VBt, "KBE": KBE}
            for s, (result, lhsT, rhs, need) in enumerate(SOLVE):
                for t in range(NT):
                    n = NT * s + t
                    ready = max(NT * need + t + 1 if need >= 0 else 0, n - 5)
                    if ready > 0:
                        pe.wait_ge(sem("sv_E"), ready)
                    for h in range(G_H):
                        m = mm((acc + col)[n % 6][:, h * P:(h + 1) * P], maps[lhsT][:, t, h, :],
                               maps[rhs][:, t, h, :], start=True, stop=True)
                    m.then_inc(sem("sv"), 1)
            pe.wait_ge(sem("sv_E"), NT * len(SOLVE))

            qdT = fT[:, 3]
            for c in range(SEQ // G_CH):
                t, r0 = c // 2, G_CH * (c % 2)
                r = slice(r0, r0 + G_CH)
                if c:
                    pe.wait_ge(sem("state"), c)
                    pe.wait_ge(sem("o_E"), c)
                    for h in range(G_H):
                        m = mm(col[0][r, h * P:(h + 1) * P], wT[:, t, h, r], St[:, h, :],
                               start=True, stop=True)
                    m.then_inc(sem("wS"), 1)
                    for h in range(G_H):
                        mm(col[1][r, h * P:(h + 1) * P], qdT[:, t, h, r], St[:, h, :],
                           start=h == 0, stop=False, skip_group_check=True)
                pe.wait_ge(sem("v_new"), c + 1)
                if c < SEQ // G_CH - 1:
                    for h in range(G_H):
                        m = mm(mb[c % 2][:, h * P:(h + 1) * P], KDt[r, t, h, :], Vn[r, t, h, :],
                               start=True, stop=True)
                    m.then_inc(sem("dS"), 1)
                for h in range(G_H):
                    m = mm(col[1][r, h * P:(h + 1) * P], qkT[r, t, h, r], Vn[r, t, h, :],
                           start=c == 0 and h == 0, stop=True, skip_group_check=True)
                m.then_inc(sem("o_T"), 1)

            pe.wait_ge(sem("gv"), upto("gv", 1))
            pe.wait_ge(sem("wst"), 1)
            for t in range(NT):
                for g in range(M_G):
                    m = mm(acc[t][:, g * P:(g + 1) * P], WST[:, g, :],
                           UV[:, t, 512 + g * P:512 + (g + 1) * P], start=True, stop=True)
                m.then_inc(sem("mix"), 1)
            pe.wait_ge(sem("oc"), upto("oc", 1))
            stream_T("oc", OC)
            row_group("out_e", None)

            def mlp(layer, freed):
                j0 = FIRST[f"mlp{layer}"]
                f0 = layer * D_FF // P

                def w1_bank(j):
                    return ((j - j0 + 1) // 2) % 2

                def w2_slot(j):
                    return ((j - j0 - 2) // 2) % 2 if j != last_of[f"mlp{layer}"] else 1

                def first_product(f, j, i):
                    if not (isinstance(f, int) and f < 2):
                        pe.wait_ge(sem("relu"), f - 1 + f0)
                    col_chunk(j, i, w1_bank(j), norm=(6 if layer else 3) if j == j0 else None)

                def second_product(f, j, i, first, last):
                    pe.wait_ge(sem("H"), f + 1 + f0)
                    slot = w2_slot(j)
                    row_chunk(j, i, lambda t: H_hi[:, slot, t * P:(t + 1) * P],
                              lambda t: H_lo[:, slot, t * P:(t + 1) * P], first, last,
                              freed if first else None)

                first_product(0, j0, 0)
                first_product(1, j0 + 1, 0)
                second_product(0, j0 + 2, 0, True, False)
                j = j0 + MLP_SKIP
                with pe.Fori(0, MLP_ROUNDS) as r:
                    first_product(2 * r + 2, j, r)
                    second_product(2 * r + 1, j + 1, r, False, False)
                    first_product(2 * r + 3, j + 2, r)
                    second_product(2 * r + 2, j + 3, r, False, False)
                second_product(D_FF // P - 1, last_of[f"mlp{layer}"], 0, False, True)

            def gated_projection(layer, n):
                norm_T(n)
                row_group(f"gate{layer}", f"ev_mlp{layer}", norm=n)
                pe.wait_ge(sem("p_split"), layer + 1)
                row_group(f"ple{layer}", f"ev_gate{layer}",
                          lambda k: lambda t: p_hi[:, k, t * P:(t + 1) * P],
                          lambda k: lambda t: p_lo[:, k, t * P:(t + 1) * P])

            norm_T(3)
            mlp(0, "ev_out_e")
            gated_projection(0, 4)

            norm_T(5)
            row_group("q1", "ev_ple0", norm=5)
            row_group("k1", "ev_q1")
            row_group("v1", "ev_k1")
            pe.wait_ge(sem("qk1"), 2)
            fills("qk1", [[(kk * SEQ + t * P, (Q1 if b < 4 else K1)[:, t, (2 * (b % 4) + kk) * P:
                                                                 (2 * (b % 4) + kk + 1) * P])
                           for kk in range(2) for t in range(NT)] for b in range(8)])
            pe.wait_ge(sem("qk1_E"), upto("qk1_E", 8))
            pe.wait_ge(sem("ev_v1"), upto("ev_v1", 4))

            def scores1(w):
                if w >= 2:
                    pe.wait_ge(sem("masked1"), w - 1)
                h, r = w // 2, slice(C_DH * (w % 2), C_DH * (w % 2) + C_DH)
                q, k = QKT[r, h, :], QKT[r, C_H + h, :]
                mm(col[w % 2][:, 0:P], q[:, 0:P], k[:, 0:P], start=True, stop=True)
                mm(col[w % 2][:, P:3 * P], q[:, P:2 * P], k, start=True, stop=True).then_inc(
                    sem("scores1"), 1)

            for w in range(2):
                scores1(w)
            for h in range(C_H):
                if h + 1 < C_H:
                    scores1(2 * h + 2)
                    scores1(2 * h + 3)
                pe.wait_ge(sem("attn1"), h + 1)
                causal_fills(h, PR1[:, (2 * h) % 4, :], "aT", "aT_E")
                pe.wait_ge(sem("aT_E"), upto("aT_E", h + 1))
                values(h, PT1[:, h % 2, :], lambda kt, h=h: V1[:, kt, h * P:(h + 1) * P],
                       lambda t, h=h: acc[2 * t + h // 4][:, (h % 4) * P:(h % 4 + 1) * P], "pv1")
            pe.wait_ge(sem("o1"), upto("o1", 1))
            stream_T("o1", O1)
            row_group("out_o", None)
            norm_T(6)
            mlp(1, "ev_out_o")
            gated_projection(1, 7)

        @block.scalar
        def _(act):
            f = nc.scalar.activation
            counts = {}

            def then(ins, name):
                counts[name] = counts.get(name, 0) + 1
                ins.then_inc(sem(name), 1)
                act.wait_ge(sem(name), upto(name, counts[name]))

            def split(j, i=0):
                s = j % RING
                act.wait_ge(sem(f"raw{s}"), upto(f"raw{s}", (j // RING + 1 + i) * 16))
                if j >= RING:
                    used(act, j - RING, i)
                w = PLAN[j][4] if j < len(PLAN) else D
                f(w_hi[:, s, 0:w], w_raw[:, s, 0:w], ACT.Copy).then_inc(sem(f"hi{s}"), 1)

            done = [0]

            def split_to(j):
                while done[0] < min(j, len(PLAN)):
                    split(done[0])
                    done[0] += 1

            def norm(n, name):
                for t in range(NT):
                    for h in range(2):
                        act.wait_ge(sem(name), upto(name, 2 * t + h + 1))
                        c = slice(h * 512, (h + 1) * 512)
                        f(junk[:, t, c], X[:, t, c], ACT.Square, scale=D ** -0.5,
                          accum_out=ss[:, t, h:h + 1]).then_inc(sem("ss"), 1)

            norms = [0]

            def norm_T(n):
                norms[0] += 1
                act.wait_ge(sem("rstd"), norms[0] + (n >= 2))
                f(XN[:, 1, :], X[:, 1, :], ACT.Copy, scale=rstd[:, 1:2]).then_inc(sem("xn1"), 1)
                for k in range(KD):
                    if k % 2 == 0:
                        act.wait_ge(sem("xnT"), 4 * n + k // 2 + 1)
                    f(hT_hi[:, k, :], norm_banks[k // 2][:, (k % 2) * SEQ:(k % 2 + 1) * SEQ],
                      ACT.Copy, scale=cols[:, 8 * n + k:8 * n + k + 1]).then_inc(sem("hT_hi"), 1)

            def evacuate(g, dst, func, ev):
                for t in range(NT):
                    for n in range(2):
                        acc_full(act, g, 2 * t + n)
                        o = dst(t, n)
                        f(o, acc[2 * t + n][:, 0:o.shape[1]], func).then_inc(sem(ev), 1)

            halves = lambda m: lambda t, n: m[:, t, n * 512:(n + 1) * 512]

            act.wait_ge(sem("eps"), 1)
            nc.scalar.dma_start(X[:, 1, :], x_dram[:, 1, :]).then_inc(sem("x1_in"), 16)
            for t in range(NT):
                act.wait_ge(sem("x1_in" if t else "x0_in"), 16)
                for h in range(2):
                    c = slice(h * 512, (h + 1) * 512)
                    f(junk[:, t, c], X[:, t, c], ACT.Square, scale=D ** -0.5,
                      accum_out=ss[:, t, h:h + 1]).then_inc(sem("ss"), 1)
            act.wait_ge(sem("cols_in"), 16)
            norm_T(0)
            split_to(FIRST["vc"] + 3)
            act.wait_ge(sem("angles"), upto("angles", 1))
            f(ang[:, :, :, :], ang[:, :, :, :], ACT.Sin).then_inc(sem("trig"), 1)
            split_to(FIRST["ga"] + 4)
            act.wait_ge(sem("ev_vc"), upto("ev_vc", 4))
            for t in range(NT):
                then(f(junk[:, 0, 0:Q_LORA], VC[:, t, 512:512 + Q_LORA], ACT.Square,
                       accum_out=stat[:, t:t + 1]), "css")
                then(f(junk[:, 0, 0:KV_LORA], VC[:, t, 768:768 + KV_LORA], ACT.Square,
                       accum_out=stat[:, 2 + t:3 + t]), "css")
            f(stat[:, 4:6], stat[:, 0:2], ACT.Sqrt, bias=epsc[:, 0:1], scale=1.0 / Q_LORA).then_inc(
                sem("crms"), 1)
            f(stat[:, 6:8], stat[:, 2:4], ACT.Sqrt, bias=epsc[:, 0:1], scale=1.0 / KV_LORA).then_inc(
                sem("crms"), 1)
            split_to(FIRST["gb"] + 4)
            evacuate("ga", halves(GA), ACT.Sigmoid, "ev_ga")
            split_to(FIRST["qup"] + 4)
            evacuate("gb", halves(GB), ACT.Sigmoid, "ev_gb")
            split_to(FIRST["br_a"] + 4)

            def copy_probs(u, dst, full, free, n, signal):
                act.wait_ge(sem(full), upto(full, n + 1))
                if n >= 2:
                    act.wait_ge(sem(free), upto(free, n - 1))
                f(dst[:, n % 2, :], mb[n % 2][:, 0:3 * P], ACT.Copy).then_inc(sem(signal), 1)

            for u in range(A_H + B_H):
                scale = (A_DH if u < A_H else B_DK) ** -0.5
                act.wait_ge(sem("masked"), u + 1)
                if u >= 2:
                    act.wait_ge(sem("pT"), upto("pT", u - 1))
                f(Pr[:, u % 2, 0:P], Sm[:, u % 2, 0:P], ACT.Exp, bias=mx[:, u, 0:1], scale=scale,
                  accum_out=sums[:, u, 0:1]).then_inc(sem("exp0"), 1)
                f(Pr[:, u % 2, P:3 * P], Sm[:, u % 2, P:3 * P], ACT.Exp, bias=mx[:, u, 1:2],
                  scale=scale, accum_out=sums[:, u, 1:2]).then_inc(sem("exp"), 1)
                if u:
                    copy_probs(u, PT, "pT", "pv", u - 1, "pT_E")
            copy_probs(0, PT, "pT", "pv", A_H + B_H - 1, "pT_E")
            split_to(FIRST["br_b"] + 4)
            split_to(FIRST["wout"] + 4)
            split_to(FIRST["query"] + 3)
            norm(1, "ev_wout")
            norm_T(1)

            for n in range(16):
                split_to(FIRST["query"] + n + 4)
                used(act, FIRST["query"] + n)
                f(QPT[:, n, :], col[n % 2][:, 0:SEQ], ACT.Copy).then_inc(sem("qp"), 1)
            for b in range(8):
                act.wait_ge(sem("scT"), b + 1)
                f(SC[:, b // 4, 4 * (b % 4):4 * (b % 4) + 4, :].rearrange("p a n -> p (a n)"),
                  mb[b % 2][:, :], ACT.Copy).then_inc(sem("sc"), 1)

            def u_round(r):
                for q in range(4):
                    split(U0 + q + AHEAD, r)
                    used(act, U0 + q, r)
                    f(act_e[:, r * 4 + q, :], col[q % 2][:, 0:SEQ], ACT.Gelu).then_inc(
                        sem("gelu"), 1)

            assert done[0] == U0 + AHEAD
            with act.Fori(0, HALF // 4) as r:
                u_round(r)
            act.wait_ge(sem("best"), upto("best", 1))
            f(tk_bv[:, :, :, :], tk_bv[:, :, :, :], ACT.Exp).then_inc(sem("best_exp"), 1)
            act.wait_ge(sem("x_spilled"), 16)
            act.wait_ge(sem("pk_E"), upto("pk_E", 2))
            with act.Fori(HALF // 4, NKEYS // 4) as r:
                u_round(r)

            def gated_hi(c, n, q):
                if not (isinstance(c, int) and c < 2):
                    used(act, V0 + (q - 2) % 4, n if q >= 2 else n - 1)
                f(W_hi[:, q % 2, :], act_e[:, c, :], ACT.Copy).then_inc(sem("W_hi"), 1)

            def v_round(r, last=False, gate_last=None):
                for q in range(4):
                    split(V0 + q + AHEAD, r)
                    if q == 3 and gate_last:
                        act.wait_ge(sem("gated"), gate_last)
                    if not (last and q == 3):
                        gated_hi(r * 4 + q + 1, r if q < 3 else r + 1, (q + 1) % 4)

            act.wait_ge(sem("gated"), HALF)
            used(act, V0 - 1)
            gated_hi(0, 0, 0)
            v_round(0)
            with act.Fori(1, HALF // 4 - 1) as r:
                v_round(r)
            v_round(HALF // 4 - 1, gate_last=NKEYS)
            with act.Fori(HALF // 4, NKEYS // 4 - 1) as r:
                v_round(r)
            v_round(NKEYS // 4 - 1, last=True)
            done[0] = FIRST["qkv_e"] + AHEAD

            norm(2, "ev_v")
            norm(3, "x_final")
            norm_T(2)
            for n in range(12):
                split_to(FIRST["qkv_e"] + n + 4)
                act.wait_ge(sem("conv"), n + 1)
                f(QKVF[:, n, :], QKVF[:, n, :], ACT.Silu).then_inc(sem("silu"), 1)
            split_to(FIRST["uv"] + 4)
            for t in range(NT):
                acc_full(act, "zba", 2 * t)
                f(Z[:, t, :], acc[2 * t][:, :], ACT.Silu).then_inc(sem("ev_zba"), 1)
                acc_full(act, "zba", 2 * t + 1)
                f(stat[:, 8 * t:8 * t + 8], acc[2 * t + 1][:, 0:8], ACT.Copy).then_inc(
                    sem("ev_zba"), 1)
            split_to(FIRST["out_e"] + 4)
            evacuate("uv", halves(UV), ACT.Gelu_apprx_tanh, "ev_uv")

            act.wait_ge(sem("rows_in"), 16)
            act.wait_ge(sem("ev_zba"), upto("ev_zba", 4))
            ba = stat[:, 0:16].rearrange("p (t n) -> p t n", t=NT)
            f(stat[:, 32:40].rearrange("p (t n) -> p t n", t=NT), ba[:, :, 0:4], ACT.Sigmoid).then_inc(
                sem("beta"), 1)
            f(stat[:, 60:64], rows[:, R_ALOG:R_ALOG + 4], ACT.Exp).then_inc(sem("beta"), 1)
            act.wait_ge(sem("sp"), upto("sp", 1))
            f(stat[:, 48:56], stat[:, 48:56], ACT.Exp).then_inc(sem("sp_exp"), 1)
            act.wait_ge(sem("sp"), upto("sp", 2))
            f(stat[:, 16:24], stat[:, 24:32], ACT.Ln).then_inc(sem("sp_ln"), 1)
            act.wait_ge(sem("l2"), upto("l2", 1))
            f(sq16[:, :], sq16[:, :], ACT.Sqrt, bias=epsc[:, 0:1], scale=1.0).then_inc(sem("l2_root"), 1)
            act.wait_ge(sem("gc"), 2)
            f(egc[:, :], gc[:, :], ACT.Exp).then_inc(sem("egc"), 1)
            for t in range(NT):
                act.wait_ge(sem("gdiff"), 2 * t + 1)
                f(decA[:, t, :, :], decA[:, t, :, :], ACT.Exp, scale=-1.0).then_inc(sem("dec"), 1)
                act.wait_ge(sem("gdiff"), 2 * t + 2)
                f(decAT[:, t, :, :], decAT[:, t, :, :], ACT.Exp).then_inc(sem("dec"), 1)
                act.wait_ge(sem("glast"), t + 1)
                f(gl[:, 8 * t:8 * t + 8], gl[:, 8 * t:8 * t + 8], ACT.Exp).then_inc(sem("gl"), 1)
            act.wait_ge(sem("o_ss"), upto("o_ss", 1))
            f(stat[:, 0:8], stat[:, 0:8], ACT.Sqrt, bias=epsc[:, 0:1], scale=1.0 / G_DK).then_inc(
                sem("o_root"), 1)
            act.wait_ge(sem("v_ss"), upto("v_ss", 1))
            f(stat[:, 8:16], stat[:, 8:16], ACT.Sqrt, bias=epsc[:, 0:1], scale=1.0 / P).then_inc(
                sem("v_root"), 1)

            def mlp(layer):
                j0 = FIRST[f"mlp{layer}"]
                f0 = layer * D_FF // P

                def relu2(blk, j, i, s):
                    used(act, j, i)
                    if layer or not (isinstance(blk, int) and blk < 2):
                        act.wait_ge(sem("H"), blk - 1 + f0)
                    f(H_r[:, s, :], col[s][:, 0:SEQ], ACT.Relu).then_inc(sem("relu"), 1)
                    act.wait_ge(sem("relu"), blk + 1 + f0)
                    f(H_q[:, s, :], H_r[:, s, :], ACT.Square).then_inc(sem("square"), 1)

                split_to(j0 + 4)
                relu2(0, j0, 0, 0)
                split_to(j0 + 5)
                relu2(1, j0 + 1, 0, 1)
                split_to(j0 + MLP_SKIP + AHEAD)
                j = j0 + MLP_SKIP
                with act.Fori(0, MLP_ROUNDS) as r:
                    for q in range(4):
                        split(j + q + AHEAD, r)
                        if q % 2 == 0:
                            relu2(2 * r + 2 + q // 2, j + q, r, (q // 2) % 2)
                done[0] = j + 4 * MLP_ROUNDS + AHEAD

            def gated_projection(layer, n):
                split_to(FIRST[f"gate{layer}"] + 3)
                norm(n, f"ev_mlp{layer}")
                norm_T(n - 1)
                split_to(FIRST[f"ple{layer}"] + 4)
                evacuate(f"gate{layer}", halves(GT), ACT.Sigmoid, f"ev_gate{layer}")

            split_to(FIRST["mlp0"] + 3)
            norm(4, "ev_out_e")
            norm_T(3)
            mlp(0)
            gated_projection(0, 5)
            split_to(FIRST["q1"] + 3)
            norm(6, "ev_ple0")
            norm_T(5)
            act.wait_ge(sem("lam_dots"), upto("lam_dots", 2))
            f(stat[:, 2:4], stat[:, 0:2], ACT.Exp).then_inc(sem("lam_exp"), 1)
            for m, nxt in enumerate(("k1", "v1")):
                split_to(FIRST[nxt] + 4)
                act.wait_ge(sem("qk_ss"), m + 1)
                f(sq32[:, :], sq32[:, :], ACT.Sqrt, bias=epsc[:, 0:1], scale=1.0 / C_DH).then_inc(
                    sem("qk_root"), 1)
            split_to(FIRST["out_o"] + 4)
            for w in range(2 * C_H):
                act.wait_ge(sem("masked1"), w + 1)
                if w >= 4:
                    act.wait_ge(sem("aT"), upto("aT", (w - 4) // 2 + 1))
                f(PR1[:, w % 4, 0:P], S1[:, w % 2, 0:P], ACT.Exp, bias=mx1[:, w, 0:1],
                  accum_out=sum1[:, w, 0:1]).then_inc(sem("exp1a"), 1)
                f(PR1[:, w % 4, P:3 * P], S1[:, w % 2, P:3 * P], ACT.Exp, bias=mx1[:, w, 1:2],
                  accum_out=sum1[:, w, 1:2]).then_inc(sem("exp1"), 1)
                if w % 2 and w > 1:
                    copy_probs(0, PT1, "aT", "pv1", w // 2 - 1, "aT_E")
            copy_probs(0, PT1, "aT", "pv1", C_H - 1, "aT_E")
            act.wait_ge(sem("o1_ss"), upto("o1_ss", 1))
            f(sq32[:, 0:16], sq32[:, 0:16], ACT.Sqrt, bias=epsc[:, 0:1], scale=1.0 / P).then_inc(
                sem("o1_root"), 1)
            split_to(FIRST["mlp1"] + 3)
            norm(7, "ev_out_o")
            norm_T(6)
            mlp(1)
            gated_projection(1, 8)
            split_to(len(PLAN))

        @block.gpsimd
        def _(pool):
            g = nc.gpsimd
            counts = {}

            def then(ins, name):
                counts[name] = counts.get(name, 0) + 1
                ins.then_inc(sem(name), 1)
                pool.wait_ge(sem(name), upto(name, counts[name]))

            g.memset(epsc[:, :], EPS).then_inc(sem("eps"), 1)
            then(g.memset(ident[:, :], 0.0), "ident")
            then(g.affine_select(out=ident[:, :], in_=ident[:, :], compare_op=ALU.not_equal,
                                 fill=1.0, base=0, pattern=[[-1, P]], channel_multiplier=1), "ident")

            def causal_mask(m):
                then(g.memset(m[:, :], 0.0), "causal")
                for c in (0, 2):
                    d = m[:, c * P:(c + 1) * P]
                    then(g.affine_select(out=d, in_=d, compare_op=ALU.is_ge, fill=NEG, base=0,
                                         pattern=[[-1, P]], channel_multiplier=1), "causal")

            causal_mask(causal)
            g.iota(iota_row[:, :], [[1, P]], base=0, channel_multiplier=0,
                   allow_small_or_imprecise_dtypes=True).then_inc(sem("iota"), 1)

            def rest(j, i=0):
                s = j % RING
                pool.wait_ge(sem(f"hi{s}"), upto(f"hi{s}", j // RING + 1 + i))
                if j >= RING:
                    used(pool, j - RING, i)
                w = PLAN[j][4]
                g.tensor_tensor(w_lo[:, s, 0:w], w_raw[:, s, 0:w], w_hi[:, s, 0:w].bitcast(F32),
                                ALU.subtract).then_inc(sem(f"lo{s}"), 1)

            def block_masks():
                pool.wait_ge(sem("gate"), NKEYS)
                pool.wait_ge(sem("hot"), NKEYS)

                causal_mask(causal1)
                for c, base in ((0, 0), (1, P), (2, 0)):
                    g.iota(dist[:, c * P:(c + 1) * P], [[-1, P]], base=base, channel_multiplier=1,
                           allow_small_or_imprecise_dtypes=True).then_inc(sem("iota"), 1)
                then(g.memset(ones[:, :], 1.0), "ones")

                def within(m, size):
                    v = masks[:, m, :].rearrange("p (b f) -> p b f", f=size)
                    then(g.memset(masks[:, m, :], 1.0), "masks")
                    then(g.affine_select(out=v, in_=v, compare_op=ALU.is_ge, fill=0.0, base=0,
                                         pattern=[[-size, P // size], [0, size]],
                                         channel_multiplier=1), "masks")
                    then(g.affine_select(out=v, in_=v, compare_op=ALU.is_ge, fill=0.0,
                                         base=size - 1, pattern=[[size, P // size], [0, size]],
                                         channel_multiplier=-1), "masks")

                def triangle(m, base, step, mult):
                    v = masks[:, m, :]
                    then(g.affine_select(out=v, in_=v, compare_op=ALU.is_ge, fill=0.0, base=base,
                                         pattern=[[step, P]], channel_multiplier=mult), "masks")

                for m, size in ((0, 64), (1, 64), (2, 64), (3, 16), (5, 32)):
                    within(m, size)
                triangle(0, -1, -1, 1)
                triangle(1, -1, 1, -1)
                triangle(2, 0, 1, -1)
                then(g.tensor_tensor(masks[:, 4, :], masks[:, 5, :], masks[:, 3, :], ALU.subtract),
                     "masks")
                then(g.tensor_tensor(masks[:, 5, :], ones[:, :], masks[:, 5, :], ALU.subtract),
                     "masks")
                pool.wait_ge(sem("wst_in"), 16)
                g.affine_select(out=WST[:, :, :], in_=WST[:, :, :], compare_op=ALU.is_ge, fill=0.0,
                                base=0, pattern=[[0, M_G], [1, P]], channel_multiplier=-1).then_inc(
                    sem("wst"), 1)

            then(g.memset(minus_half[:, :], -0.5), "half")
            norms = [0]

            def row_rstd():
                norms[0] += 1
                pool.wait_ge(sem("ss"), 4 * norms[0])
                then(g.tensor_tensor(ms[:, :], ss[:, :, 0], ss[:, :, 1], ALU.add), "ms")
                then(g.tensor_scalar(ms[:, :], ms[:, :], EPS, None, ALU.add), "ms")
                g.tensor_tensor(rstd[:, :], ms[:, :], minus_half[:, :], ALU.pow).then_inc(
                    sem("rstd"), 1)

            row_rstd()
            norm_at = [FIRST[name] + 3 for name in ("query", "qkv_e", "mlp0", "gate0", "q1", "mlp1",
                                                    "gate1")]
            j = 0
            while j < len(PLAN):
                if j in norm_at:
                    row_rstd()
                    if j == FIRST["qkv_e"] + 3:
                        row_rstd()
                if j in LOOPS:
                    with pool.Fori(0, LOOPS[j]) as i:
                        for q in range(4):
                            rest(j + q, i)
                    j += 4 * LOOPS[j]
                    continue
                if j == FIRST["zba"]:
                    block_masks()
                rest(j)
                j += 1

        @block.vector
        def _(dve):
            v = nc.vector
            counts = {}

            def then(ins, name="dve"):
                counts[name] = counts.get(name, 0) + 1
                ins.then_inc(sem(name), 1)
                dve.wait_ge(sem(name), upto(name, counts[name]))

            def over(ap, shape, axis):
                return ap.unsqueeze(axis).to_broadcast(shape)

            def hi_lo(hi, lo, src, name):
                then(v.tensor_copy(hi, src))
                then(v.tensor_tensor(lo, src, hi.bitcast(F32), ALU.subtract), name)

            def hi_lo_gain(hi, lo, src, gain, name):
                then(v.tensor_scalar(hi, src, gain, None, ALU.mult))
                then(v.scalar_tensor_tensor(out=lo, in0=src, scalar=gain, in1=hi.bitcast(F32),
                                            op0=ALU.mult, op1=ALU.subtract), name)

            norms = [0]

            def rows_rstd():
                norms[0] += 1
                dve.wait_ge(sem("rstd"), norms[0])

            def norm_T(n):
                rows_rstd()
                v.tensor_scalar(XN[:, 0, :], X[:, 0, :], rstd[:, 0:1], None, ALU.mult).then_inc(
                    sem("xn0"), 1)
                for k in range(KD):
                    if k % 2 == 0:
                        dve.wait_ge(sem("hT_hi"), KD * n + k + 2)
                    v.scalar_tensor_tensor(
                        out=hT_lo[:, k, :], in0=norm_banks[k // 2][:, (k % 2) * SEQ:(k % 2 + 1) * SEQ],
                        scalar=cols[:, 8 * n + k:8 * n + k + 1], in1=hT_hi[:, k, :].bitcast(F32),
                        op0=ALU.mult, op1=ALU.subtract).then_inc(sem("hT"), 1)

            def stream_T(name):
                for b in range(4):
                    dve.wait_ge(sem(name + "_T"), upto(name + "_T", b + 1))
                    hi_lo(hT_hi[:, 2 * b:2 * b + 2, :].rearrange("p k s -> p (k s)"),
                          hT_lo[:, 2 * b:2 * b + 2, :].rearrange("p k s -> p (k s)"),
                          mb[b % 2][:, :], name + "_E")

            def banks(g):
                for t in range(NT):
                    for n in range(2):
                        acc_full(dve, g, 2 * t + n)
                        yield t, n, acc[2 * t + n]

            def evac(g, dst):
                for t, n, a in banks(g):
                    o = dst(t, n)
                    then(v.tensor_copy(o, a[:, 0:o.shape[1]]), "ev_" + g)

            def half(m):
                return lambda t, n: m[:, t, n * 512:(n + 1) * 512]

            def residual(g, old=X):
                for t, n, a in banks(g):
                    c = slice(n * 512, (n + 1) * 512)
                    v.tensor_tensor(X[:, t, c], a[:, :], old[:, t, c], ALU.add).then_inc(
                        sem("ev_" + g), 1)

            def copies(name, fill_dst):
                for b, dst in enumerate(fill_dst):
                    dve.wait_ge(sem(name + "_T"), upto(name + "_T", b + 1))
                    then(v.tensor_copy(dst, mb[b % 2][0:dst.shape[0], 0:dst.shape[1]]), name + "_E")

            dve.wait_ge(sem("cols_in"), 16)
            norm_T(0)
            dve.wait_ge(sem("pos_in"), 16)
            dve.wait_ge(sem("freq_in"), 16)
            then(v.tensor_copy(pos_f[:, :], pos_i[:, :]))
            for t in range(NT):
                for ph in range(2):
                    then(v.tensor_scalar(ang[:, t, ph, :], rows_f[:, :], pos_f[:, t:t + 1], None,
                                         ALU.mult))
            for ph in range(2):
                then(v.tensor_scalar(ang_k[:, :, ph, :], ang[:, :, ph, :], 1 / (2 * math.pi),
                                     0.25 * ph, ALU.mult, ALU.add))
            then(v.tensor_scalar(ang_k[:, :, :, :], ang_k[:, :, :, :], ROUND, None, ALU.add))
            then(v.tensor_scalar(ang_k[:, :, :, :], ang_k[:, :, :, :], ROUND, None, ALU.subtract))
            a_flat = ang[:, :, :, :].rearrange("p t a f -> p (t a f)")
            k_flat = ang_k[:, :, :, :].rearrange("p t a f -> p (t a f)")
            for turn in TURN:
                then(v.scalar_tensor_tensor(out=a_flat, in0=k_flat, scalar=-turn, in1=a_flat,
                                            op0=ALU.mult, op1=ALU.add))
            then(v.tensor_scalar(ang[:, :, 1, :], ang[:, :, 1, :], math.pi / 2, None, ALU.add))
            then(v.tensor_scalar(a_flat, a_flat, 3.1415925, -3.1415925, ALU.min, ALU.max), "angles")

            evac("qk", lambda t, n: QK[:, t, 8 * n:8 * n + 8, :].rearrange("p h d -> p (h d)"))
            evac("vc", lambda t, n: VC[:, t, 512 * n:(512, VC_W)[n]])
            dve.wait_ge(sem("crms"), upto("crms", 2))
            then(v.reciprocal(stat[:, 8:12], stat[:, 4:8]))
            for t in range(NT):
                for m, (a, b) in enumerate(((0, Q_LORA), (Q_LORA, Q_LORA + KV_LORA))):
                    i = v.tensor_scalar(CN[:, t, a:b], VC[:, t, 512 + a:512 + b],
                                        stat[:, 8 + 2 * m + t:9 + 2 * m + t], None, ALU.mult)
                    then(i, "cn" if (t, m) == (1, 1) else "dve")

            def rotate(dst1, dst2, x1, x2, shape, axis, f0, f1, tmp, name):
                cos, sin = (ang[:, :, ph, f0:f1] if axis is None else
                            over(ang[:, :, ph, f0:f1], shape, axis) for ph in (1, 0))
                for o, x, y in ((tmp[0], x1, cos), (tmp[1], x2, sin), (tmp[2], x2, cos),
                                (tmp[3], x1, sin)):
                    then(v.tensor_tensor(o, x, y, ALU.mult))
                then(v.tensor_tensor(dst1, tmp[0], tmp[1], ALU.subtract))
                then(v.tensor_tensor(dst2, tmp[2], tmp[3], ALU.add), name)

            dve.wait_ge(sem("trig"), upto("trig", 1))
            rotate(QR[:, :, :, 0:32], QR[:, :, :, 32:64], QK[:, :, :, 0:32], QK[:, :, :, 32:64],
                   [P, NT, 16, 32], 2, 0, 32,
                   [QR[:, :, :, 0:32], rope_t[:, :, :, :], QR[:, :, :, 32:64],
                    rope_u[:, :, :, :]], "rope_a")
            for k in range(3):
                dve.wait_ge(sem("c_T"), upto("c_T", k // 2 + 1))
                hi_lo_gain(cT_hi[:, k, :], cT_lo[:, k, :],
                           mb[k // 2][:, (k % 2) * SEQ:(k % 2 + 1) * SEQ],
                           cols[:, C_QN + k:C_QN + k + 1], "cT")
            evac("qup", lambda t, n: QB[:, t, 4 * n:4 * n + 4, :].rearrange("p h d -> p (h d)"))
            for t, n, a in banks("kvup"):
                kv = a[:, :].rearrange("p (h d) -> p h d", h=4)
                then(v.tensor_copy(KF[:, t, 4 * n:4 * n + 4, 0:B_NOPE], kv[:, :, 0:B_NOPE]))
                then(v.tensor_copy(VB[:, t, 4 * n:4 * n + 4, :], kv[:, :, B_NOPE:]), "ev_kvup")
            tmp = [rope_t[:, :, 8 * a:8 * a + 8, 16 * b:16 * b + 16] for a in range(2)
                   for b in range(2)]
            rotate(QB[:, :, :, 64:80], QB[:, :, :, 80:96], QB[:, :, :, 64:80], QB[:, :, :, 80:96],
                   [P, NT, 8, 16], 2, 32, 48, tmp, "rope_q")
            tmp = [rope_t[:, :, a, 0:16] for a in range(6)]
            rotate(tmp[4], tmp[5], VC[:, :, 896:912], VC[:, :, 912:928], None, None, 32, 48,
                   tmp[:4], "rope_k")
            for n in range(2):
                then(v.tensor_copy(KF[:, :, :, 64 + 16 * n:80 + 16 * n],
                                   over(tmp[4 + n], [P, NT, 8, 16], 2)), "rope_b")
            copies("qa", [QTA[:, 2 * b:2 * b + 2, :].rearrange("p a s -> p (a s)") for b in range(4)])
            copies("qb", [QTB[0:B_DK, 2 * b:2 * b + 2, :].rearrange("p a s -> p (a s)")
                          for b in range(8)])

            def masked(dst, src, mask, top, scale, name):
                for t, (a, b) in enumerate(((0, P), (P, 3 * P))):
                    then(v.tensor_tensor_reduce(dst[:, a:b], src[:, a:b], mask[:, a:b], 1.0, LOWEST,
                                                ALU.add, ALU.max, top[:, t:t + 1]))
                then(v.tensor_scalar(top, top, -scale, None, ALU.mult), name)

            dve.wait_ge(sem("causal"), 3)
            for u in range(A_H + B_H):
                dve.wait_ge(sem("scores"), u + 1)
                if u >= 2:
                    dve.wait_ge(sem("exp"), u - 1)
                masked(Sm[:, u % 2, :], col[u % 2], causal, mx[:, u, :],
                       (A_DH if u < A_H else B_DK) ** -0.5, "masked")
            dve.wait_ge(sem("exp"), A_H + B_H)
            then(v.reciprocal(sums[:, :, :], sums[:, :, :]))
            for br in range(2):
                dve.wait_ge(sem("pv"), 8 * br + 8)
                for t in range(NT):
                    then(v.tensor_tensor(Y[:, br, t, :, :],
                                         acc[2 * br + t][:, :].rearrange("p (h d) -> p h d", h=8),
                                         over(sums[:, 8 * br:8 * br + 8, t], [P, 8, 64], 2),
                                         ALU.mult), "y")
            stream_T("y")
            for t, n, a in banks("br_a"):
                c = slice(n * 512, (n + 1) * 512)
                then(v.tensor_tensor(M[:, t, c], a[:, :], GA[:, t, c], ALU.mult), "ev_br_a")
            for t, n, a in banks("br_b"):
                c = slice(n * 512, (n + 1) * 512)
                then(v.tensor_tensor(M2[:, t, c], a[:, :], GB[:, t, c], ALU.mult))
                then(v.tensor_tensor(M[:, t, c], M[:, t, c], M2[:, t, c], ALU.add), "ev_br_b")
            stream_T("m")
            residual("wout")
            norm_T(1)

            def top16(values, index, scores, rest):
                then(v.max(values[:, 0:8], scores))
                then(v.max_index(index[:, 0:8], values[:, 0:8], scores))
                then(v.match_replace(rest, values[:, 0:8], scores, LOWEST))
                then(v.max(values[:, 8:16], rest))
                then(v.max_index(index[:, 8:16], values[:, 8:16], rest))

            for t in range(NT):
                for n in range(16):
                    if n % 4 == 0:
                        dve.wait_ge(sem("sc"), 4 * t + n // 4 + 1)
                    top16(tk_v[:, t, n, :], tk_i[:, t, n, :], SC[:, t, n, :], tk_s2[:, 0:NKEYS])
            then(v.tensor_copy(tk_if[:, :, :, :], tk_i[:, :, :, :]))
            for t in range(NT):
                for h in range(PE_H):
                    then(v.tensor_tensor(tk_c[:, :].rearrange("p (a b) -> p a b", a=TOPK),
                                         over(tk_v[:, t, 2 * h, :], [P, TOPK, TOPK], 2),
                                         over(tk_v[:, t, 2 * h + 1, :], [P, TOPK, TOPK], 1),
                                         ALU.add))
                    top16(tk_bv[:, t, h, :], tk_bp[:, t, h, :], tk_c[:, :], tk_s2[:, :])
            then(v.tensor_scalar(tk_pa[:, 0], tk_bp[:, :, :, :], 4, None, ALU.logical_shift_right))
            then(v.tensor_scalar(tk_pa[:, 1], tk_bp[:, :, :, :], 15, None, ALU.bitwise_and))
            then(v.tensor_copy(tk_pf[:, :, :, :, :].rearrange("p m t h k -> p (m t h k)"),
                               tk_pa[:, :, :, :, :].rearrange("p m t h k -> p (m t h k)")))
            dve.wait_ge(sem("iota"), 1)
            for m in range(2):
                for t in range(NT):
                    ix = tk_if[:, t, :, :].rearrange("p (h m) a -> p m h a", m=2)[:, m]
                    e = tk_e[:, :, :, :].rearrange("p h k a -> p (h k) a")
                    then(v.tensor_tensor(
                        e, over(tk_pf[:, m, t, :, :].rearrange("p h k -> p (h k)"),
                                [P, PE_H * TOPK, TOPK], 2),
                        over(iota_row[:, 0:TOPK], [P, PE_H * TOPK, TOPK], 1), ALU.is_equal))
                    then(v.tensor_tensor(tk_e[:, :, :, :], tk_e[:, :, :, :],
                                         over(ix, [P, PE_H, TOPK, TOPK], 2), ALU.mult))
                    then(v.tensor_reduce(tk_sel[:, m, t, :, :].rearrange("p h k -> p (h k)"), e,
                                         AX_X, ALU.add))
            bv = tk_bv[:, :, :, :].rearrange("p t h k -> p (t h) k")
            then(v.tensor_copy(stat[:, 0:16], bv[:, :, 0]))
            then(v.tensor_tensor(bv, bv, over(stat[:, 0:16], [P, 16, TOPK], 2), ALU.subtract),
                 "best")
            dve.wait_ge(sem("best_exp"), upto("best_exp", 1))
            then(v.tensor_reduce(stat[:, 16:32], bv, AX_X, ALU.add))
            then(v.reciprocal(stat[:, 16:32], stat[:, 16:32]))
            then(v.tensor_tensor(bv, bv, over(stat[:, 16:32], [P, 16, TOPK], 2), ALU.mult), "picks")
            dve.wait_ge(sem("pk_T"), upto("pk_T", 1))
            hi_lo(g_hi[:, :], g_lo[:, :], mb[0][:, 0:SEQ], "dve")
            then(v.tensor_copy(i1T[:, :], mb[0][:, SEQ:2 * SEQ]), "pk_E")
            dve.wait_ge(sem("pk_T"), upto("pk_T", 2))
            then(v.tensor_copy(i2T[:, :], mb[1][:, 0:SEQ]), "pk_E")

            def hot(n, n_half, q, part):
                if not (isinstance(n, int) and n < 2):
                    dve.wait_ge(sem("gate"), n - 1)
                tok = bass.ds(n_half * 4, 4)
                v.tensor_tensor(hot2[:, q % 2, :, :], over(iota_row[:, :], [P, 4, NKEYS], 1),
                                over(i2T[:, tok], [P, 4, NKEYS], 2), ALU.is_equal).then_inc(
                    sem("hot2"), 1)
                if not (isinstance(n, int) and n == 0):
                    dve.wait_ge(sem("hot"), n)
                v.tensor_tensor(is1[:, :, :], over(iota_row[:, part * HALF:(part + 1) * HALF],
                                                   [P, 4, HALF], 1),
                                over(i1T[:, tok], [P, 4, HALF], 2), ALU.is_equal).then_inc(
                    sem("hot1"), 1)
                dve.wait_ge(sem("hot1"), n + 1)
                v.tensor_tensor(hot_hi[:, q % 2, :, :], is1[:, :, :],
                                over(g_hi[:, tok].bitcast(F32), [P, 4, HALF], 2),
                                ALU.mult).then_inc(sem("hot_hi"), 1)
                v.tensor_tensor(hot_lo[:, q % 2, :, :], is1[:, :, :],
                                over(g_lo[:, tok].bitcast(F32), [P, 4, HALF], 2),
                                ALU.mult).then_inc(sem("hot"), 1)

            def apply_gates(n, n_half, q, part):
                dve.wait_ge(sem("gate"), n + 1)
                e = act_e[:, part * HALF:(part + 1) * HALF, bass.ds(n_half * 4, 4)]
                v.tensor_tensor(e, mb[q % 2][:, 0:4 * HALF].rearrange("p (t c) -> p c t", t=4), e,
                                ALU.mult).then_inc(sem("gated"), 1)

            def gated_lo(c, q):
                dve.wait_ge(sem("W_hi"), c + 1)
                v.tensor_tensor(W_lo[:, q % 2, :], act_e[:, c, :],
                                W_hi[:, q % 2, :].bitcast(F32), ALU.subtract).then_inc(
                    sem("W_lo"), 1)

            ROUNDS = HALF // 4
            hot(0, 0, 0, 0)
            hot(1, 1, 1, 0)
            dve.wait_ge(sem("gelu"), HALF)
            with dve.Fori(0, ROUNDS - 1) as r:
                for q in range(4):
                    apply_gates(r * 4 + q, r * 4 + q, q, 0)
                    hot(r * 4 + q + 2, r * 4 + q + 2, q, 0)
            for q in range(4):
                n = HALF - 4 + q
                apply_gates(n, n, q, 0)
                hot(n + 2, (n + 2) % HALF, q, (n + 2) // HALF)
            dve.wait_ge(sem("gelu"), NKEYS)
            gated_lo(0, 0)
            with dve.Fori(0, ROUNDS - 1) as r:
                for q in range(4):
                    gated_lo(r * 4 + q + 1, q + 1)
                    apply_gates(r * 4 + q + HALF, r * 4 + q, q, 1)
                    hot(r * 4 + q + HALF + 2, r * 4 + q + 2, q, 1)
            for q in range(4):
                n = HALF - 4 + q
                if q < 3:
                    gated_lo(n + 1, q + 1)
                apply_gates(n + HALF, n, q, 1)
                if q < 2:
                    hot(n + HALF + 2, n + 2, q, 1)
            gated_lo(HALF, 0)
            with dve.Fori(ROUNDS, 2 * ROUNDS - 1) as r:
                for q in range(4):
                    gated_lo(r * 4 + q + 1, q + 1)
            for q in range(3):
                gated_lo(NKEYS - 4 + q + 1, q + 1)
            dve.wait_ge(sem("x_back"), 16)
            residual("v", XB)
            dve.wait_ge(sem("rows_in"), 16)
            rows_rstd()
            for t in range(NT):
                for h in range(2):
                    c = slice(h * 512, (h + 1) * 512)
                    v.scalar_tensor_tensor(
                        out=X[:, t, c], in0=X[:, t, c], scalar=rstd[:, t:t + 1],
                        in1=rows[:, R_FINAL + h * 512:R_FINAL + (h + 1) * 512], op0=ALU.mult,
                        op1=ALU.mult).then_inc(sem("x_final"), 1)
            norm_T(2)

            for n in range(12):
                used(dve, FIRST["qkv_e"] + n)
                y, x = QKVF[:, n, :], col[n % 2]
                tap = [cols[:, C_CONV + 4 * n + j:C_CONV + 4 * n + j + 1] for j in range(4)]
                then(v.tensor_scalar(y, x[:, 0:SEQ], tap[3], None, ALU.mult))
                for back in range(1, 4):
                    then(v.scalar_tensor_tensor(out=y[:, back:], in0=x[:, 0:SEQ - back],
                                                scalar=tap[3 - back], in1=y[:, back:], op0=ALU.mult,
                                                op1=ALU.add), "conv" if back == 3 else "dve")
            def th(ap):
                return ap.rearrange("p (t h) -> p t h", t=NT)

            dve.wait_ge(sem("ev_zba"), upto("ev_zba", 4))
            ba = stat[:, 0:16].rearrange("p (t n) -> p t n", t=NT)
            x, e, u, ln = stat[:, 40:48], stat[:, 48:56], stat[:, 24:32], stat[:, 16:24]
            d, low, r = sq32[:, 0:8], sq32[:, 8:16], sq32[:, 16:24]
            then(v.tensor_tensor(th(x), ba[:, :, 4:8], over(rows[:, R_DT:R_DT + 4], [P, NT, 4], 1),
                                 ALU.add))
            then(v.scalar_tensor_tensor(out=e, in0=x, scalar=-1.0, in1=x, op0=ALU.mult,
                                        op1=ALU.min), "sp")
            dve.wait_ge(sem("sp_exp"), upto("sp_exp", 1))
            then(v.tensor_scalar(u, e, 1.0, None, ALU.add), "sp")
            then(v.tensor_scalar(d, u, 1.0, None, ALU.subtract))
            then(v.scalar_tensor_tensor(out=low, in0=d, scalar=0.0, in1=e, op0=ALU.is_equal,
                                        op1=ALU.mult))
            then(v.tensor_scalar(r, d, 1e-30, None, ALU.max))
            then(v.reciprocal(r, r))
            then(v.tensor_tensor(r, r, e, ALU.mult))
            dve.wait_ge(sem("sp_ln"), upto("sp_ln", 1))
            then(v.tensor_tensor(r, r, ln, ALU.mult))
            then(v.tensor_tensor(r, r, low, ALU.add))
            then(v.scalar_tensor_tensor(out=r, in0=x, scalar=0.0, in1=r, op0=ALU.max, op1=ALU.add))
            dve.wait_ge(sem("beta"), upto("beta", 2))
            then(v.tensor_scalar(r, r, -1.0, None, ALU.mult))
            then(v.tensor_tensor(th(stat[:, 16:24]), th(r), over(stat[:, 60:64], [P, NT, 4], 1),
                                 ALU.mult), "g_ready")
            dve.wait_ge(sem("masks"), 20)
            copies("tok", [m[:, t, :, :].rearrange("p h d -> p (h d)") for m in (Qt, Kt, Vt)
                           for t in range(NT)])

            def groups(m):
                return m[:, :, :, :].rearrange("p t h d -> p (t h) d")

            def scale_groups(dst, src, s, name="dve"):
                then(v.tensor_tensor(groups(dst), groups(src), over(s, [P, 8, P], 2), ALU.mult),
                     name)

            for t in range(NT):
                dve.wait_ge(sem("gcT"), upto("gcT", t + 1))
                then(v.tensor_copy(gc[:, 4 * t:4 * t + 4], mb[t][:, 0:4]), "gc")
                then(v.tensor_tensor(DG[:, t, :, :], over(ident[:, :], [P, 4, P], 1),
                                     over(gc[:, 4 * t:4 * t + 4], [P, 4, P], 2), ALU.mult), "diag")
            for t in range(NT):
                dve.wait_ge(sem("gcrow"), upto("gcrow", t + 1))
                row = acc[t][:, :].rearrange("p (h f) -> p h f", h=4)
                then(v.tensor_tensor(D0[:, t, :, :], row, over(gc[:, 4 * t:4 * t + 4], [P, 4, P], 2),
                                     ALU.subtract))
                then(v.tensor_scalar(decA[:, t, :, :], D0[:, t, :, :], 0.0, None, ALU.max), "gdiff")
                then(v.tensor_scalar(decAT[:, t, :, :], D0[:, t, :, :], 0.0, None, ALU.min), "gdiff")
                then(v.tensor_copy(gl[:, 8 * t:8 * t + 8].rearrange("p (c h) -> p c h", c=2),
                                   acc[t][:, :].rearrange("p (h c f) -> p c h f", h=4, c=2)
                                   [:, :, :, G_CH - 1]), "glast")
            for m, src in enumerate((Qt, Kt)):
                then(v.tensor_tensor(groups(D0), groups(src), groups(src), ALU.mult))
                then(v.tensor_reduce(sq16[:, 8 * m:8 * m + 8], groups(D0), AX_X, ALU.add),
                     "l2" if m else "dve")
            dve.wait_ge(sem("l2_root"), upto("l2_root", 1))
            then(v.reciprocal(sq16[:, :], sq16[:, :]))
            then(v.tensor_scalar(sq16[:, 0:8], sq16[:, 0:8], G_DK ** -0.5, None, ALU.mult))
            scale_groups(Qt, Qt, sq16[:, 0:8])
            scale_groups(Kt, Kt, sq16[:, 8:16])
            scale_groups(KBt, Kt, stat[:, 32:40])
            scale_groups(VBt, Vt, stat[:, 32:40])
            dve.wait_ge(sem("egc"), upto("egc", 1))
            scale_groups(QDt, Qt, egc[:, :])
            scale_groups(KBE, KBt, egc[:, :], "tokmaps")
            dve.wait_ge(sem("dec"), 4)
            for t in range(NT):
                for c in range(2):
                    rr = slice(G_CH * c, G_CH * c + G_CH)
                    last = G_CH * c + G_CH - 1
                    then(v.tensor_tensor(KDt[rr, t, :, :], Kt[rr, t, :, :],
                                         over(decAT[rr, t, :, last], [G_CH, 4, P], 2), ALU.mult))
            for dst, src, m in ((decQ, decAT, 2), (decAT, decAT, 1), (decA, decA, 0)):
                then(v.tensor_tensor(groups(dst), groups(src), over(masks[:, m, :], [P, 8, P], 1),
                                     ALU.mult))
            for f in range(8):
                dve.wait_ge(sem("fT_T"), upto("fT_T", f + 1))
                then(v.tensor_copy(fT[:, f % 4, f // 4, :, :].rearrange("p h d -> p (h d)"),
                                   mb[f % 2][:, :]), "fT_E")

            def four(m, t):
                return m[:, t, :, :]

            plain = {"N2": N2, "N2T": N2T, "N4": N4, "N4T": N4T, "N8": N8, "P1": P1, "P2": P2,
                     "u": Ut, "wT": wT}
            for s, (result, _, _, _) in enumerate(SOLVE):
                for t in range(NT):
                    n = NT * s + t
                    dve.wait_ge(sem("sv"), n + 1)
                    src = (acc + col)[n % 6][:, :].rearrange("p (h f) -> p h f", h=4)
                    if result in plain:
                        then(v.tensor_copy(four(plain[result], t), src), "sv_E")
                    elif result == "qkT":
                        then(v.tensor_tensor(four(qkT, t), src, four(decQ, t), ALU.mult), "sv_E")
                    elif result in ("a", "aT"):
                        m, n1, y, dec = ((aM, N1, YI, decA) if result == "a" else
                                         (aT, N1T, YIT, decAT))
                        then(v.tensor_tensor(four(m, t), src, four(dec, t), ALU.mult))
                        then(v.tensor_tensor(four(n1, t), four(m, t),
                                             over(masks[:, 3, :], [P, 4, P], 1), ALU.mult))
                        then(v.tensor_tensor(four(y, t), over(ident[:, :], [P, 4, P], 1),
                                             four(n1, t), ALU.subtract), "sv_E")
                    else:
                        y = YIT if result.startswith("YT") else YI
                        if s in (11, 12):
                            then(v.tensor_tensor(four(L1T if s == 11 else L2T, t), four(aT, t),
                                                 over(masks[:, 4 if s == 11 else 5, :], [P, 4, P], 1),
                                                 ALU.mult))
                        if result.endswith("+"):
                            then(v.tensor_tensor(four(y, t), src, four(y, t), ALU.add), "sv_E")
                        else:
                            then(v.tensor_tensor(four(y, t), four(y, t), src, ALU.subtract), "sv_E")

            dve.wait_ge(sem("gl"), 2)
            for c in range(SEQ // G_CH):
                t, rr = c // 2, slice(G_CH * (c % 2), G_CH * (c % 2) + G_CH)
                if c:
                    dve.wait_ge(sem("wS"), c)
                    then(v.tensor_tensor(Vn[rr, t, :, :], Ut[rr, t, :, :],
                                         col[0][rr, :].rearrange("p (h f) -> p h f", h=4),
                                         ALU.subtract), "v_new")
                else:
                    then(v.tensor_copy(Vn[rr, t, :, :], Ut[rr, t, :, :]), "v_new")
                if c < SEQ // G_CH - 1:
                    dve.wait_ge(sem("dS"), c + 1)
                    if c:
                        for h in range(G_H):
                            g = 8 * t + 4 * (c % 2) + h
                            then(v.scalar_tensor_tensor(
                                out=St[:, h, :], in0=St[:, h, :], scalar=gl[:, g:g + 1],
                                in1=mb[c % 2][:, h * P:(h + 1) * P], op0=ALU.mult, op1=ALU.add),
                                "state" if h == G_H - 1 else "dve")
                    else:
                        then(v.tensor_copy(St[:, :, :].rearrange("p h f -> p (h f)"), mb[0][:, :]),
                             "state")
                dve.wait_ge(sem("o_T"), c + 1)
                then(v.tensor_copy(Ot[rr, t, :, :],
                                   col[1][rr, :].rearrange("p (h f) -> p h f", h=4)), "o_E")
            then(v.tensor_tensor(groups(decA), groups(Ot), groups(Ot), ALU.mult))
            then(v.tensor_reduce(stat[:, 0:8], groups(decA), AX_X, ALU.add), "o_ss")
            dve.wait_ge(sem("o_root"), upto("o_root", 1))
            then(v.reciprocal(stat[:, 0:8], stat[:, 0:8]))
            scale_groups(Ot, Ot, stat[:, 0:8])
            then(v.tensor_tensor(groups(Ot), groups(Ot),
                                 over(rows[:, R_OG:R_OG + P], [P, 8, P], 1), ALU.mult))
            then(v.tensor_tensor(OC[:, :, 512:1024], Ot[:, :, :, :].rearrange("p t h d -> p t (h d)"),
                                 Z[:, :, :], ALU.mult))
            dve.wait_ge(sem("ev_uv"), upto("ev_uv", 4))
            gv = UV[:, :, 512:1024].rearrange("p t (g d) -> p t g d", g=M_G)
            scr = decA[:, :, :, :]
            th4 = lambda ap: over(th(ap), [P, NT, M_G, P], 3)
            then(v.tensor_reduce(th(sq32[:, 0:8]), gv, AX_X, ALU.add))
            then(v.tensor_scalar(sq32[:, 0:8], sq32[:, 0:8], 1.0 / P, None, ALU.mult))
            then(v.tensor_tensor(gv, gv, th4(sq32[:, 0:8]), ALU.subtract))
            then(v.tensor_tensor(scr, gv, gv, ALU.mult))
            then(v.tensor_reduce(th(stat[:, 8:16]), scr, AX_X, ALU.add), "v_ss")
            dve.wait_ge(sem("v_root"), upto("v_root", 1))
            then(v.reciprocal(stat[:, 8:16], stat[:, 8:16]))
            then(v.tensor_tensor(gv, gv, th4(stat[:, 8:16]), ALU.mult))
            then(v.tensor_tensor(UV[:, :, 512:1024], UV[:, :, 512:1024],
                                 over(rows[:, R_VG:R_VG + 512], [P, NT, 512], 1), ALU.mult), "gv")
            for t in range(NT):
                dve.wait_ge(sem("mix"), upto("mix", t + 1))
                for g in range(M_G):
                    c = slice(g * P, (g + 1) * P)
                    then(v.scalar_tensor_tensor(out=OC[:, t, c], in0=acc[t][:, c],
                                                scalar=cols[:, C_BS + g:C_BS + g + 1],
                                                in1=UV[:, t, c], op0=ALU.add, op1=ALU.mult),
                         "oc" if (t, g) == (1, 3) else "dve")
            stream_T("oc")
            residual("out_e")

            def mlp(layer):
                j0 = FIRST[f"mlp{layer}"]
                f0 = layer * D_FF // P

                def squares(blk, s):
                    dve.wait_ge(sem("square"), blk + 1 + f0)
                    v.tensor_copy(H_hi[:, s, :], H_q[:, s, :]).then_inc(sem("H_hi"), 1)
                    dve.wait_ge(sem("H_hi"), blk + 1 + f0)
                    v.tensor_tensor(H_lo[:, s, :], H_q[:, s, :], H_hi[:, s, :].bitcast(F32),
                                    ALU.subtract).then_inc(sem("H"), 1)

                squares(0, 0)
                squares(1, 1)
                with dve.Fori(0, MLP_ROUNDS) as r:
                    for s in range(2):
                        used(dve, j0 + 2 + 2 * s, r)
                        squares(2 * r + 2 + s, s)
                residual(f"mlp{layer}")

            def gated_projection(layer, n):
                norm_T(n)
                dve.wait_ge(sem("p_in"), 16 * (layer + 1))
                hi_lo(p_hi[:, :, :], p_lo[:, :, :], p_raw[:, :, :], "p_split")
                for t, k, a in banks(f"ple{layer}"):
                    c = slice(k * 512, (k + 1) * 512)
                    then(v.tensor_tensor(G2[:, t, c], a[:, :], GT[:, t, c], ALU.mult))
                    then(v.tensor_tensor(X[:, t, c], X[:, t, c], G2[:, t, c], ALU.add),
                         f"ev_ple{layer}")

            norm_T(3)
            mlp(0)
            gated_projection(0, 4)

            norm_T(5)
            dve.wait_ge(sem("causal"), 6)
            dve.wait_ge(sem("iota"), 4)
            for h in range(C_H):
                then(v.scalar_tensor_tensor(out=ALIBI[:, h, :], in0=dist[:, :],
                                            scalar=-2.0 ** (-8.0 * (h + 1) / C_H), in1=causal1[:, :],
                                            op0=ALU.mult, op1=ALU.add))
            for n in range(2):
                lam = [rows[:, R_LAM + 64 * (2 * n + i):R_LAM + 64 * (2 * n + i + 1)]
                       for i in range(2)]
                then(v.tensor_tensor_reduce(SQ[:, 0, 0:64], lam[0], lam[1], 1.0, 0.0, ALU.mult,
                                            ALU.add, stat[:, n:n + 1]), "lam_dots")
            dve.wait_ge(sem("lam_exp"), upto("lam_exp", 1))
            then(v.tensor_scalar(stat[:, 4:5], stat[:, 2:3], stat[:, 3:4], LAM_INIT, ALU.subtract,
                                 ALU.add))
            for m, (g, src, gain) in enumerate((("q1", Q1, R_QG), ("k1", K1, R_KG))):
                evac(g, half(src))
                x = src[:, :, :].rearrange("p t (n d) -> p (t n) d", d=C_DH)
                y = SQ[:, :, :].rearrange("p t (n d) -> p (t n) d", d=C_DH)
                then(v.tensor_tensor(y, x, x, ALU.mult))
                then(v.tensor_reduce(sq32[:, :], y, AX_X, ALU.add), "qk_ss")
                dve.wait_ge(sem("qk_root"), upto("qk_root", m + 1))
                then(v.reciprocal(sq32[:, :], sq32[:, :]))
                if m == 0:
                    then(v.tensor_scalar(sq32[:, :], sq32[:, :], C_DH ** -0.5, None, ALU.mult))
                then(v.tensor_tensor(x, x, over(sq32[:, :], [P, 32, C_DH], 2), ALU.mult))
                then(v.tensor_tensor(x, x, over(rows[:, gain:gain + C_DH], [P, 32, C_DH], 1),
                                     ALU.mult), "qk1")
            evac("v1", half(V1))
            copies("qk1", [QKT[:, 2 * b:2 * b + 2, :].rearrange("p a s -> p (a s)")
                           for b in range(8)])

            def masked1(w):
                dve.wait_ge(sem("scores1"), w + 1)
                if w >= 2:
                    dve.wait_ge(sem("exp1"), w - 1)
                masked(S1[:, w % 2, :], col[w % 2], ALIBI[:, w // 2, :], mx1[:, w, :], 1.0,
                       "masked1")

            masked1(0)
            masked1(1)
            for h in range(C_H):
                if h + 1 < C_H:
                    masked1(2 * h + 2)
                    masked1(2 * h + 3)
                dve.wait_ge(sem("exp1"), 2 * h + 2)
                s01 = sum1[:, 2 * h:2 * h + 2, :]
                then(v.reciprocal(s01, s01))
                then(v.tensor_scalar(sum1[:, 2 * h + 1, :], sum1[:, 2 * h + 1, :], stat[:, 4:5],
                                     None, ALU.mult))
                p0, p1 = PR1[:, (2 * h) % 4, :], PR1[:, (2 * h + 1) % 4, :]
                for t, (a, b) in enumerate(((0, P), (P, 3 * P))):
                    then(v.tensor_scalar(p1[:, a:b], p1[:, a:b], sum1[:, 2 * h + 1, t:t + 1], None,
                                         ALU.mult))
                    then(v.scalar_tensor_tensor(out=p0[:, a:b], in0=p0[:, a:b],
                                                scalar=sum1[:, 2 * h, t:t + 1], in1=p1[:, a:b],
                                                op0=ALU.mult, op1=ALU.subtract),
                         "attn1" if t else "dve")
            dve.wait_ge(sem("pv1"), C_H)
            for t in range(NT):
                for n in range(2):
                    then(v.tensor_copy(O1[:, t, n * 512:(n + 1) * 512], acc[2 * t + n][:, :]))
            x = O1[:, :, :].rearrange("p t (n d) -> p (t n) d", d=P)
            y = SQ[:, :, :].rearrange("p t (n d) -> p (t n) d", d=P)
            then(v.tensor_tensor(y, x, x, ALU.mult))
            then(v.tensor_reduce(sq32[:, 0:16], y, AX_X, ALU.add), "o1_ss")
            dve.wait_ge(sem("o1_root"), upto("o1_root", 1))
            then(v.reciprocal(sq32[:, 0:16], sq32[:, 0:16]))
            then(v.tensor_scalar(sq32[:, 0:16], sq32[:, 0:16], 1.0 - LAM_INIT, None, ALU.mult))
            then(v.tensor_tensor(x, x, over(sq32[:, 0:16], [P, 16, P], 2), ALU.mult))
            then(v.tensor_tensor(x, x, over(rows[:, R_SG:R_SG + P], [P, 16, P], 1), ALU.mult), "o1")
            stream_T("o1")
            residual("out_o")
            norm_T(6)
            mlp(1)
            gated_projection(1, 7)


def kernel(**inputs):
    import concourse.bacc as bacc
    from concourse.bass_utils import run_bass_kernel_spmd

    a = {k: np.ascontiguousarray(x) for k, x in inputs.items()}

    def col_form(w):
        k, n = w.shape
        return np.ascontiguousarray(w.reshape(k // P, P, n // P, P).transpose(2, 1, 0, 3)).reshape(
            n // P, P, k)

    def columns(v):
        return v.reshape(-1, P).T

    gains = [a["mix_norm_g"][0], a["ffn_norm_g"][0], a["ln_mix_e_2"][0], a["ln_mlp_2"][0],
             a["ln_ple_2"][0], a["ln_mix_o_2"][0], a["ln_mlp_2"][1], a["ln_ple_2"][1]]
    conv = a["gdn_conv_2"][0].reshape(4, 12, P).transpose(2, 1, 0).reshape(P, 48)
    w_in_e = a["w_in_e_2"][0]
    freqs = [np.float32(10000.0) ** (-np.arange(0, dim, 2, dtype=np.float32) / np.float32(dim))
             for dim in (A_DH, B_ROPE)]
    keys = np.stack([a["peer_sub_keys_1"][0], a["peer_sub_keys_2"][0]], 1)
    arrays = {
        "x": a["x"][0],
        "positions": a["positions"][0].reshape(NT, P).T,
        "freqs": np.concatenate(freqs).astype(np.float32)[None],
        "cols": np.concatenate([columns(g) for g in gains] + [
            columns(a["q_norm_g"][0]), columns(a["kv_norm_g"][0]), conv, a["gmlp_bs_2"][0].T], 1),
        "rows": np.concatenate([
            a["final_norm_g"], a["gmlp_v_gain_2"][0], a["gdn_out_gain_2"][0], a["attn_q_gain_2"][0],
            a["attn_k_gain_2"][0], a["attn_sub_gain_2"][0], a["diff_lambda_2"][0].reshape(-1),
            a["gdn_a_log_2"][0], a["gdn_dt_bias_2"][0]])[None],
        "w_in": a["w_in"][0],
        "w_q_up": a["w_q_up"][0],
        "w_kv_up": a["w_kv_up"][0],
        "w_branch_a": a["w_branch_a"][0],
        "w_branch_b": a["w_branch_b"][0],
        "w_out": a["w_out"][0],
        "w_query": col_form(a["w_peer_query"][0]),
        "sub_keys": keys.transpose(3, 0, 1, 2).reshape(P, 16, NKEYS),
        "expert_u": col_form(a["peer_expert_u"][0].T),
        "expert_v": a["peer_expert_v"][0],
        "w_in_e": np.concatenate([w_in_e[:, :2560], w_in_e[:, 2560:]], 1),
        "w_qkv_e": col_form(w_in_e[:, 1024:2560]),
        "gmlp_w": a["gmlp_ws_2"][0].transpose(2, 0, 1),
        "w_out_e": a["w_out_e_2"][0],
        "w_qkv_o": a["w_qkv_o_2"][0],
        "w_out_o": a["w_out_o_2"][0],
        "p": a["p_2"][:, 0].transpose(0, 2, 1).reshape(2, PLE // P, P, SEQ).transpose(0, 2, 1, 3),
    }
    for n in range(2):
        arrays[f"w_mlp1_{n}"] = col_form(a["w_mlp1_2"][n])
        arrays[f"w_mlp2_{n}"] = a["w_mlp2_2"][n]
        arrays[f"w_gate_{n}"] = a["w_ple_gate_2"][n]
        arrays[f"w_ple_{n}"] = a["w_ple_proj_2"][n]
    arrays = {k: np.ascontiguousarray(x) for k, x in arrays.items()}

    nc = bacc.Bacc("TRN2", target_bir_lowering=False, num_devices=1)
    feeds = {f"in_{k}": x for k, x in arrays.items()}
    ins = {k: nc.dram_tensor(f"in_{k}", x.shape, mybir.dt.from_np(x.dtype),
                             kind="ExternalInput").ap() for k, x in arrays.items()}
    out = nc.dram_tensor("out_x", [SEQ, D], F32, kind="ExternalOutput").ap()
    program(nc, ins, out)
    r = run_bass_kernel_spmd(nc, [feeds], core_ids=[0])
    return r.results[0]["out_x"].reshape(1, SEQ, D)
```

```python
from contextlib import ExitStack
import math

import numpy as np
import concourse.bass as bass
from concourse import mybir

F32 = mybir.dt.float32
F32R = mybir.dt.float32r
BF16 = mybir.dt.bfloat16
U32 = mybir.dt.uint32
I32 = mybir.dt.int32
ACT = mybir.ActivationFunctionType
ALU = mybir.AluOpType
AX_X = mybir.AxisListType.X

P = 128
SEQ, D = 256, 1024
NT = SEQ // P
KD = D // P
NEG = -1e30
LOWEST = -3.0e38
EPS = 1e-6

A_H, A_DH = 8, 64
B_H, B_NOPE, B_ROPE, B_V = 8, 64, 32, 64
B_DK = B_NOPE + B_ROPE
Q_LORA, KV_LORA = 256, 128
VC_W = 512 + Q_LORA + KV_LORA + B_ROPE
PE_H, NKEYS, TOPK = 8, 128, 16
G_H, G_DK, G_CH = 4, 128, 64
M_G = 4
C_H, C_DH = 8, 64
ROUND = 1.5 * 2.0 ** 23
TURN = [6.28125, 0.00193500518798828125, 2 * math.pi - 6.28125 - 0.00193500518798828125]
D_FF = 4 * D
PLE = 256
LAM_INIT = 0.8 - 0.6 * math.exp(-0.3)

RING = 4
AHEAD = 3

GAINS = ["mix", "ffn", "ln_e", "mlp0", "ple0", "ln_o", "mlp1", "ple1"]
C_QN = 8 * len(GAINS)
C_KVN = C_QN + 2
C_CONV = C_KVN + 1
C_BS = C_CONV + 48
C_ALL = C_BS + 4
R_FINAL = 0
R_VG = R_FINAL + D
R_OG = R_VG + 512
R_QG = R_OG + 128
R_KG = R_QG + 64
R_SG = R_KG + 64
R_LAM = R_SG + 128
R_ALOG = R_LAM + 256
R_DT = R_ALOG + 4
R_ALL = R_DT + 4
N_FREQ = A_DH // 2 + B_ROPE // 2
ROWS_OVER = -(-R_ALL // SEQ)


def chunk_plan():
    plan, first = [], {}

    def rows(name, src, blocks, c0, width):
        first[name] = len(plan)
        plan.extend((src, "row", k, c0, width) for k in blocks)

    def cols(name, src, blocks):
        first[name] = len(plan)
        plan.extend((src, "col", n, 0, D) for n in blocks)

    rows("qk", "w_in", range(KD), 0, 1024)
    rows("vc", "w_in", range(KD), 1024, VC_W)
    rows("ga", "w_in", range(KD), 1024 + VC_W, 1024)
    rows("gb", "w_in", range(KD), 2048 + VC_W, 1024)
    rows("qup", "w_q_up", range(2), 0, B_H * B_DK)
    rows("kvup", "w_kv_up", range(1), 0, B_H * (B_NOPE + B_V))
    rows("br_a", "w_branch_a", range(4), 0, D)
    rows("br_b", "w_branch_b", range(4), 0, D)
    rows("wout", "w_out", range(KD), 0, D)
    cols("query", "w_query", range(16))
    cols("u", "expert_u", range(NKEYS))
    rows("v", "expert_v", range(NKEYS), 0, D)
    cols("qkv_e", "w_qkv_e", range(12))
    rows("zba", "w_in_e", range(KD), 2560, 520)
    rows("uv", "w_in_e", range(KD), 0, 1024)
    rows("out_e", "w_out_e", range(KD), 0, D)
    for layer in range(2):
        if layer:
            for n, name in enumerate(("q1", "k1", "v1")):
                rows(name, "w_qkv_o", range(KD), n * D, D)
            rows("out_o", "w_out_o", range(KD), 0, D)
        first[f"mlp{layer}"] = len(plan)
        for f in range(D_FF // P + 1):
            if f < D_FF // P:
                plan.append((f"w_mlp1_{layer}", "col", f, 0, D))
            if f:
                plan.append((f"w_mlp2_{layer}", "row", f - 1, 0, D))
        rows(f"ple{layer}", f"w_ple_{layer}", range(PLE // P), 0, D)
        rows(f"gate{layer}", f"w_gate_{layer}", range(KD), 0, D)
    return plan, first


PLAN, FIRST = chunk_plan()
GROUPS = ["qk", "vc", "ga", "gb", "qup", "kvup", "br_a", "br_b", "wout", "v", "zba", "uv", "out_e",
          "mlp0", "ple0", "gate0", "q1", "k1", "v1", "out_o", "mlp1", "ple1", "gate1"]
U0, V0 = FIRST["u"], FIRST["v"]
HALF = NKEYS // 2

MLP_SKIP = 3
MLP_ROUNDS = (D_FF // P - 2) // 2
LOOPS = {U0: NKEYS // 4, V0: NKEYS // 4}
LOOPS.update({FIRST[f"mlp{n}"] + MLP_SKIP: MLP_ROUNDS for n in range(2)})


SOLVE = [
    ("a", "kbT", "kT", -1), ("aT", "kT", "kbT", -1),
    ("N2", "N1T", "N1", 1), ("N2T", "N1", "N1T", 1),
    ("Y+", "YT", "N2", 2), ("YT+", "N2", "YT", 2),
    ("N4", "N2T", "N2", 3), ("N4T", "N2", "N2T", 3),
    ("Y+", "YT", "N4", 6), ("YT+", "N4", "YT", 6),
    ("N8", "N4T", "N4", 7),
    ("Y+", "YT", "N8", 10), ("YT+", "N8", "YT", 10),
    ("P1", "L1T", "Y", 11),
    ("Y-", "YT", "P1", 13), ("YT-", "P1", "YT", 13),
    ("P2", "L2T", "Y", 14),
    ("YT-", "P2", "YT", 16),
    ("u", "YT", "VB", 17), ("wT", "KBE", "YT", 17), ("qkT", "kT", "qT", -1),
]


PLAIN = ("N2", "N2T", "N4", "N4T", "N8", "P1", "P2", "u", "wT")
MIX_AT, GMLP_T_AT = 4, 10


def solved(n):
    act = sum(SOLVE[i // NT][0] in PLAIN for i in range(n))
    return n - act, act


def share(semaphore, signals):
    base, shared = 0, {}
    for name, count in signals:
        shared[name] = (semaphore, base)
        base += count
    return shared


SHARED = {
    **share("acc_read_dve", [("ev_" + g, 4) for g in (
        "qk", "vc", "qup", "kvup", "br_a", "br_b", "wout", "v", "out_e", "mlp0", "ple0", "q1", "k1",
        "v1", "out_o", "mlp1", "ple1")]),
    **share("acc_read_act", [("ev_" + g, 4) for g in ("ga", "gb", "zba", "uv", "gate0", "gate1")]),
    **share("x_gated", [("x_ple0", 4), ("x_ple1", 4)]),
    **share("filled", [("c_T", 2), ("qa_T", 4), ("qb_T", 8), ("pT", 16), ("y_T", 4), ("m_T", 4),
                       ("pk_T", 2), ("tok_T", 6), ("fT_T", 8), ("oc_T", 4), ("qk1_T", 8), ("aT", 8),
                       ("o1_T", 4)]),
    **share("fill_read_dve", [("qb_E", 4), ("y_E", 4), ("m_E", 4), ("pk_E", 2),
                              ("tok_E", 6), ("fT_E", 4), ("oc_E", 4), ("qk1_E", 8), ("o1_E", 4)]),
    **share("fill_read_act", [("qa_E", 4), ("qb_A", 4), ("pT_E", 16), ("fT_A", 4), ("aT_E", 8)]),
    **share("stream_hi", [("y_H", 4), ("m_H", 4), ("oc_H", 4), ("o1_H", 4)]),
    **share("small_act", [("trig", 1), ("crms", 2), ("best_exp", 1), ("beta", 2), ("sp_exp", 1),
                          ("sp_ln", 1), ("l2_ss", 1), ("egc", 1), ("v_ss", 1), ("qd", 1),
                          ("kbe", 1), ("o_ss", 2),
                          ("lam_exp", 1), ("qk_root", 2), ("o1_ss", 4)]),
    **share("small_dve", [("angles", 1), ("cn", 1), ("rope_a", 1), ("cT", 3), ("rope_q", 1),
                          ("rope_k", 1), ("rope_b", 2), ("y", 4), ("best", 1), ("picks", 1),
                          ("x_final", 4), ("sp", 2), ("g_ready", 1), ("k_map", 1),
                          ("q_map", 1), ("kb_map", 1), ("kd_factor", 1), ("y0", 1), ("oc", 2), ("lam_dots", 2),
                          ("o1", 2)]),
    **share("small_pool", [("l2_r", 1), ("v_mean", 1), ("vb", 1), ("v_r", 1), ("gv", 1), ("kd", 1),
                           ("dec_q", 1), ("zg", 1), ("o_r", 2),
                           ("o1_r", 4)]),
    **share("small_pe", [("gcT", 2), ("gcrow", 2), ("mix", 2)]),
}


def program(nc, ins, out):
    ctx = ExitStack()
    with ctx:
        base = -(-nc.sbuf_base // 32) * 32

        def at(name, offset, shape, dtype=F32):
            return nc.alloc_sbuf_tensor_at(name, shape, dtype, offset=base + offset)

        sems = {}

        def sem(name):
            name = SHARED.get(name, (name, 0))[0]
            if name not in sems:
                sems[name] = ctx.enter_context(nc.semaphore(name))
            return sems[name]

        def upto(name, value):
            return value + SHARED.get(name, (name, 0))[1]

        KB = 1024
        BIG, HT, MISC = 48 * KB, 176 * KB, 192 * KB
        w_raw = at("w_raw", 0, [P, RING, 1024])
        w_hi = at("w_hi", 16 * KB, [P, RING, 1024], F32R)
        w_lo = at("w_lo", 32 * KB, [P, RING, 1024], F32R)
        hT_hi = at("hT_hi", HT, [P, KD, SEQ], F32R)
        hT_lo = at("hT_lo", HT + 8 * KB, [P, KD, SEQ], F32R)
        misc_at = [MISC]

        def small(name, shape, dtype=F32):
            size = (2 if dtype == BF16 else 4) * int(np.prod(shape[1:]))
            t = at(name, misc_at[0], shape, dtype)
            misc_at[0] += -(-size // 32) * 32
            return t

        ident = small("ident", [P, P])
        iota_row = small("iota_row", [P, P])
        cols = small("cols", [P, C_ALL])
        GT_AT = misc_at[0]
        g_parts = small("g_parts", [P, 2, SEQ], F32R)
        i1T = small("i1T", [P, SEQ], BF16)
        i2T = small("i2T", [P, SEQ], BF16)
        HOT2 = misc_at[0]
        hot2 = small("hot2", [P, 2, 4, NKEYS], F32R)
        IS1 = misc_at[0]
        is1 = small("is1", [P, 4, HALF])
        hot1 = small("hot1", [P, 2, 4, 2, HALF], F32R)
        g4 = small("g4", [P, 4, HALF])
        causal = at("causal", GT_AT, [P, 3 * P])
        causal1 = at("causal1", HOT2 + 2 * KB, [P, 3 * P])
        WST = at("WST", HOT2, [P, M_G, P])
        masks = at("masks", GT_AT, [P, 6, P])
        ones = at("ones", HOT2 + 3 * KB + KB // 2, [P, P])
        dist = at("dist", IS1, [P, 3 * P])
        ss = small("ss", [P, 2, 2])
        ms = small("ms", [P, 2])
        rstd = small("rstd", [P, 2])
        minus_half = small("minus_half", [P, 16])
        gsum = small("gsum", [P, 8])
        gvar = small("gvar", [P, 8])
        kdf = small("kdf", [P, 8])
        epsc = small("epsc", [P, 1])
        rows_f = small("rows_f", [P, N_FREQ])
        pos_i = small("pos_i", [P, 2], I32)
        pos_f = small("pos_f", [P, 2])
        stat = small("stat", [P, 64])
        sq16 = small("sq16", [P, 16])
        sq32 = small("sq32", [P, 32])
        gc = small("gc", [P, 8])
        egc = small("egc", [P, 8])
        gl = small("gl", [P, 16])
        mx1 = small("mx1", [P, 16, 2])
        sum1 = small("sum1", [P, 16, 2])
        assert base + misc_at[0] <= nc.sbuf_usable_end, misc_at[0]

        def big(name, kb, shape, dtype=F32):
            assert kb * KB + 4 * int(np.prod(shape[1:])) <= 128 * KB, name
            return at(name, BIG + int(kb * KB), shape, dtype)

        X = big("X", 120, [P, NT, D])
        XN = big("XN", 98, [P, NT, D])
        junk = big("junk", 106, [P, NT, D])
        QK = big("QK", 0, [P, NT, 16, 64])
        VC = big("VC", 8, [P, NT, VC_W])
        GA = big("GA", 16, [P, NT, D])
        GB = big("GB", 24, [P, NT, D])
        QR = big("QR", 32, [P, NT, 16, 64])
        QTA = big("QTA", 40, [P, 8, SEQ])
        QB = big("QB", 48, [P, NT, B_H, B_DK])
        KF = big("KF", 54, [P, NT, B_H, B_DK])
        VB = big("VB", 60, [P, NT, B_H, B_V])
        QTB = big("QTB", 64, [P, 2 * B_H, SEQ])
        Sm = big("Sm", 80, [P, 2, 3 * P])
        Pr = big("Pr", 83, [P, 2, 3 * P])
        PT = big("PT", 86, [P, 2, 3 * P])
        Y = big("Y", 90, [P, 2, NT, 8, 64])
        rope_t = big("rope_t", 114, [P, NT, 16, 32])
        rope_u = big("rope_u", 109, [P, NT, 16, 32])
        ang = big("ang", 118, [P, NT, 2, N_FREQ])
        ang_k = big("ang_k", 118.75, [P, NT, 2, N_FREQ])
        CN = big("CN", 106, [P, NT, 384])
        mx = big("mx", 119.5, [P, 16, 2])
        sums = big("sums", 119.625, [P, 16, 2])
        M = big("M", 0, [P, NT, D])
        M2 = big("M2", 32, [P, NT, D])
        cT_hi = big("cT_hi", 40, [P, 3, SEQ], F32R)
        cT_lo = big("cT_lo", 43, [P, 3, SEQ], F32R)
        act_e = big("act_e", 0, [P, NKEYS, SEQ])
        QPT = big("QPT", 64, [P, 16, SEQ])
        KST = big("KST", 80, [P, 16, NKEYS])
        SC = big("SC", 88, [P, NT, 16, NKEYS])
        tk_s2 = big("tk_s2", 104, [P, 256])
        tk_v = big("tk_v", 105, [P, NT, 16, TOPK])
        tk_i = big("tk_i", 107, [P, NT, 16, TOPK], U32)
        tk_if = big("tk_if", 109, [P, NT, 16, TOPK])
        tk_bv = big("tk_bv", 111, [P, NT, PE_H, TOPK])
        tk_bp = big("tk_bp", 112, [P, NT, PE_H, TOPK], U32)
        tk_pa = big("tk_pa", 113, [P, 2, NT, PE_H, TOPK], U32)
        tk_pf = big("tk_pf", 115, [P, 2, NT, PE_H, TOPK])
        tk_c = big("tk_c", 117, [P, 256])
        tk_sel = big("tk_sel", 118, [P, 2, NT, PE_H, TOPK])
        tk_e = big("tk_e", 96, [P, PE_H, TOPK, TOPK])
        W_hi = at("W_hi", HT, [P, 4, SEQ], F32R)
        W_lo = at("W_lo", HT + 12 * KB, [P, 4, SEQ], F32R)
        XB = at("XB", HT + 4 * KB, [P, NT, D])
        rows = big("rows", 0, [P, R_ALL])

        QKVF = big("QKVF", 9, [P, 12, SEQ])
        UV = big("UV", 21, [P, NT, D])
        Z = big("Z", 29, [P, NT, 512])
        Qt = big("Qt", 33, [P, NT, G_H, P])
        Kt = big("Kt", 37, [P, NT, G_H, P])
        Vt = big("Vt", 41, [P, NT, G_H, P])
        KBt = big("KBt", 45, [P, NT, G_H, P])
        KBE = big("KBE", 49, [P, NT, G_H, P])
        VBt = big("VBt", 53, [P, NT, G_H, P])
        QDt = big("QDt", 57, [P, NT, G_H, P])
        KDt = big("KDt", 61, [P, NT, G_H, P])
        fT = big("fT", 65, [P, 4, NT, G_H, P])
        decA = big("decA", 81, [P, NT, G_H, P])
        decAT = big("decAT", 85, [P, NT, G_H, P])
        decQ = big("decQ", 89, [P, NT, G_H, P])
        D0 = big("D0", 93, [P, NT, G_H, P])
        aT = big("aT", 101, [P, NT, G_H, P])
        N1 = big("N1", 97, [P, NT, G_H, P])
        N1T = big("N1T", 57, [P, NT, G_H, P])
        N2 = big("N2", 105, [P, NT, G_H, P])
        N2T = big("N2T", 109, [P, NT, G_H, P])
        N4 = big("N4", 113, [P, NT, G_H, P])
        N4T = big("N4T", 9, [P, NT, G_H, P])
        N8 = big("N8", 13, [P, NT, G_H, P])
        YI = big("YI", 17, [P, NT, G_H, P])
        YIT = big("YIT", 93, [P, NT, G_H, P])
        L1T = big("L1T", 105, [P, NT, G_H, P])
        P1 = big("P1", 109, [P, NT, G_H, P])
        L2T = big("L2T", 113, [P, NT, G_H, P])
        P2 = big("P2", 9, [P, NT, G_H, P])
        Ut = big("Ut", 45, [P, NT, G_H, P])
        wT = big("wT", 57, [P, NT, G_H, P])
        qkT = big("qkT", 13, [P, NT, G_H, P])
        Vn = big("Vn", 113, [P, NT, G_H, P])
        St = big("St", 117, [P, G_H, P])
        Ot = big("Ot", 17, [P, NT, G_H, P])
        DG = big("DG", 105, [P, NT, G_H, P])
        OC = big("OC", 37, [P, NT, D])
        decATm = big("decATm", 113, [P, NT, G_H, P])
        Q1 = big("Q1", 9, [P, NT, D])
        K1 = big("K1", 17, [P, NT, D])
        V1 = big("V1", 25, [P, NT, D])
        QKT = big("QKT", 33, [P, 16, SEQ])
        ALIBI = big("ALIBI", 49, [P, C_H, 3 * P])
        S1 = big("S1", 61, [P, 2, 3 * P])
        PR1 = big("PR1", 64, [P, 4, 3 * P])
        PT1 = big("PT1", 70, [P, 2, 3 * P])
        O1 = big("O1", 73, [P, NT, D])
        SQ = big("SQ", 81, [P, NT, D])
        H_hi = big("H_hi", 33, [P, 2, SEQ], F32R)
        H_lo = big("H_lo", 35, [P, 2, SEQ], F32R)
        H_r = big("H_r", 37, [P, 2, SEQ])
        H_q = big("H_q", 39, [P, 2, SEQ])
        p_raw = big("p_raw", 41, [P, 2, SEQ])
        p_hi = big("p_hi", 43, [P, 2, SEQ], F32R)
        p_lo = big("p_lo", 45, [P, 2, SEQ], F32R)
        GT = big("GT", 89, [P, NT, D])
        G2 = big("G2", 81, [P, NT, D])

        x_dram = ins["x"].rearrange("(t p) d -> p t d", p=P)
        out_dram = out.rearrange("(t p) d -> p t d", p=P)
        x_spill = nc.dram_tensor("x_spill", [P, NT * D], F32).ap()

        acc = [ctx.enter_context(nc.psum_tensor(f"acc{i}", [P, 512], F32)) for i in range(4)]
        col = [ctx.enter_context(nc.psum_tensor(f"col{i}", [P, 512], F32)) for i in range(2)]
        mb = [ctx.enter_context(nc.psum_tensor(f"mb{i}", [P, 512], F32)) for i in range(2)]

        norm_banks = [col[0], col[1], mb[0], mb[1]]

        block = ctx.enter_context(nc.Block())

        def src_of(j):
            name, kind, b, c0, width = PLAN[j]
            if kind == "col":
                return ins[name][b]
            return ins[name][b * P:(b + 1) * P, c0:c0 + width]

        def splits_of(j):
            width = PLAN[j][4]
            if width == VC_W:
                return [(0, 512), (512, VC_W)]
            if width == 520:
                return [(0, 512), (512, 520)]
            return [(0, width // 2), (width // 2, width)]

        last_of = {g: FIRST[g] - 1 for g in GROUPS}
        for g in GROUPS:
            if g.startswith("mlp"):
                last_of[g] = FIRST[g] + 2 * D_FF // P - 1
            else:
                last_of[g] = FIRST[g]
                while last_of[g] + 1 < len(PLAN) and last_of[g] + 1 not in FIRST.values():
                    last_of[g] += 1

        def acc_full(eng, g, bank):
            if bank < 3:
                eng.wait_ge(sem("acc_full"), 3 * GROUPS.index(g) + bank + 1)
            else:
                used(eng, last_of[g])

        def used(eng, j, i=0):
            eng.wait_ge(sem(f"used{j % RING}"), upto(f"used{j % RING}", j // RING + i + 1))

        @block.sync
        def _(sp):
            sp.dma_start(X[:, 0, :], x_dram[:, 0, :]).then_inc(sem("x0_in"), 16)
            sp.dma_start(cols[:, :], ins["cols"]).then_inc(sem("cols_in"), 16)

            def load(j, src=None, i=0):
                s = j % RING
                use = j // RING + i
                if j >= RING:
                    sp.wait_ge(sem(f"hi{s}"), upto(f"hi{s}", use))
                    sp.wait_ge(sem(f"lo{s}"), upto(f"lo{s}", use))
                width = PLAN[j][4]
                sp.dma_start(w_raw[:, s, 0:width], src_of(j) if src is None else src).then_inc(
                    sem(f"raw{s}"), 16)

            j = 0
            while j < len(PLAN):
                if j == RING:
                    sp.dma_start(pos_i[:, :], ins["positions"]).then_inc(sem("pos_in"), 16)
                    sp.dma_start(rows_f[:, :], ins["freqs"].to_broadcast([P, N_FREQ])).then_inc(
                        sem("freq_in"), 16)
                if j == FIRST["query"] + 8:
                    sp.wait_ge(sem("ev_wout"), upto("ev_wout", 4))
                    sp.dma_start(x_spill, X[:, :, :]).then_inc(sem("x_spilled"), 16)
                    sp.dma_start(KST[:, :, :], ins["sub_keys"]).then_inc(sem("keys_in"), 16)
                if j == FIRST["qkv_e"]:
                    used(sp, V0 - 1)
                    sp.wait_ge(sem("x_spilled"), 16)
                    sp.dma_start(XB[:, :, :], x_spill).then_inc(sem("x_back"), 16)
                    sp.wait_ge(sem("gate"), NKEYS)
                    sp.dma_start(WST[:, :, :], ins["gmlp_w"]).then_inc(sem("wst_in"), 16)
                    sp.wait_ge(sem("W_lo"), ROWS_OVER)
                    sp.dma_start(rows[:, :], ins["rows"].to_broadcast([P, R_ALL])).then_inc(
                        sem("rows_in"), 16)
                for layer in range(2):
                    if j == FIRST[f"ple{layer}"]:
                        mixed = "ev_out_o" if layer else "ev_out_e"
                        sp.wait_ge(sem(mixed), upto(mixed, 4))
                        sp.dma_start(p_raw[:, :, :], ins["p"][layer]).then_inc(sem("p_in"), 16)
                if j in LOOPS:
                    with sp.Fori(0, LOOPS[j]) as i:
                        for q in range(4):
                            name, kind, b = PLAN[j + q][:3]
                            n = i * (PLAN[j + 4 + q][2] - b) + b
                            src = ins[name][n] if kind == "col" else ins[name][bass.ds(n * P, P), :]
                            load(j + q, src, i)
                    j += 4 * LOOPS[j]
                    continue
                load(j)
                j += 1
            sp.wait_ge(sem("x_ple1"), upto("x_ple1", 4))
            sp.dma_start(out_dram, X[:, :, :]).then_inc(sem("stored"), 16)
            sp.wait_ge(sem("stored"), 16)
            sp.wait_ge(sem("x_spilled"), 16)

        @block.tensor
        def _(pe):
            mm = nc.tensor.matmul

            def chunk_in(j, i=0):
                pe.wait_ge(sem(f"hi{j % RING}"), upto(f"hi{j % RING}", j // RING + i + 1))
                pe.wait_ge(sem(f"lo{j % RING}"), upto(f"lo{j % RING}", j // RING + i + 1))

            def row_chunk(j, i, hi, lo, first, last, freed=None):
                s = j % RING
                chunk_in(j, i)
                for t in range(NT):
                    for n, (a, b) in enumerate(splits_of(j)):
                        o = acc[2 * t + n][:, 0:b - a]
                        if first and freed:
                            pe.wait_ge(sem(freed), upto(freed, 2 * t + n + 1))
                        mm(o, hi(t), w_hi[:, s, a:b], start=first, stop=False)
                        mm(o, hi(t), w_lo[:, s, a:b], start=False, stop=False)
                        m = mm(o, lo(t), w_hi[:, s, a:b], start=False, stop=last)
                        if last and 2 * t + n < 3:
                            m.then_inc(sem("acc_full"), 1)
                m.then_inc(sem(f"used{s}"), 1)

            def row_group(g, freed, hi=None, lo=None, blocks=None, norm=None, before=None,
                          stream=None):
                j0 = FIRST[g]
                hi = hi or (lambda k: lambda t: hT_hi[:, k, t * P:(t + 1) * P])
                lo = lo or (lambda k: lambda t: hT_lo[:, k, t * P:(t + 1) * P])
                count = last_of[g] - j0 + 1
                for k in range(count):
                    b = k if blocks is None else blocks[k]
                    if norm is not None:
                        block_in(norm, k)
                    if stream and b % 2 == 0:
                        pe.wait_ge(sem(stream + "_E"), upto(stream + "_E", b // 2 + 1))
                    if before and k == before[0]:
                        before[1]()
                    row_chunk(j0 + k, 0, hi(b), lo(b), k == 0, k == count - 1, freed)

            def col_chunk(j, i, bank, norm=None):
                s = j % RING
                chunk_in(j, i)
                wh = w_hi[:, s, :].rearrange("p (k n) -> p k n", k=KD)
                wl = w_lo[:, s, :].rearrange("p (k n) -> p k n", k=KD)
                o = col[bank][:, 0:SEQ]
                for k in range(KD):
                    if norm is not None:
                        block_in(norm, k)
                    mm(o, wh[:, k, :], hT_hi[:, k, :], start=k == 0, stop=False)
                    mm(o, wh[:, k, :], hT_lo[:, k, :], start=False, stop=False)
                    m = mm(o, wl[:, k, :], hT_hi[:, k, :], start=False, stop=k == KD - 1)
                m.then_inc(sem(f"used{s}"), 1)

            def norm_T(n):
                for t in range(NT):
                    pe.wait_ge(sem("xn1" if t else "xn0"), n + 1)
                    for b, bank in enumerate(norm_banks):
                        for kk in range(2):
                            k = 2 * b + kk
                            m = pe.transpose(bank[:, kk * SEQ + t * P:kk * SEQ + (t + 1) * P],
                                             XN[:, t, k * P:(k + 1) * P], ident[:, :])
                        if t == NT - 1:
                            m.then_inc(sem("xnT"), 1)

            def block_in(norm, k):
                pe.wait_ge(sem("hT"), KD * norm + max(k, 1) + 1)

            def fills(name, banks, n0=0):
                for b, parts in enumerate(banks):
                    if b + n0 >= 2:
                        pe.wait_ge(sem(name + "_E"), upto(name + "_E", b + n0 - 1))
                    for c, src in parts:
                        rows_, n = src.shape[1], src.shape[0]
                        m = pe.transpose(mb[b % 2][0:rows_, c:c + n], src, ident[:, :])
                    m.then_inc(sem(name + "_T"), 1)

            pe.wait_ge(sem("ident"), 2)
            norm_T(0)
            row_group("qk", None, norm=0)
            row_group("vc", "ev_qk")
            row_group("ga", "ev_vc")
            pe.wait_ge(sem("cn"), upto("cn", 1))
            fills("c", [[(kk * SEQ + t * P, CN[:, t, k * P:(k + 1) * P])
                         for kk, k in enumerate(ks) for t in range(NT)] for ks in ((0, 1), (2,))])
            row_group("gb", "ev_ga")
            pe.wait_ge(sem("cT"), upto("cT", 3))
            for g, base, freed in (("qup", 0, "ev_gb"), ("kvup", 2, "ev_qup")):
                row_group(g, freed,
                          lambda k, base=base: lambda t: cT_hi[:, base + k, t * P:(t + 1) * P],
                          lambda k, base=base: lambda t: cT_lo[:, base + k, t * P:(t + 1) * P])

            pe.wait_ge(sem("rope_a"), upto("rope_a", 1))
            fills("qa", [[(kk * SEQ + t * P, QR[:, t, 2 * (2 * b + kk):2 * (2 * b + kk) + 2, :]
                           .rearrange("p h d -> p (h d)")) for kk in range(2) for t in range(NT)]
                         for b in range(4)])
            pe.wait_ge(sem("qa_E"), upto("qa_E", 4))
            pe.wait_ge(sem("rope_b"), upto("rope_b", 2))
            for b in range(8):
                if b >= 2:
                    read = "qb_A" if b % 2 else "qb_E"
                    pe.wait_ge(sem(read), upto(read, b // 2))
                for kk in range(2):
                    for t in range(NT):
                        m = pe.transpose(mb[b % 2][0:B_DK, kk * SEQ + t * P:kk * SEQ + (t + 1) * P],
                                         (QB if b < 4 else KF)[:, t, 2 * (b % 4) + kk, :], ident[:, :])
                m.then_inc(sem("qb_T"), 1)
            pe.wait_ge(sem("qb_E"), upto("qb_E", 4))
            pe.wait_ge(sem("qb_A"), upto("qb_A", 4))

            def qk_of(u):
                if u < A_H:
                    r = slice(64 * (u % 2), 64 * (u % 2) + 64)
                    return QTA[r, u // 2, :], QTA[r, 4 + u // 2, :]
                return QTB[0:B_DK, u - A_H, :], QTB[0:B_DK, u, :]

            def scores(u):
                if u >= 2:
                    pe.wait_ge(sem("masked"), u - 1)
                q, k = qk_of(u)
                mm(col[u % 2][:, 0:P], q[:, 0:P], k[:, 0:P], start=True, stop=True)
                mm(col[u % 2][:, P:3 * P], q[:, P:2 * P], k, start=True, stop=True).then_inc(
                    sem("scores"), 1)

            def causal_fills(u, probs, done, freed):
                if u >= 2:
                    pe.wait_ge(sem(freed), upto(freed, u - 1))
                for c in range(3):
                    m = pe.transpose(mb[u % 2][:, c * P:(c + 1) * P], probs[:, c * P:(c + 1) * P],
                                     ident[:, :])
                m.then_inc(sem(done), 1)

            def values(u, pt, v, o, done):
                mm(o(0), pt[:, 0:P], v(0), start=True, stop=True)
                mm(o(1), pt[:, P:2 * P], v(0), start=True, stop=False)
                mm(o(1), pt[:, 2 * P:3 * P], v(1), start=False, stop=True).then_inc(sem(done), 1)

            def head_values(u):
                pe.wait_ge(sem("pT_E"), upto("pT_E", u + 1))
                if u == 0:
                    pe.wait_ge(sem("ev_kvup"), upto("ev_kvup", 4))
                h = u % 8
                v = ((lambda kt: VC[:, kt, h * 64:(h + 1) * 64]) if u < A_H else
                     (lambda kt: VB[:, kt, h, :]))
                values(u, PT[:, u % 2, :], v,
                       lambda t: acc[2 * (u // 8) + t][:, h * 64:(h + 1) * 64], "pv")

            scores(0)
            scores(1)
            for u in range(A_H + B_H):
                pe.wait_ge(sem("exp"), u + 1)
                causal_fills(u, Pr[:, u % 2, :], "pT", "pT_E")
                if u + 2 < A_H + B_H:
                    scores(u + 2)
                if u:
                    head_values(u - 1)
            head_values(A_H + B_H - 1)

            for br in range(2):
                pe.wait_ge(sem("y"), upto("y", 2 * br + 2))
                fills("y", [[(kk * SEQ + t * P, Y[:, br, t, 2 * (2 * b + kk):2 * (2 * b + kk) + 2, :]
                              .rearrange("p h d -> p (h d)")) for kk in range(2) for t in range(NT)]
                            for b in range(2)], n0=2 * br)
            row_group("br_a", None, stream="y")
            row_group("br_b", "ev_br_a", blocks=[4, 5, 6, 7], stream="y")
            pe.wait_ge(sem("ev_br_b"), upto("ev_br_b", 4))

            pe.wait_ge(sem("merged"), 4)
            fills("m", [[(kk * SEQ + t * P, M[:, t, (2 * b + kk) * P:(2 * b + kk + 1) * P])
                         for kk in range(2) for t in range(NT)] for b in range(4)])
            row_group("wout", "ev_br_b", stream="m")

            norm_T(1)
            for n in range(16):
                if n >= 2:
                    pe.wait_ge(sem("qp"), n - 1)
                col_chunk(FIRST["query"] + n, 0, n % 2, norm=1 if n == 0 else None)
            pe.wait_ge(sem("keys_in"), 16)
            pe.wait_ge(sem("qp"), 16)
            for t in range(NT):
                for b in range(4):
                    f = 4 * t + b
                    if f >= 2:
                        pe.wait_ge(sem("sc"), f - 1)
                    for q in range(4):
                        n = 4 * b + q
                        m = mm(mb[f % 2][:, q * P:(q + 1) * P], QPT[:, n, t * P:(t + 1) * P],
                               KST[:, n, :], start=True, stop=True)
                    m.then_inc(sem("scT"), 1)

            def u_round(r):
                for q in range(4):
                    n = r * 4 + q
                    if not (isinstance(n, int) and n < 2):
                        pe.wait_ge(sem("gelu"), n - 1)
                    col_chunk(U0 + q, r, q % 2)
                    yield q

            def gates(n, q):
                pe.wait_ge(sem("hot"), n + 1)
                if not (isinstance(n, int) and n < 2):
                    pe.wait_ge(sem("gated"), n - 1)
                for t in range(4):
                    m = mm(mb[q % 2][:, t * P:(t + 1) * P], hot2[:, q % 2, t, :],
                           hot1[:, q % 2, t, :, :].rearrange("p a c -> p (a c)"), start=True,
                           stop=True)
                m.then_inc(sem("gate"), 1)

            def v_round(r, first=False, last=False):
                for q in range(4):
                    n = r * 4 + q
                    pe.wait_ge(sem("W_hi"), n + 1)
                    pe.wait_ge(sem("W_lo"), n + 1)
                    row_chunk(V0 + q, r, lambda t: W_hi[:, q, t * P:(t + 1) * P],
                              lambda t: W_lo[:, q, t * P:(t + 1) * P],
                              first and q == 0, last and q == 3)
                    yield q

            QUARTER = HALF // 4
            for _ in u_round(0):
                pass
            with pe.Fori(1, QUARTER) as r:
                for _ in u_round(r):
                    pass
            pe.wait_ge(sem("sc"), 8)
            pe.wait_ge(sem("picks"), upto("picks", 1))
            pick_maps = [tk_bv[:, :, :, :], tk_sel[:, 0, :, :, :], tk_sel[:, 1, :, :, :]]
            fills("pk", [[((m % 2) * SEQ + t * P, pick_maps[m][:, t].rearrange("p h k -> p (h k)"))
                          for m in ms for t in range(NT)] for ms in ((0, 1), (2,))])
            pe.wait_ge(sem("pk_E"), upto("pk_E", 2))
            for q in u_round(QUARTER):
                gates(q, q)
            with pe.Fori(QUARTER + 1, 2 * QUARTER) as r:
                for q in u_round(r):
                    gates((r - QUARTER) * 4 + q, q)

            for q in v_round(0, first=True):
                gates(HALF + q, q)
            with pe.Fori(1, QUARTER) as r:
                for q in v_round(r):
                    gates(r * 4 + q + HALF, q)
            with pe.Fori(QUARTER, 2 * QUARTER - 1) as r:
                for _ in v_round(r):
                    pass
            for _ in v_round(2 * QUARTER - 1, last=True):
                pass

            norm_T(2)
            for n in range(12):
                if n >= 2:
                    pe.wait_ge(sem("conv"), n - 1)
                col_chunk(FIRST["qkv_e"] + n, 0, n % 2, norm=2 if n == 0 else None)

            def token_major():
                pe.wait_ge(sem("silu"), 12)
                fills("tok", [[(h * P, QKVF[:, 4 * m + h, t * P:(t + 1) * P]) for h in range(G_H)]
                              for m in range(3) for t in range(NT)])

            row_group("zba", "ev_v", before=(4, token_major))
            row_group("uv", "ev_zba")

            pe.wait_ge(sem("tok_E"), upto("tok_E", 6))
            pe.wait_ge(sem("ev_uv"), upto("ev_uv", 4))
            for t in range(NT):
                if t == 0:
                    pe.wait_ge(sem("g_ready"), upto("g_ready", 1))
                mm(mb[t][:, 0:G_H], masks[:, 2, :], stat[:, 16 + 4 * t:20 + 4 * t], start=True,
                   stop=True).then_inc(sem("gcT"), 1)
            for t in range(NT):
                if t == 0:
                    pe.wait_ge(sem("ones"), 1)
                pe.wait_ge(sem("diag"), t + 1)
                mm(acc[t][:, :], ones[:, :], DG[:, t, :, :].rearrange("p h f -> p (h f)"),
                   start=True, stop=True).then_inc(sem("gcrow"), 1)
            for t in range(NT):
                for m, (src, ready) in enumerate(((Kt, "k_map"), (KBt, "kb_map"), (Qt, "q_map"),
                                                  (QDt, "qd"))):
                    f = 4 * t + m
                    if t == 0:
                        pe.wait_ge(sem(ready), upto(ready, 1))
                    if f >= 2:
                        read = "fT_A" if f % 2 else "fT_E"
                        pe.wait_ge(sem(read), upto(read, f // 2))
                    for h in range(G_H):
                        x = pe.transpose(mb[f % 2][:, h * P:(h + 1) * P], src[:, t, h, :], ident[:, :])
                    x.then_inc(sem("fT_T"), 1)
            pe.wait_ge(sem("fT_E"), upto("fT_E", 4))
            pe.wait_ge(sem("fT_A"), upto("fT_A", 4))

            def oc_blocks(part):
                return [[(kk * SEQ + t * P, OC[:, t, k * P:(k + 1) * P])
                         for kk, k in enumerate((4 * part + 2 * b, 4 * part + 2 * b + 1))
                         for t in range(NT)] for b in range(2)]

            def out_chunk(k):
                row_chunk(FIRST["out_e"] + k, 0, lambda t: hT_hi[:, k, t * P:(t + 1) * P],
                          lambda t: hT_lo[:, k, t * P:(t + 1) * P], k == 0, k == KD - 1)

            maps = {"kT": fT[:, 0], "kbT": fT[:, 1], "qT": fT[:, 2], "N1": N1, "N1T": N1T,
                    "N2": N2, "N2T": N2T, "N4": N4, "N4T": N4T, "N8": N8, "Y": YI, "YT": YIT,
                    "L1T": L1T, "P1": P1, "L2T": L2T, "P2": P2, "VB": VBt, "KBE": KBE}
            for s, (result, lhsT, rhs, need) in enumerate(SOLVE):
                if s == 4:
                    pe.wait_ge(sem("y0"), upto("y0", 1))
                if s == MIX_AT:
                    pe.wait_ge(sem("gv"), upto("gv", 1))
                    pe.wait_ge(sem("wst"), 1)
                    for t in range(NT):
                        for g in range(M_G):
                            m = mm(mb[t][:, g * P:(g + 1) * P], WST[:, g, :],
                                   UV[:, t, 512 + g * P:512 + (g + 1) * P], start=True, stop=True)
                        m.then_inc(sem("mix"), 1)
                if s == GMLP_T_AT:
                    pe.wait_ge(sem("oc"), upto("oc", 1))
                    fills("oc", oc_blocks(0))
                if result == "u":
                    pe.wait_ge(sem("vb"), upto("vb", 1))
                    pe.wait_ge(sem("kbe"), upto("kbe", 1))
                for t in range(NT):
                    n = NT * s + t
                    ready = max(NT * need + t + 1 if need >= 0 else 0, n - 5)
                    by_dve, by_act = solved(ready)
                    if by_dve > 0:
                        pe.wait_ge(sem("sv_E"), by_dve)
                    if by_act > 0:
                        pe.wait_ge(sem("sv_A"), by_act)
                    for h in range(G_H):
                        m = mm((acc + col)[n % 6][:, h * P:(h + 1) * P], maps[lhsT][:, t, h, :],
                               maps[rhs][:, t, h, :], start=True, stop=True)
                    m.then_inc(sem("sv"), 1)
            pe.wait_ge(sem("sv_E"), solved(NT * len(SOLVE))[0])
            pe.wait_ge(sem("sv_A"), solved(NT * len(SOLVE))[1])
            pe.wait_ge(sem("kd"), upto("kd", 1))
            pe.wait_ge(sem("oc_E"), upto("oc_E", 2))

            qdT = fT[:, 3]
            for c in range(SEQ // G_CH):
                t, r0 = c // 2, G_CH * (c % 2)
                r = slice(r0, r0 + G_CH)
                if c:
                    pe.wait_ge(sem("state"), c)
                    pe.wait_ge(sem("o_E"), c)
                    for h in range(G_H):
                        m = mm(col[0][r, h * P:(h + 1) * P], wT[:, t, h, r], St[:, h, :],
                               start=True, stop=True)
                    m.then_inc(sem("wS"), 1)
                    for h in range(G_H):
                        mm(col[1][r, h * P:(h + 1) * P], qdT[:, t, h, r], St[:, h, :],
                           start=h == 0, stop=False, skip_group_check=True)
                pe.wait_ge(sem("v_new"), c + 1)
                if c < SEQ // G_CH - 1:
                    for h in range(G_H):
                        m = mm(mb[c % 2][:, h * P:(h + 1) * P], KDt[r, t, h, :], Vn[r, t, h, :],
                               start=True, stop=True)
                    m.then_inc(sem("dS"), 1)
                for h in range(G_H):
                    m = mm(col[1][r, h * P:(h + 1) * P], qkT[r, t, h, r], Vn[r, t, h, :],
                           start=c == 0 and h == 0, stop=True, skip_group_check=True)
                m.then_inc(sem("o_T"), 1)
                out_chunk(c)

            pe.wait_ge(sem("oc"), upto("oc", 2))
            fills("oc", oc_blocks(1), n0=2)
            for k in range(KD // 2, KD):
                if k % 2 == 0:
                    pe.wait_ge(sem("oc_E"), upto("oc_E", k // 2 + 1))
                out_chunk(k)

            def mlp(layer, freed):
                j0 = FIRST[f"mlp{layer}"]
                f0 = layer * D_FF // P

                def w1_bank(j):
                    return ((j - j0 + 1) // 2) % 2

                def w2_slot(j):
                    return ((j - j0 - 2) // 2) % 2 if j != last_of[f"mlp{layer}"] else 1

                def first_product(f, j, i):
                    if not (isinstance(f, int) and f < 2):
                        pe.wait_ge(sem("relu"), f - 1 + f0)
                    col_chunk(j, i, w1_bank(j), norm=(6 if layer else 3) if j == j0 else None)

                def second_product(f, j, i, first, last):
                    pe.wait_ge(sem("H"), f + 1 + f0)
                    slot = w2_slot(j)
                    row_chunk(j, i, lambda t: H_hi[:, slot, t * P:(t + 1) * P],
                              lambda t: H_lo[:, slot, t * P:(t + 1) * P], first, last,
                              freed if first else None)

                first_product(0, j0, 0)
                first_product(1, j0 + 1, 0)
                second_product(0, j0 + 2, 0, True, False)
                j = j0 + MLP_SKIP
                with pe.Fori(0, MLP_ROUNDS) as r:
                    first_product(2 * r + 2, j, r)
                    second_product(2 * r + 1, j + 1, r, False, False)
                    first_product(2 * r + 3, j + 2, r)
                    second_product(2 * r + 2, j + 3, r, False, False)
                second_product(D_FF // P - 1, last_of[f"mlp{layer}"], 0, False, True)

            def gated_projection(layer, n):
                pe.wait_ge(sem("p_split"), layer + 1)
                row_group(f"ple{layer}", f"ev_mlp{layer}",
                          lambda k: lambda t: p_hi[:, k, t * P:(t + 1) * P],
                          lambda k: lambda t: p_lo[:, k, t * P:(t + 1) * P])
                norm_T(n)
                row_group(f"gate{layer}", f"ev_ple{layer}", norm=n)

            norm_T(3)
            mlp(0, "ev_out_e")
            gated_projection(0, 4)

            norm_T(5)
            row_group("q1", "ev_gate0", norm=5)
            row_group("k1", "ev_q1")
            row_group("v1", "ev_k1")
            pe.wait_ge(sem("qk1"), 2)
            fills("qk1", [[(kk * SEQ + t * P, (Q1 if b < 4 else K1)[:, t, (2 * (b % 4) + kk) * P:
                                                                 (2 * (b % 4) + kk + 1) * P])
                           for kk in range(2) for t in range(NT)] for b in range(8)])
            pe.wait_ge(sem("qk1_E"), upto("qk1_E", 8))
            pe.wait_ge(sem("ev_v1"), upto("ev_v1", 4))

            def scores1(w):
                if w >= 2:
                    pe.wait_ge(sem("masked1"), w - 1)
                h, r = w // 2, slice(C_DH * (w % 2), C_DH * (w % 2) + C_DH)
                q, k = QKT[r, h, :], QKT[r, C_H + h, :]
                mm(col[w % 2][:, 0:P], q[:, 0:P], k[:, 0:P], start=True, stop=True)
                mm(col[w % 2][:, P:3 * P], q[:, P:2 * P], k, start=True, stop=True).then_inc(
                    sem("scores1"), 1)

            def head_values1(h):
                pe.wait_ge(sem("aT_E"), upto("aT_E", h + 1))
                values(h, PT1[:, h % 2, :], lambda kt: V1[:, kt, h * P:(h + 1) * P],
                       lambda t: acc[2 * t + h // 4][:, (h % 4) * P:(h % 4 + 1) * P], "pv1")

            for w in range(4):
                scores1(w)
            for h in range(C_H):
                if h + 2 < C_H:
                    scores1(2 * h + 4)
                    scores1(2 * h + 5)
                pe.wait_ge(sem("attn1"), h + 1)
                causal_fills(h, PR1[:, (2 * h) % 4, :], "aT", "aT_E")
                if h:
                    head_values1(h - 1)
            head_values1(C_H - 1)
            for part in range(2):
                pe.wait_ge(sem("o1"), upto("o1", part + 1))
                fills("o1", [[(kk * SEQ + t * P, O1[:, t, (4 * part + 2 * b + kk) * P:
                                                    (4 * part + 2 * b + kk + 1) * P])
                              for kk in range(2) for t in range(NT)] for b in range(2)], n0=2 * part)
            row_group("out_o", None, stream="o1")
            norm_T(6)
            mlp(1, "ev_out_o")
            gated_projection(1, 7)

        @block.scalar
        def _(act):
            f = nc.scalar.activation
            counts = {}

            def then(ins, name):
                counts[name] = counts.get(name, 0) + 1
                ins.then_inc(sem(name), 1)
                act.wait_ge(sem(name), upto(name, counts[name]))

            def split(j, i=0):
                s = j % RING
                act.wait_ge(sem(f"raw{s}"), upto(f"raw{s}", (j // RING + 1 + i) * 16))
                if j >= RING:
                    used(act, j - RING, i)
                w = PLAN[j][4] if j < len(PLAN) else D
                f(w_hi[:, s, 0:w], w_raw[:, s, 0:w], ACT.Copy).then_inc(sem(f"hi{s}"), 1)

            done = [0]

            def split_to(j):
                while done[0] < min(j, len(PLAN)):
                    split(done[0])
                    done[0] += 1

            def norm(n, name):
                for t in range(NT):
                    for h in range(2):
                        act.wait_ge(sem(name), upto(name, 2 * t + h + 1))
                        c = slice(h * 512, (h + 1) * 512)
                        f(junk[:, t, c], X[:, t, c], ACT.Square, scale=D ** -0.5,
                          accum_out=ss[:, t, h:h + 1]).then_inc(sem("ss"), 1)

            norms = [0]

            def norm_T(n, ahead=None):
                norms[0] += 1
                act.wait_ge(sem("rstd"), NT * (norms[0] + (n >= 2)))
                f(XN[:, 1, :], X[:, 1, :], ACT.Copy, scale=rstd[:, 1:2]).then_inc(sem("xn1"), 1)
                if ahead:
                    split_to(ahead)
                for k in range(KD):
                    if k % 2 == 0:
                        act.wait_ge(sem("xnT"), 4 * n + k // 2 + 1)
                    f(hT_hi[:, k, :], norm_banks[k // 2][:, (k % 2) * SEQ:(k % 2 + 1) * SEQ],
                      ACT.Copy, scale=cols[:, 8 * n + k:8 * n + k + 1]).then_inc(sem("hT_hi"), 1)

            def evacuate(g, dst, func, ev):
                for t in range(NT):
                    for n in range(2):
                        acc_full(act, g, 2 * t + n)
                        o = dst(t, n)
                        f(o, acc[2 * t + n][:, 0:o.shape[1]], func).then_inc(sem(ev), 1)

            halves = lambda m: lambda t, n: m[:, t, n * 512:(n + 1) * 512]

            def stream_hi(name, fills=range(4)):
                for b in fills:
                    act.wait_ge(sem(name + "_T"), upto(name + "_T", b + 1))
                    f(hT_hi[:, 2 * b:2 * b + 2, :].rearrange("p k s -> p (k s)"), mb[b % 2][:, :],
                      ACT.Copy).then_inc(sem(name + "_H"), 1)

            act.wait_ge(sem("eps"), 1)
            nc.scalar.dma_start(X[:, 1, :], x_dram[:, 1, :]).then_inc(sem("x1_in"), 16)
            for t in range(NT):
                act.wait_ge(sem("x1_in" if t else "x0_in"), 16)
                for h in range(2):
                    c = slice(h * 512, (h + 1) * 512)
                    f(junk[:, t, c], X[:, t, c], ACT.Square, scale=D ** -0.5,
                      accum_out=ss[:, t, h:h + 1]).then_inc(sem("ss"), 1)
            act.wait_ge(sem("cols_in"), 16)
            norm_T(0, ahead=2)
            split_to(FIRST["vc"] + 3)
            act.wait_ge(sem("angles"), upto("angles", 1))
            f(ang[:, :, :, :], ang[:, :, :, :], ACT.Sin).then_inc(sem("trig"), 1)
            split_to(FIRST["ga"] + 4)
            act.wait_ge(sem("ev_vc"), upto("ev_vc", 4))
            for t in range(NT):
                then(f(junk[:, 0, 0:Q_LORA], VC[:, t, 512:512 + Q_LORA], ACT.Square,
                       accum_out=stat[:, t:t + 1]), "css")
                then(f(junk[:, 0, 0:KV_LORA], VC[:, t, 768:768 + KV_LORA], ACT.Square,
                       accum_out=stat[:, 2 + t:3 + t]), "css")
            f(stat[:, 4:6], stat[:, 0:2], ACT.Sqrt, bias=epsc[:, 0:1], scale=1.0 / Q_LORA).then_inc(
                sem("crms"), 1)
            f(stat[:, 6:8], stat[:, 2:4], ACT.Sqrt, bias=epsc[:, 0:1], scale=1.0 / KV_LORA).then_inc(
                sem("crms"), 1)
            split_to(FIRST["gb"] + 4)
            evacuate("ga", halves(GA), ACT.Sigmoid, "ev_ga")
            split_to(FIRST["qup"] + 4)
            evacuate("gb", halves(GB), ACT.Sigmoid, "ev_gb")
            split_to(FIRST["br_a"] + 4)

            for b in range(4):
                act.wait_ge(sem("qa_T"), upto("qa_T", b + 1))
                f(QTA[:, 2 * b:2 * b + 2, :].rearrange("p a s -> p (a s)"), mb[b % 2][:, :],
                  ACT.Copy).then_inc(sem("qa_E"), 1)
            for b in range(1, 8, 2):
                act.wait_ge(sem("qb_T"), upto("qb_T", b + 1))
                f(QTB[0:B_DK, 2 * b:2 * b + 2, :].rearrange("p a s -> p (a s)"), mb[1][0:B_DK, :],
                  ACT.Copy).then_inc(sem("qb_A"), 1)

            def copy_probs(u, dst, full, free, n, signal):
                act.wait_ge(sem(full), upto(full, n + 1))
                if n >= 2:
                    act.wait_ge(sem(free), upto(free, n - 1))
                f(dst[:, n % 2, :], mb[n % 2][:, 0:3 * P], ACT.Copy).then_inc(sem(signal), 1)

            for u in range(A_H + B_H):
                scale = (A_DH if u < A_H else B_DK) ** -0.5
                act.wait_ge(sem("masked"), u + 1)
                if u >= 2:
                    act.wait_ge(sem("pT"), upto("pT", u - 1))
                f(Pr[:, u % 2, 0:P], Sm[:, u % 2, 0:P], ACT.Exp, bias=mx[:, u, 0:1], scale=scale,
                  accum_out=sums[:, u, 0:1]).then_inc(sem("exp0"), 1)
                f(Pr[:, u % 2, P:3 * P], Sm[:, u % 2, P:3 * P], ACT.Exp, bias=mx[:, u, 1:2],
                  scale=scale, accum_out=sums[:, u, 1:2]).then_inc(sem("exp"), 1)
                if u:
                    copy_probs(u, PT, "pT", "pv", u - 1, "pT_E")
            copy_probs(0, PT, "pT", "pv", A_H + B_H - 1, "pT_E")
            stream_hi("y")
            split_to(FIRST["br_b"] + 4)
            split_to(FIRST["wout"] + 4)
            stream_hi("m")
            split_to(FIRST["query"] + 3)
            norm(1, "ev_wout")
            norm_T(1)

            for n in range(16):
                split_to(FIRST["query"] + n + 4)
                used(act, FIRST["query"] + n)
                f(QPT[:, n, :], col[n % 2][:, 0:SEQ], ACT.Copy).then_inc(sem("qp"), 1)
            for b in range(8):
                act.wait_ge(sem("scT"), b + 1)
                f(SC[:, b // 4, 4 * (b % 4):4 * (b % 4) + 4, :].rearrange("p a n -> p (a n)"),
                  mb[b % 2][:, :], ACT.Copy).then_inc(sem("sc"), 1)

            def gates_of(q):
                return mb[q % 2][:, :].rearrange("p (t a c) -> p t a c", t=4, a=2)

            def gate_rest(n, q):
                act.wait_ge(sem("gate"), n + 1)
                if not (isinstance(n, int) and n == 0):
                    act.wait_ge(sem("gated"), n)
                f(g4[:, :, :], gates_of(q)[:, :, 1, :], ACT.Copy).then_inc(sem("gate_rest"), 1)

            def u_round(r, gates_from=None):
                for q in range(4):
                    split(U0 + q + AHEAD, r)
                    used(act, U0 + q, r)
                    f(act_e[:, r * 4 + q, :], col[q % 2][:, 0:SEQ], ACT.Gelu).then_inc(
                        sem("gelu"), 1)
                    if gates_from is not None:
                        gate_rest(r * 4 + q - gates_from, q)

            assert done[0] == U0 + AHEAD
            with act.Fori(0, HALF // 4 - 2) as r:
                u_round(r)
            act.wait_ge(sem("best"), upto("best", 1))
            f(tk_bv[:, :, :, :], tk_bv[:, :, :, :], ACT.Exp).then_inc(sem("best_exp"), 1)
            with act.Fori(HALF // 4 - 2, HALF // 4) as r:
                u_round(r)
            act.wait_ge(sem("x_spilled"), 16)
            act.wait_ge(sem("pk_E"), upto("pk_E", 2))
            u_round(HALF // 4, HALF)
            with act.Fori(HALF // 4 + 1, NKEYS // 4) as r:
                u_round(r, HALF)

            def gated_hi(r, q):
                c = 4 * r + q % 4 if q < 4 else 4 * (r + 1) + q % 4
                q, n = q % 4, r if q < 4 else r + 1
                if not (isinstance(c, int) and c < 4):
                    used(act, V0 + q, n - 1)
                f(W_hi[:, q, :], act_e[:, c, :], ACT.Copy).then_inc(sem("W_hi"), 1)

            def v_round(r, count=4, rests=False):
                for q in range(4):
                    split(V0 + q + AHEAD, r)
                    if q < count:
                        gated_hi(r, q + 2)
                    if rests:
                        gate_rest(r * 4 + q + HALF, q)

            act.wait_ge(sem("gated"), HALF)
            used(act, V0 - 1)
            gated_hi(0, 0)
            gated_hi(0, 1)
            v_round(0, rests=True)
            with act.Fori(1, HALF // 4 - 1) as r:
                v_round(r, rests=True)
            v_round(HALF // 4 - 1, count=2, rests=True)
            act.wait_ge(sem("gated"), NKEYS)
            gated_hi(HALF // 4, 0)
            gated_hi(HALF // 4, 1)
            with act.Fori(HALF // 4, NKEYS // 4 - 1) as r:
                v_round(r)
            v_round(NKEYS // 4 - 1, count=2)
            done[0] = FIRST["qkv_e"] + AHEAD

            norm(2, "ev_v")
            norm(3, "x_final")
            norm_T(2)
            for n in range(12):
                split_to(FIRST["qkv_e"] + n + 4)
                act.wait_ge(sem("conv"), n + 1)
                f(QKVF[:, n, :], QKVF[:, n, :], ACT.Silu).then_inc(sem("silu"), 1)
            split_to(FIRST["uv"] + 4)
            for t in range(NT):
                acc_full(act, "zba", 2 * t)
                f(Z[:, t, :], acc[2 * t][:, :], ACT.Silu).then_inc(sem("ev_zba"), 1)
                acc_full(act, "zba", 2 * t + 1)
                f(stat[:, 8 * t:8 * t + 8], acc[2 * t + 1][:, 0:8], ACT.Copy).then_inc(
                    sem("ev_zba"), 1)

            act.wait_ge(sem("rows_in"), 16)
            act.wait_ge(sem("ev_zba"), upto("ev_zba", 4))
            ba = stat[:, 0:16].rearrange("p (t n) -> p t n", t=NT)
            f(stat[:, 32:40].rearrange("p (t n) -> p t n", t=NT), ba[:, :, 0:4], ACT.Sigmoid).then_inc(
                sem("beta"), 1)
            f(stat[:, 60:64], rows[:, R_ALOG:R_ALOG + 4], ACT.Exp).then_inc(sem("beta"), 1)
            act.wait_ge(sem("sp"), upto("sp", 1))
            f(stat[:, 48:56], stat[:, 48:56], ACT.Exp).then_inc(sem("sp_exp"), 1)
            act.wait_ge(sem("sp"), upto("sp", 2))
            f(stat[:, 16:24], stat[:, 24:32], ACT.Ln).then_inc(sem("sp_ln"), 1)
            split_to(FIRST["uv"] + 6)
            act.wait_ge(sem("tok_E"), upto("tok_E", 4))
            for m, (src, squares) in enumerate(((Qt, D0), (Kt, N2))):
                for t in range(NT):
                    for h in range(G_H):
                        i = 8 * m + 4 * t + h
                        x = f(squares[:, t, h, :], src[:, t, h, :], ACT.Square,
                              accum_out=sq16[:, i:i + 1])
            x.then_inc(sem("l2_ss"), 1)
            split_to(FIRST["uv"] + 8)
            for t in range(NT):
                acc_full(act, "uv", 2 * t)
                f(UV[:, t, 0:512], acc[2 * t][:, :], ACT.Gelu_apprx_tanh).then_inc(sem("ev_uv"), 1)
                acc_full(act, "uv", 2 * t + 1)
                for g in range(M_G):
                    x = f(UV[:, t, 512 + g * P:512 + (g + 1) * P],
                          acc[2 * t + 1][:, g * P:(g + 1) * P], ACT.Gelu_apprx_tanh,
                          accum_out=gsum[:, 4 * t + g:4 * t + g + 1])
                x.then_inc(sem("ev_uv"), 1)
            act.wait_ge(sem("gc"), 2)
            f(egc[:, :], gc[:, :], ACT.Exp).then_inc(sem("egc"), 1)
            act.wait_ge(sem("v_mean"), upto("v_mean", 1))
            for t in range(NT):
                for g in range(M_G):
                    x = f(N2T[:, t, g, :], UV[:, t, 512 + g * P:512 + (g + 1) * P], ACT.Square,
                          bias=gsum[:, 4 * t + g:4 * t + g + 1],
                          accum_out=gvar[:, 4 * t + g:4 * t + g + 1])
            x.then_inc(sem("v_ss"), 1)
            for t in range(NT):
                act.wait_ge(sem("gdiff"), 2 * t + 1)
                f(decA[:, t, :, :], decA[:, t, :, :], ACT.Exp, scale=-1.0).then_inc(sem("dec"), 1)
                act.wait_ge(sem("gdiff"), 2 * t + 2)
                f(decAT[:, t, :, :], decAT[:, t, :, :], ACT.Exp).then_inc(sem("dec"), 1)
                act.wait_ge(sem("glast"), t + 1)
                f(gl[:, 8 * t:8 * t + 8], gl[:, 8 * t:8 * t + 8], ACT.Exp).then_inc(sem("gl"), 1)
            act.wait_ge(sem("egc"), upto("egc", 1))

            def times_egc(dst, src, ready, name):
                act.wait_ge(sem(ready), upto(ready, 1))
                for t in range(NT):
                    for h in range(G_H):
                        x = f(dst[:, t, h, :], src[:, t, h, :], ACT.Copy,
                              scale=egc[:, 4 * t + h:4 * t + h + 1])
                x.then_inc(sem(name), 1)

            times_egc(QDt, Qt, "q_map", "qd")
            for n in range(1, 8, 2):
                act.wait_ge(sem("fT_T"), upto("fT_T", n + 1))
                f(fT[:, n % 4, n // 4, :, :].rearrange("p h d -> p (h d)"), mb[1][:, :],
                  ACT.Copy).then_inc(sem("fT_A"), 1)
            times_egc(KBE, KBt, "kb_map", "kbe")

            plain = {"N2": N2, "N2T": N2T, "N4": N4, "N4T": N4T, "N8": N8, "P1": P1, "P2": P2,
                     "u": Ut, "wT": wT}
            for s, (result, _, _, _) in enumerate(SOLVE):
                if s == GMLP_T_AT:
                    stream_hi("oc", range(2))
                if result == "u":
                    split_to(FIRST["out_e"] + 4)
                for t in range(NT):
                    if result in PLAIN:
                        n = NT * s + t
                        act.wait_ge(sem("sv"), n + 1)
                        f(plain[result][:, t, :, :].rearrange("p h f -> p (h f)"),
                          (acc + col)[n % 6][:, :], ACT.Copy).then_inc(sem("sv_A"), 1)
            for t in range(NT):
                split_to(FIRST["out_e"] + (6 if t == 0 else KD))
                act.wait_ge(sem("o_E"), 2 * t + 2)
                for h in range(G_H):
                    x = f(decA[:, t, h, :], Ot[:, t, h, :], ACT.Square, scale=G_DK ** -0.5,
                          accum_out=stat[:, 4 * t + h:4 * t + h + 1])
                x.then_inc(sem("o_ss"), 1)
            stream_hi("oc", range(2, 4))

            def mlp(layer):
                j0 = FIRST[f"mlp{layer}"]
                f0 = layer * D_FF // P

                def relu2(blk, j, i, s):
                    used(act, j, i)
                    if layer or not (isinstance(blk, int) and blk < 2):
                        act.wait_ge(sem("H"), blk - 1 + f0)
                    f(H_r[:, s, :], col[s][:, 0:SEQ], ACT.Relu).then_inc(sem("relu"), 1)
                    act.wait_ge(sem("relu"), blk + 1 + f0)
                    f(H_q[:, s, :], H_r[:, s, :], ACT.Square).then_inc(sem("square"), 1)

                split_to(j0 + 4)
                relu2(0, j0, 0, 0)
                split_to(j0 + 5)
                relu2(1, j0 + 1, 0, 1)
                split_to(j0 + MLP_SKIP + AHEAD)
                j = j0 + MLP_SKIP
                with act.Fori(0, MLP_ROUNDS) as r:
                    for q in range(4):
                        split(j + q + AHEAD, r)
                        if q % 2 == 0:
                            relu2(2 * r + 2 + q // 2, j + q, r, (q // 2) % 2)
                done[0] = j + 4 * MLP_ROUNDS + AHEAD

            def gated_projection(layer, n):
                split_to(FIRST[f"ple{layer}"] + 3)
                norm(n, f"ev_mlp{layer}")
                norm_T(n - 1, ahead=FIRST[f"gate{layer}"] + 3)
                split_to(FIRST[f"gate{layer}"] + KD + 3)
                evacuate(f"gate{layer}", halves(GT), ACT.Sigmoid, f"ev_gate{layer}")

            split_to(FIRST["mlp0"] + 3)
            norm(4, "ev_out_e")
            norm_T(3)
            mlp(0)
            gated_projection(0, 5)
            split_to(FIRST["q1"] + 3)
            norm(6, "x_ple0")
            norm_T(5)
            for m, nxt in enumerate(("k1", "v1")):
                split_to(FIRST[nxt] + 4)
                if m == 0:
                    act.wait_ge(sem("lam_dots"), upto("lam_dots", 2))
                    f(stat[:, 2:4], stat[:, 0:2], ACT.Exp).then_inc(sem("lam_exp"), 1)
                act.wait_ge(sem("qk_ss"), m + 1)
                f(sq32[:, :], sq32[:, :], ACT.Sqrt, bias=epsc[:, 0:1], scale=1.0 / C_DH).then_inc(
                    sem("qk_root"), 1)
            split_to(FIRST["out_o"] + 4)
            def squares1(part):
                act.wait_ge(sem("pv1"), 4 * part + 4)
                for t in range(NT):
                    for h in range(4):
                        i = 8 * part + 4 * t + h
                        x = f(SQ[:, t, (4 * part + h) * P:(4 * part + h + 1) * P],
                              acc[2 * t + part][:, h * P:(h + 1) * P], ACT.Square, scale=P ** -0.5,
                              accum_out=sq16[:, i:i + 1])
                    x.then_inc(sem("o1_ss"), 1)

            for w in range(2 * C_H):
                act.wait_ge(sem("masked1"), w + 1)
                if w >= 4:
                    act.wait_ge(sem("aT"), upto("aT", (w - 4) // 2 + 1))
                f(PR1[:, w % 4, 0:P], S1[:, w % 2, 0:P], ACT.Exp, bias=mx1[:, w, 0:1],
                  accum_out=sum1[:, w, 0:1]).then_inc(sem("exp1a"), 1)
                f(PR1[:, w % 4, P:3 * P], S1[:, w % 2, P:3 * P], ACT.Exp, bias=mx1[:, w, 1:2],
                  accum_out=sum1[:, w, 1:2]).then_inc(sem("exp1"), 1)
                if w % 2 and w > 1:
                    copy_probs(0, PT1, "aT", "pv1", w // 2 - 1, "aT_E")
                if w == 2 * (C_H // 2 + 1) + 1:
                    squares1(0)
            copy_probs(0, PT1, "aT", "pv1", C_H - 1, "aT_E")
            squares1(1)
            stream_hi("o1")
            split_to(FIRST["mlp1"] + 3)
            norm(7, "ev_out_o")
            norm_T(6)
            mlp(1)
            gated_projection(1, 8)
            split_to(len(PLAN))

        @block.gpsimd
        def _(pool):
            g = nc.gpsimd
            counts = {}

            def then(ins, name):
                counts[name] = counts.get(name, 0) + 1
                ins.then_inc(sem(name), 1)
                pool.wait_ge(sem(name), upto(name, counts[name]))

            g.memset(epsc[:, :], EPS).then_inc(sem("eps"), 1)
            then(g.memset(ident[:, :], 0.0), "ident")
            then(g.affine_select(out=ident[:, :], in_=ident[:, :], compare_op=ALU.not_equal,
                                 fill=1.0, base=0, pattern=[[-1, P]], channel_multiplier=1), "ident")

            def causal_mask(m):
                then(g.memset(m[:, :], 0.0), "causal")
                for c in (0, 2):
                    d = m[:, c * P:(c + 1) * P]
                    then(g.affine_select(out=d, in_=d, compare_op=ALU.is_ge, fill=NEG, base=0,
                                         pattern=[[-1, P]], channel_multiplier=1), "causal")

            causal_mask(causal)
            g.iota(iota_row[:, :], [[1, P]], base=0, channel_multiplier=0,
                   allow_small_or_imprecise_dtypes=True).then_inc(sem("iota"), 1)

            def rest(j, i=0):
                s = j % RING
                pool.wait_ge(sem(f"hi{s}"), upto(f"hi{s}", j // RING + 1 + i))
                if j >= RING:
                    used(pool, j - RING, i)
                w = PLAN[j][4]
                g.tensor_tensor(w_lo[:, s, 0:w], w_raw[:, s, 0:w], w_hi[:, s, 0:w].bitcast(F32),
                                ALU.subtract).then_inc(sem(f"lo{s}"), 1)

            def block_masks():
                pool.wait_ge(sem("gate"), NKEYS)
                pool.wait_ge(sem("hot"), NKEYS)

                causal_mask(causal1)
                for c, base in ((0, 0), (1, P), (2, 0)):
                    g.iota(dist[:, c * P:(c + 1) * P], [[-1, P]], base=base, channel_multiplier=1,
                           allow_small_or_imprecise_dtypes=True).then_inc(sem("iota"), 1)
                then(g.memset(ones[:, :], 1.0), "ones")

                def within(m, size):
                    v = masks[:, m, :].rearrange("p (b f) -> p b f", f=size)
                    then(g.memset(masks[:, m, :], 1.0), "masks")
                    then(g.affine_select(out=v, in_=v, compare_op=ALU.is_ge, fill=0.0, base=0,
                                         pattern=[[-size, P // size], [0, size]],
                                         channel_multiplier=1), "masks")
                    then(g.affine_select(out=v, in_=v, compare_op=ALU.is_ge, fill=0.0,
                                         base=size - 1, pattern=[[size, P // size], [0, size]],
                                         channel_multiplier=-1), "masks")

                def triangle(m, base, step, mult):
                    v = masks[:, m, :]
                    then(g.affine_select(out=v, in_=v, compare_op=ALU.is_ge, fill=0.0, base=base,
                                         pattern=[[step, P]], channel_multiplier=mult), "masks")

                for m, size in ((0, 16), (1, 64), (2, 64), (3, 16), (5, 32)):
                    within(m, size)
                triangle(0, -1, -1, 1)
                triangle(1, -1, 1, -1)
                triangle(2, 0, 1, -1)
                then(g.tensor_tensor(masks[:, 4, :], masks[:, 5, :], masks[:, 3, :], ALU.subtract),
                     "masks")
                then(g.tensor_tensor(masks[:, 5, :], ones[:, :], masks[:, 5, :], ALU.subtract),
                     "masks")
                pool.wait_ge(sem("wst_in"), 16)
                g.affine_select(out=WST[:, :, :], in_=WST[:, :, :], compare_op=ALU.is_ge, fill=0.0,
                                base=0, pattern=[[0, M_G], [1, P]], channel_multiplier=-1).then_inc(
                    sem("wst"), 1)

            then(g.memset(minus_half[:, :], -0.5), "half")
            norms = [0]

            def row_rstd():
                for t in range(NT):
                    r = slice(t, t + 1)
                    pool.wait_ge(sem("ss"), 4 * norms[0] + 2 * t + 2)
                    then(g.tensor_tensor(ms[:, r], ss[:, t, 0:1], ss[:, t, 1:2], ALU.add), "ms")
                    then(g.tensor_scalar(ms[:, r], ms[:, r], EPS, None, ALU.add), "ms")
                    g.tensor_tensor(rstd[:, r], ms[:, r], minus_half[:, r], ALU.pow).then_inc(
                        sem("rstd"), 1)
                norms[0] += 1

            row_rstd()
            def per_head(s):
                return s.unsqueeze(2).to_broadcast([P, 8, P])

            def heads(m):
                return m[:, :, :, :].rearrange("p t h d -> p (t h) d")

            def delta_and_gmlp_maps():
                pool.wait_ge(sem("ev_uv"), upto("ev_uv", 4))
                g.tensor_scalar(gsum[:, :], gsum[:, :], -1.0 / P, None, ALU.mult).then_inc(
                    sem("v_mean"), 1)
                pool.wait_ge(sem("tok_E"), upto("tok_E", 6))
                pool.wait_ge(sem("beta"), upto("beta", 1))
                g.tensor_tensor(heads(VBt), heads(Vt), per_head(stat[:, 32:40]),
                                ALU.mult).then_inc(sem("vb"), 1)
                pool.wait_ge(sem("v_ss"), upto("v_ss", 1))
                then(g.tensor_scalar(gvar[:, :], gvar[:, :], 1.0 / P, EPS, ALU.mult, ALU.add),
                     "pool")
                then(g.tensor_tensor(gvar[:, :], gvar[:, :], minus_half[:, 0:8], ALU.pow), "v_r")
                pool.wait_ge(sem("v_mean"), upto("v_mean", 1))
                for t in range(NT):
                    for m in range(M_G):
                        i = 4 * t + m
                        x = UV[:, t, 512 + m * P:512 + (m + 1) * P]
                        last = g.tensor_scalar(x, x, gsum[:, i:i + 1], gvar[:, i:i + 1], ALU.add,
                                               ALU.mult)
                then(last, "pool")
                pool.wait_ge(sem("rows_in"), 16)
                g.tensor_tensor(UV[:, :, 512:1024], UV[:, :, 512:1024],
                                rows[:, R_VG:R_VG + 512].unsqueeze(1).to_broadcast([P, NT, 512]),
                                ALU.mult).then_inc(sem("gv"), 1)
                pool.wait_ge(sem("kd_factor"), upto("kd_factor", 1))
                g.tensor_tensor(heads(KDt), heads(Kt), per_head(kdf[:, :]), ALU.mult).then_inc(
                    sem("kd"), 1)
                pool.wait_ge(sem("dec"), 4)
                g.tensor_tensor(heads(decQ), heads(decAT),
                                masks[:, 2, :].unsqueeze(1).to_broadcast([P, 8, P]),
                                ALU.mult).then_inc(sem("dec_q"), 1)
                pool.wait_ge(sem("ev_zba"), upto("ev_zba", 4))
                z = Z[:, :, :].rearrange("p t (h d) -> p (t h) d", d=P)
                g.tensor_tensor(z, z, rows[:, R_OG:R_OG + P].unsqueeze(1).to_broadcast([P, 8, P]),
                                ALU.mult).then_inc(sem("zg"), 1)

            norm_at = [FIRST[name] + 3 for name in ("query", "qkv_e", "mlp0", "ple0", "q1", "mlp1",
                                                    "ple1")]
            j = 0
            while j < len(PLAN):
                if j in norm_at:
                    row_rstd()
                    if j == FIRST["qkv_e"] + 3:
                        row_rstd()
                        block_masks()
                if j in LOOPS:
                    with pool.Fori(0, LOOPS[j]) as i:
                        for q in range(4):
                            rest(j + q, i)
                    j += 4 * LOOPS[j]
                    continue
                if j == FIRST["uv"] + 6:
                    pool.wait_ge(sem("l2_ss"), upto("l2_ss", 1))
                    then(g.tensor_scalar(sq16[:, :], sq16[:, :], EPS, None, ALU.add), "pool")
                    g.tensor_tensor(sq16[:, :], sq16[:, :], minus_half[:, :], ALU.pow).then_inc(
                        sem("l2_r"), 1)
                if j == FIRST["out_e"]:
                    delta_and_gmlp_maps()
                if j == FIRST["out_o"] + 4:
                    for n in range(2 * NT):
                        r = sq16[:, 4 * n:4 * n + 4]
                        pool.wait_ge(sem("o1_ss"), upto("o1_ss", n + 1))
                        then(g.tensor_scalar(r, r, EPS, None, ALU.add), "pool")
                        then(g.tensor_tensor(r, r, minus_half[:, 0:4], ALU.pow), "pool")
                        g.tensor_scalar(r, r, 1.0 - LAM_INIT, None, ALU.mult).then_inc(
                            sem("o1_r"), 1)
                if j in (FIRST["out_e"] + 6, FIRST["mlp0"]):
                    t = int(j == FIRST["mlp0"])
                    r = stat[:, 4 * t:4 * t + 4]
                    pool.wait_ge(sem("o_ss"), upto("o_ss", t + 1))
                    then(g.tensor_scalar(r, r, EPS, None, ALU.add), "pool")
                    g.tensor_tensor(r, r, minus_half[:, 0:4], ALU.pow).then_inc(sem("o_r"), 1)
                rest(j)
                j += 1

        @block.vector
        def _(dve):
            v = nc.vector
            counts = {}

            def then(ins, name="dve"):
                counts[name] = counts.get(name, 0) + 1
                ins.then_inc(sem(name), 1)
                dve.wait_ge(sem(name), upto(name, counts[name]))

            def go(ins, name="dve"):
                counts[name] = counts.get(name, 0) + 1
                ins.then_inc(sem(name), 1)

            def over(ap, shape, axis):
                return ap.unsqueeze(axis).to_broadcast(shape)

            def hi_lo(hi, lo, src, name):
                then(v.tensor_copy(hi, src))
                then(v.tensor_tensor(lo, src, hi.bitcast(F32), ALU.subtract), name)

            def hi_lo_gain(hi, lo, src, gain, name):
                then(v.tensor_scalar(hi, src, gain, None, ALU.mult))
                then(v.scalar_tensor_tensor(out=lo, in0=src, scalar=gain, in1=hi.bitcast(F32),
                                            op0=ALU.mult, op1=ALU.subtract), name)

            norms = [0]

            def row_rstd(t):
                dve.wait_ge(sem("rstd"), NT * norms[0] + t + 1)

            def norm_T(n, between=None):
                row_rstd(0)
                norms[0] += 1
                v.tensor_scalar(XN[:, 0, :], X[:, 0, :], rstd[:, 0:1], None, ALU.mult).then_inc(
                    sem("xn0"), 1)
                if between:
                    between()
                for k in range(KD):
                    if k % 2 == 0:
                        dve.wait_ge(sem("hT_hi"), KD * n + k + 2)
                    v.scalar_tensor_tensor(
                        out=hT_lo[:, k, :], in0=norm_banks[k // 2][:, (k % 2) * SEQ:(k % 2 + 1) * SEQ],
                        scalar=cols[:, 8 * n + k:8 * n + k + 1], in1=hT_hi[:, k, :].bitcast(F32),
                        op0=ALU.mult, op1=ALU.subtract).then_inc(sem("hT"), 1)

            def stream_T(name, fills=range(4)):
                for b in fills:
                    dve.wait_ge(sem(name + "_H"), upto(name + "_H", b + 1))
                    k = slice(2 * b, 2 * b + 2)
                    v.tensor_tensor(hT_lo[:, k, :].rearrange("p k s -> p (k s)"), mb[b % 2][:, :],
                                    hT_hi[:, k, :].bitcast(F32).rearrange("p k s -> p (k s)"),
                                    ALU.subtract).then_inc(sem(name + "_E"), 1)

            def banks(g):
                for t in range(NT):
                    for n in range(2):
                        acc_full(dve, g, 2 * t + n)
                        yield t, n, acc[2 * t + n]

            def evac(g, dst):
                for t, n, a in banks(g):
                    o = dst(t, n)
                    i = v.tensor_copy(o, a[:, 0:o.shape[1]])
                    (then if (t, n) == (1, 1) else go)(i, "ev_" + g)

            def half(m):
                return lambda t, n: m[:, t, n * 512:(n + 1) * 512]

            def residual(g, old=X):
                for t, n, a in banks(g):
                    c = slice(n * 512, (n + 1) * 512)
                    v.tensor_tensor(X[:, t, c], a[:, :], old[:, t, c], ALU.add).then_inc(
                        sem("ev_" + g), 1)

            def copies(name, fill_dst):
                for b, dst in enumerate(fill_dst):
                    dve.wait_ge(sem(name + "_T"), upto(name + "_T", b + 1))
                    then(v.tensor_copy(dst, mb[b % 2][0:dst.shape[0], 0:dst.shape[1]]), name + "_E")

            dve.wait_ge(sem("cols_in"), 16)
            norm_T(0)
            dve.wait_ge(sem("pos_in"), 16)
            dve.wait_ge(sem("freq_in"), 16)
            then(v.tensor_copy(pos_f[:, :], pos_i[:, :]))
            for t in range(NT):
                for ph in range(2):
                    then(v.tensor_scalar(ang[:, t, ph, :], rows_f[:, :], pos_f[:, t:t + 1], None,
                                         ALU.mult))
            for ph in range(2):
                then(v.tensor_scalar(ang_k[:, :, ph, :], ang[:, :, ph, :], 1 / (2 * math.pi),
                                     0.25 * ph, ALU.mult, ALU.add))
            then(v.tensor_scalar(ang_k[:, :, :, :], ang_k[:, :, :, :], ROUND, None, ALU.add))
            then(v.tensor_scalar(ang_k[:, :, :, :], ang_k[:, :, :, :], ROUND, None, ALU.subtract))
            a_flat = ang[:, :, :, :].rearrange("p t a f -> p (t a f)")
            k_flat = ang_k[:, :, :, :].rearrange("p t a f -> p (t a f)")
            for turn in TURN:
                then(v.scalar_tensor_tensor(out=a_flat, in0=k_flat, scalar=-turn, in1=a_flat,
                                            op0=ALU.mult, op1=ALU.add))
            then(v.tensor_scalar(ang[:, :, 1, :], ang[:, :, 1, :], math.pi / 2, None, ALU.add))
            then(v.tensor_scalar(a_flat, a_flat, 3.1415925, -3.1415925, ALU.min, ALU.max), "angles")

            evac("qk", lambda t, n: QK[:, t, 8 * n:8 * n + 8, :].rearrange("p h d -> p (h d)"))
            evac("vc", lambda t, n: VC[:, t, 512 * n:(512, VC_W)[n]])
            dve.wait_ge(sem("crms"), upto("crms", 2))
            then(v.reciprocal(stat[:, 8:12], stat[:, 4:8]))
            for t in range(NT):
                for m, (a, b) in enumerate(((0, Q_LORA), (Q_LORA, Q_LORA + KV_LORA))):
                    i = v.tensor_scalar(CN[:, t, a:b], VC[:, t, 512 + a:512 + b],
                                        stat[:, 8 + 2 * m + t:9 + 2 * m + t], None, ALU.mult)
                    then(i, "cn" if (t, m) == (1, 1) else "dve")

            def rotate(dst1, dst2, x1, x2, shape, axis, f0, f1, tmp, name):
                cos, sin = (ang[:, :, ph, f0:f1] if axis is None else
                            over(ang[:, :, ph, f0:f1], shape, axis) for ph in (1, 0))
                for o, x, y in ((tmp[0], x1, cos), (tmp[1], x2, sin), (tmp[2], x2, cos),
                                (tmp[3], x1, sin)):
                    then(v.tensor_tensor(o, x, y, ALU.mult))
                then(v.tensor_tensor(dst1, tmp[0], tmp[1], ALU.subtract))
                then(v.tensor_tensor(dst2, tmp[2], tmp[3], ALU.add), name)

            dve.wait_ge(sem("trig"), upto("trig", 1))
            rotate(QR[:, :, :, 0:32], QR[:, :, :, 32:64], QK[:, :, :, 0:32], QK[:, :, :, 32:64],
                   [P, NT, 16, 32], 2, 0, 32,
                   [QR[:, :, :, 0:32], rope_t[:, :, :, :], QR[:, :, :, 32:64],
                    rope_u[:, :, :, :]], "rope_a")
            for k in range(3):
                dve.wait_ge(sem("c_T"), upto("c_T", k // 2 + 1))
                hi_lo_gain(cT_hi[:, k, :], cT_lo[:, k, :],
                           mb[k // 2][:, (k % 2) * SEQ:(k % 2 + 1) * SEQ],
                           cols[:, C_QN + k:C_QN + k + 1], "cT")
            evac("qup", lambda t, n: QB[:, t, 4 * n:4 * n + 4, :].rearrange("p h d -> p (h d)"))
            for t, n, a in banks("kvup"):
                kv = a[:, :].rearrange("p (h d) -> p h d", h=4)
                then(v.tensor_copy(KF[:, t, 4 * n:4 * n + 4, 0:B_NOPE], kv[:, :, 0:B_NOPE]))
                then(v.tensor_copy(VB[:, t, 4 * n:4 * n + 4, :], kv[:, :, B_NOPE:]), "ev_kvup")
            tmp = [rope_t[:, :, 8 * a:8 * a + 8, 16 * b:16 * b + 16] for a in range(2)
                   for b in range(2)]
            rotate(QB[:, :, :, 64:80], QB[:, :, :, 80:96], QB[:, :, :, 64:80], QB[:, :, :, 80:96],
                   [P, NT, 8, 16], 2, 32, 48, tmp, "rope_q")
            tmp = [rope_t[:, :, a, 0:16] for a in range(6)]
            rotate(tmp[4], tmp[5], VC[:, :, 896:912], VC[:, :, 912:928], None, None, 32, 48,
                   tmp[:4], "rope_k")
            for n in range(2):
                then(v.tensor_copy(KF[:, :, :, 64 + 16 * n:80 + 16 * n],
                                   over(tmp[4 + n], [P, NT, 8, 16], 2)), "rope_b")
            for b in range(0, 8, 2):
                dve.wait_ge(sem("qb_T"), upto("qb_T", b + 1))
                then(v.tensor_copy(QTB[0:B_DK, 2 * b:2 * b + 2, :].rearrange("p a s -> p (a s)"),
                                   mb[0][0:B_DK, :]), "qb_E")

            def masked(dst, src, mask, top, scale, name):
                for t, (a, b) in enumerate(((0, P), (P, 3 * P))):
                    i = v.tensor_tensor_reduce(dst[:, a:b], src[:, a:b], mask[:, a:b], 1.0, LOWEST,
                                               ALU.add, ALU.max, top[:, t:t + 1])
                    if t == 0:
                        go(i)
                then(i)
                then(v.tensor_scalar(top, top, -scale, None, ALU.mult), name)

            def branch_out(br):
                dve.wait_ge(sem("exp"), 8 * br + 8)
                then(v.reciprocal(sums[:, 8 * br:8 * br + 8, :], sums[:, 8 * br:8 * br + 8, :]))
                dve.wait_ge(sem("pv"), 8 * br + 8)
                for t in range(NT):
                    then(v.tensor_tensor(Y[:, br, t, :, :],
                                         acc[2 * br + t][:, :].rearrange("p (h d) -> p h d", h=8),
                                         over(sums[:, 8 * br:8 * br + 8, t], [P, 8, 64], 2),
                                         ALU.mult), "y")

            dve.wait_ge(sem("causal"), 3)
            for u in range(A_H + B_H):
                dve.wait_ge(sem("scores"), u + 1)
                if u >= 2:
                    dve.wait_ge(sem("exp"), u - 1)
                masked(Sm[:, u % 2, :], col[u % 2], causal, mx[:, u, :],
                       (A_DH if u < A_H else B_DK) ** -0.5, "masked")
                if u == A_H + 3:
                    branch_out(0)
            branch_out(1)
            stream_T("y")
            for t, n, a in banks("br_a"):
                c = slice(n * 512, (n + 1) * 512)
                then(v.tensor_tensor(M[:, t, c], a[:, :], GA[:, t, c], ALU.mult), "ev_br_a")
            for t, n, a in banks("br_b"):
                c = slice(n * 512, (n + 1) * 512)
                v.tensor_tensor(M2[:, t, c], a[:, :], GB[:, t, c], ALU.mult).then_inc(
                    sem("ev_br_b"), 1)
                dve.wait_ge(sem("ev_br_b"), upto("ev_br_b", 2 * t + n + 1))
                go(v.tensor_tensor(M[:, t, c], M[:, t, c], M2[:, t, c], ALU.add), "merged")
            stream_T("m")
            residual("wout")
            norm_T(1)

            def top16(values, index, scores, rest):
                then(v.max(values[:, 0:8], scores))
                then(v.max_index(index[:, 0:8], values[:, 0:8], scores))
                then(v.match_replace(rest, values[:, 0:8], scores, LOWEST))
                then(v.max(values[:, 8:16], rest))
                then(v.max_index(index[:, 8:16], values[:, 8:16], rest))

            for t in range(NT):
                for n in range(16):
                    if n % 4 == 0:
                        dve.wait_ge(sem("sc"), 4 * t + n // 4 + 1)
                    top16(tk_v[:, t, n, :], tk_i[:, t, n, :], SC[:, t, n, :], tk_s2[:, 0:NKEYS])
            then(v.tensor_copy(tk_if[:, :, :, :], tk_i[:, :, :, :]))
            for t in range(NT):
                for h in range(PE_H):
                    then(v.tensor_tensor(tk_c[:, :].rearrange("p (a b) -> p a b", a=TOPK),
                                         over(tk_v[:, t, 2 * h, :], [P, TOPK, TOPK], 2),
                                         over(tk_v[:, t, 2 * h + 1, :], [P, TOPK, TOPK], 1),
                                         ALU.add))
                    top16(tk_bv[:, t, h, :], tk_bp[:, t, h, :], tk_c[:, :], tk_s2[:, :])
            then(v.tensor_scalar(tk_pa[:, 0], tk_bp[:, :, :, :], 4, None, ALU.logical_shift_right))
            then(v.tensor_scalar(tk_pa[:, 1], tk_bp[:, :, :, :], 15, None, ALU.bitwise_and))
            then(v.tensor_copy(tk_pf[:, :, :, :, :].rearrange("p m t h k -> p (m t h k)"),
                               tk_pa[:, :, :, :, :].rearrange("p m t h k -> p (m t h k)")))
            dve.wait_ge(sem("iota"), 1)
            for m in range(2):
                for t in range(NT):
                    ix = tk_if[:, t, :, :].rearrange("p (h m) a -> p m h a", m=2)[:, m]
                    e = tk_e[:, :, :, :].rearrange("p h k a -> p (h k) a")
                    then(v.tensor_tensor(
                        e, over(tk_pf[:, m, t, :, :].rearrange("p h k -> p (h k)"),
                                [P, PE_H * TOPK, TOPK], 2),
                        over(iota_row[:, 0:TOPK], [P, PE_H * TOPK, TOPK], 1), ALU.is_equal))
                    then(v.tensor_tensor(tk_e[:, :, :, :], tk_e[:, :, :, :],
                                         over(ix, [P, PE_H, TOPK, TOPK], 2), ALU.mult))
                    then(v.tensor_reduce(tk_sel[:, m, t, :, :].rearrange("p h k -> p (h k)"), e,
                                         AX_X, ALU.add))
            bv = tk_bv[:, :, :, :].rearrange("p t h k -> p (t h) k")
            then(v.tensor_copy(stat[:, 0:16], bv[:, :, 0]))
            then(v.tensor_tensor(bv, bv, over(stat[:, 0:16], [P, 16, TOPK], 2), ALU.subtract),
                 "best")
            dve.wait_ge(sem("best_exp"), upto("best_exp", 1))
            then(v.tensor_reduce(stat[:, 16:32], bv, AX_X, ALU.add))
            then(v.reciprocal(stat[:, 16:32], stat[:, 16:32]))
            then(v.tensor_tensor(bv, bv, over(stat[:, 16:32], [P, 16, TOPK], 2), ALU.mult), "picks")
            dve.wait_ge(sem("pk_T"), upto("pk_T", 1))
            hi_lo(g_parts[:, 0, :], g_parts[:, 1, :], mb[0][:, 0:SEQ], "dve")
            then(v.tensor_copy(i1T[:, :], mb[0][:, SEQ:2 * SEQ]), "pk_E")
            dve.wait_ge(sem("pk_T"), upto("pk_T", 2))
            then(v.tensor_copy(i2T[:, :], mb[1][:, 0:SEQ]), "pk_E")

            def hot(n, n_half, q, part):
                if not (isinstance(n, int) and n < 2):
                    dve.wait_ge(sem("gate"), n - 1)
                tok = bass.ds(n_half * 4, 4)
                v.tensor_tensor(hot2[:, q % 2, :, :], over(iota_row[:, :], [P, 4, NKEYS], 1),
                                over(i2T[:, tok], [P, 4, NKEYS], 2), ALU.is_equal).then_inc(
                    sem("hot2"), 1)
                if not (isinstance(n, int) and n == 0):
                    dve.wait_ge(sem("hot"), n)
                v.tensor_tensor(is1[:, :, :], over(iota_row[:, part * HALF:(part + 1) * HALF],
                                                   [P, 4, HALF], 1),
                                over(i1T[:, tok], [P, 4, HALF], 2), ALU.is_equal).then_inc(
                    sem("hot1"), 1)
                dve.wait_ge(sem("hot1"), n + 1)
                v.tensor_tensor(
                    hot1[:, q % 2, :, :, :], is1[:, :, :].unsqueeze(2).to_broadcast([P, 4, 2, HALF]),
                    g_parts[:, :, tok].bitcast(F32).rearrange("p a t -> p t a").unsqueeze(3)
                    .to_broadcast([P, 4, 2, HALF]), ALU.mult).then_inc(sem("hot"), 1)

            def apply_gates(n, n_half, q, part):
                dve.wait_ge(sem("gate_rest"), n + 1)
                v.tensor_tensor(g4[:, :, :], mb[q % 2][:, :].rearrange(
                    "p (t a c) -> p t a c", t=4, a=2)[:, :, 0, :], g4[:, :, :], ALU.add).then_inc(
                    sem("gate_sum"), 1)
                dve.wait_ge(sem("gate_sum"), n + 1)
                e = act_e[:, part * HALF:(part + 1) * HALF, bass.ds(n_half * 4, 4)]
                v.tensor_tensor(e, g4[:, :, :].rearrange("p t c -> p c t"), e,
                                ALU.mult).then_inc(sem("gated"), 1)

            def gated_lo(c, q):
                dve.wait_ge(sem("W_hi"), c + 1)
                v.tensor_tensor(W_lo[:, q, :], act_e[:, c, :],
                                W_hi[:, q, :].bitcast(F32), ALU.subtract).then_inc(
                    sem("W_lo"), 1)

            ROUNDS = HALF // 4
            hot(0, 0, 0, 0)
            hot(1, 1, 1, 0)
            dve.wait_ge(sem("gelu"), HALF)
            with dve.Fori(0, ROUNDS - 1) as r:
                for q in range(4):
                    apply_gates(r * 4 + q, r * 4 + q, q, 0)
                    hot(r * 4 + q + 2, r * 4 + q + 2, q, 0)
            for q in range(4):
                n = HALF - 4 + q
                apply_gates(n, n, q, 0)
                hot(n + 2, (n + 2) % HALF, q, (n + 2) // HALF)
            dve.wait_ge(sem("gelu"), NKEYS)
            gated_lo(0, 0)
            gated_lo(1, 1)
            with dve.Fori(0, ROUNDS - 1) as r:
                for q in range(4):
                    gated_lo(r * 4 + q + 2, (q + 2) % 4)
                    apply_gates(r * 4 + q + HALF, r * 4 + q, q, 1)
                    hot(r * 4 + q + HALF + 2, r * 4 + q + 2, q, 1)
            for q in range(4):
                n = HALF - 4 + q
                if q < 2:
                    gated_lo(n + 2, q + 2)
                apply_gates(n + HALF, n, q, 1)
                if q < 2:
                    hot(n + HALF + 2, n + 2, q, 1)
            gated_lo(HALF, 0)
            gated_lo(HALF + 1, 1)
            with dve.Fori(ROUNDS, 2 * ROUNDS - 1) as r:
                for q in range(4):
                    gated_lo(r * 4 + q + 2, (q + 2) % 4)
            for q in range(2):
                gated_lo(NKEYS - 2 + q, q + 2)
            dve.wait_ge(sem("x_back"), 16)
            residual("v", XB)
            dve.wait_ge(sem("rows_in"), 16)
            for t in range(NT):
                row_rstd(t)
                for h in range(2):
                    c = slice(h * 512, (h + 1) * 512)
                    v.scalar_tensor_tensor(
                        out=X[:, t, c], in0=X[:, t, c], scalar=rstd[:, t:t + 1],
                        in1=rows[:, R_FINAL + h * 512:R_FINAL + (h + 1) * 512], op0=ALU.mult,
                        op1=ALU.mult).then_inc(sem("x_final"), 1)
            norms[0] += 1
            norm_T(2)

            for n in range(12):
                used(dve, FIRST["qkv_e"] + n)
                y, x = QKVF[:, n, :], col[n % 2]
                tap = [cols[:, C_CONV + 4 * n + j:C_CONV + 4 * n + j + 1] for j in range(4)]
                then(v.tensor_scalar(y, x[:, 0:SEQ], tap[3], None, ALU.mult))
                for back in range(1, 4):
                    then(v.scalar_tensor_tensor(out=y[:, back:], in0=x[:, 0:SEQ - back],
                                                scalar=tap[3 - back], in1=y[:, back:], op0=ALU.mult,
                                                op1=ALU.add), "conv" if back == 3 else "dve")
            def th(ap):
                return ap.rearrange("p (t h) -> p t h", t=NT)

            copies("tok", [m[:, t, :, :].rearrange("p h d -> p (h d)") for m in (Qt, Kt, Vt)
                           for t in range(NT)])
            dve.wait_ge(sem("ev_zba"), upto("ev_zba", 4))
            dve.wait_ge(sem("rows_in"), 16)
            ba = stat[:, 0:16].rearrange("p (t n) -> p t n", t=NT)
            x, e, u, ln = stat[:, 40:48], stat[:, 48:56], stat[:, 24:32], stat[:, 16:24]
            d, low, r = sq32[:, 0:8], sq32[:, 8:16], sq32[:, 16:24]
            then(v.tensor_tensor(th(x), ba[:, :, 4:8], over(rows[:, R_DT:R_DT + 4], [P, NT, 4], 1),
                                 ALU.add))
            then(v.scalar_tensor_tensor(out=e, in0=x, scalar=-1.0, in1=x, op0=ALU.mult,
                                        op1=ALU.min), "sp")
            dve.wait_ge(sem("sp_exp"), upto("sp_exp", 1))
            then(v.tensor_scalar(u, e, 1.0, None, ALU.add), "sp")
            then(v.tensor_scalar(d, u, 1.0, None, ALU.subtract))
            then(v.scalar_tensor_tensor(out=low, in0=d, scalar=0.0, in1=e, op0=ALU.is_equal,
                                        op1=ALU.mult))
            then(v.tensor_scalar(r, d, 1e-30, None, ALU.max))
            then(v.reciprocal(r, r))
            then(v.tensor_tensor(r, r, e, ALU.mult))
            dve.wait_ge(sem("sp_ln"), upto("sp_ln", 1))
            then(v.tensor_tensor(r, r, ln, ALU.mult))
            then(v.tensor_tensor(r, r, low, ALU.add))
            then(v.scalar_tensor_tensor(out=r, in0=x, scalar=0.0, in1=r, op0=ALU.max, op1=ALU.add))
            dve.wait_ge(sem("beta"), upto("beta", 2))
            then(v.tensor_scalar(r, r, -1.0, None, ALU.mult))
            then(v.tensor_tensor(th(stat[:, 16:24]), th(r), over(stat[:, 60:64], [P, NT, 4], 1),
                                 ALU.mult), "g_ready")
            dve.wait_ge(sem("masks"), 20)

            def groups(m):
                return m[:, :, :, :].rearrange("p t h d -> p (t h) d")

            def scale_groups(dst, src, s, name="dve"):
                then(v.tensor_tensor(groups(dst), groups(src), over(s, [P, 8, P], 2), ALU.mult),
                     name)

            dve.wait_ge(sem("l2_r"), upto("l2_r", 1))
            then(v.tensor_scalar(sq16[:, 0:8], sq16[:, 0:8], G_DK ** -0.5, None, ALU.mult))
            scale_groups(Kt, Kt, sq16[:, 8:16], "k_map")
            scale_groups(Qt, Qt, sq16[:, 0:8], "q_map")
            scale_groups(KBt, Kt, stat[:, 32:40], "kb_map")
            for t in range(NT):
                dve.wait_ge(sem("gcT"), upto("gcT", t + 1))
                then(v.tensor_copy(gc[:, 4 * t:4 * t + 4], mb[t][:, 0:4]), "gc")
                then(v.tensor_tensor(DG[:, t, :, :], over(ident[:, :], [P, 4, P], 1),
                                     over(gc[:, 4 * t:4 * t + 4], [P, 4, P], 2), ALU.mult), "diag")
            for t in range(NT):
                dve.wait_ge(sem("gcrow"), upto("gcrow", t + 1))
                row = acc[t][:, :].rearrange("p (h f) -> p h f", h=4)
                then(v.tensor_tensor(D0[:, t, :, :], row, over(gc[:, 4 * t:4 * t + 4], [P, 4, P], 2),
                                     ALU.subtract))
                then(v.tensor_scalar(decA[:, t, :, :], D0[:, t, :, :], 0.0, None, ALU.max), "gdiff")
                then(v.tensor_scalar(decAT[:, t, :, :], D0[:, t, :, :], 0.0, None, ALU.min), "gdiff")
                then(v.tensor_copy(gl[:, 8 * t:8 * t + 8].rearrange("p (c h) -> p c h", c=2),
                                   acc[t][:, :].rearrange("p (h c f) -> p c h f", h=4, c=2)
                                   [:, :, :, G_CH - 1]), "glast")
            for n in range(0, 8, 2):
                dve.wait_ge(sem("fT_T"), upto("fT_T", n + 1))
                then(v.tensor_copy(fT[:, n % 4, n // 4, :, :].rearrange("p h d -> p (h d)"),
                                   mb[0][:, :]), "fT_E")
            dve.wait_ge(sem("dec"), 4)
            for c in range(2):
                rr = slice(G_CH * c, G_CH * c + G_CH)
                then(v.tensor_copy(th(kdf[rr, :]), decAT[rr, :, :, G_CH * c + G_CH - 1]),
                     "kd_factor" if c else "dve")
            for dst, src, m in ((decA, decA, 0), (decATm, decAT, 1)):
                then(v.tensor_tensor(groups(dst), groups(src), over(masks[:, m, :], [P, 8, P], 1),
                                     ALU.mult))
            def four(m, t):
                return m[:, t, :, :]

            for s, (result, _, _, _) in enumerate(SOLVE):
                if s == MIX_AT + 1:
                    dve.wait_ge(sem("kd"), upto("kd", 1))
                    for t in range(NT):
                        dve.wait_ge(sem("mix"), upto("mix", t + 1))
                        for g in range(M_G):
                            c = slice(g * P, (g + 1) * P)
                            x = v.scalar_tensor_tensor(out=OC[:, t, c], in0=mb[t][:, c],
                                                       scalar=cols[:, C_BS + g:C_BS + g + 1],
                                                       in1=UV[:, t, c], op0=ALU.add, op1=ALU.mult)
                    then(x, "oc")
                if s == 2:
                    for y, n1 in ((YI, N1), (YIT, N1T)):
                        i = v.tensor_tensor(groups(y), over(ident[:, :], [P, 8, P], 1), groups(n1),
                                            ALU.subtract)
                        if y is YI:
                            go(i)
                    then(i, "y0")
                    dve.wait_ge(sem("dve"), counts["dve"])
                if s == GMLP_T_AT + 1:
                    stream_T("oc", range(2))
                if result in PLAIN:
                    continue
                if result == "qkT":
                    dve.wait_ge(sem("dec_q"), upto("dec_q", 1))
                for t in range(NT):
                    n = NT * s + t
                    dve.wait_ge(sem("sv"), n + 1)
                    src = (acc + col)[n % 6][:, :].rearrange("p (h f) -> p h f", h=4)
                    if result == "qkT":
                        then(v.tensor_tensor(four(qkT, t), src, four(decQ, t), ALU.mult), "sv_E")
                    elif result == "a":
                        then(v.tensor_tensor(four(N1, t), src, four(decA, t), ALU.mult), "sv_E")
                    elif result == "aT":
                        then(v.tensor_tensor(four(aT, t), src, four(decATm, t), ALU.mult))
                        then(v.tensor_tensor(four(N1T, t), four(aT, t),
                                             over(masks[:, 3, :], [P, 4, P], 1), ALU.mult), "sv_E")
                    else:
                        y = YIT if result.startswith("YT") else YI
                        if s in (11, 12):
                            then(v.tensor_tensor(four(L1T if s == 11 else L2T, t), four(aT, t),
                                                 over(masks[:, 4 if s == 11 else 5, :], [P, 4, P], 1),
                                                 ALU.mult))
                        if result.endswith("+"):
                            then(v.tensor_tensor(four(y, t), src, four(y, t), ALU.add), "sv_E")
                        else:
                            then(v.tensor_tensor(four(y, t), four(y, t), src, ALU.subtract), "sv_E")

            def head_norm(t):
                dve.wait_ge(sem("zg"), upto("zg", 1))
                dve.wait_ge(sem("o_r"), upto("o_r", t + 1))
                for h in range(G_H):
                    x = v.scalar_tensor_tensor(
                        out=OC[:, t, 512 + h * P:512 + (h + 1) * P], in0=Ot[:, t, h, :],
                        scalar=stat[:, 4 * t + h:4 * t + h + 1],
                        in1=Z[:, t, h * P:(h + 1) * P], op0=ALU.mult, op1=ALU.mult)
                then(x, "oc" if t else "dve")

            dve.wait_ge(sem("gl"), 2)
            dve.wait_ge(sem("sv_A"), solved(NT * len(SOLVE))[1])
            for c in range(SEQ // G_CH):
                t, rr = c // 2, slice(G_CH * (c % 2), G_CH * (c % 2) + G_CH)
                if c:
                    dve.wait_ge(sem("wS"), c)
                    then(v.tensor_tensor(Vn[rr, t, :, :], Ut[rr, t, :, :],
                                         col[0][rr, :].rearrange("p (h f) -> p h f", h=4),
                                         ALU.subtract), "v_new")
                else:
                    then(v.tensor_copy(Vn[rr, t, :, :], Ut[rr, t, :, :]), "v_new")
                if c < SEQ // G_CH - 1:
                    dve.wait_ge(sem("dS"), c + 1)
                    if c:
                        for h in range(G_H):
                            g = 8 * t + 4 * (c % 2) + h
                            then(v.scalar_tensor_tensor(
                                out=St[:, h, :], in0=St[:, h, :], scalar=gl[:, g:g + 1],
                                in1=mb[c % 2][:, h * P:(h + 1) * P], op0=ALU.mult, op1=ALU.add),
                                "state" if h == G_H - 1 else "dve")
                    else:
                        then(v.tensor_copy(St[:, :, :].rearrange("p h f -> p (h f)"), mb[0][:, :]),
                             "state")
                dve.wait_ge(sem("o_T"), c + 1)
                then(v.tensor_copy(Ot[rr, t, :, :],
                                   col[1][rr, :].rearrange("p (h f) -> p h f", h=4)), "o_E")
                if c == 2:
                    head_norm(0)
            head_norm(1)
            stream_T("oc", range(2, 4))
            residual("out_e")

            def mlp(layer):
                j0 = FIRST[f"mlp{layer}"]
                f0 = layer * D_FF // P

                def squares(blk, s):
                    dve.wait_ge(sem("square"), blk + 1 + f0)
                    v.tensor_copy(H_hi[:, s, :], H_q[:, s, :]).then_inc(sem("H_hi"), 1)
                    dve.wait_ge(sem("H_hi"), blk + 1 + f0)
                    v.tensor_tensor(H_lo[:, s, :], H_q[:, s, :], H_hi[:, s, :].bitcast(F32),
                                    ALU.subtract).then_inc(sem("H"), 1)

                squares(0, 0)
                squares(1, 1)
                with dve.Fori(0, MLP_ROUNDS) as r:
                    for s in range(2):
                        used(dve, j0 + 2 + 2 * s, r)
                        squares(2 * r + 2 + s, s)
                dve.wait_ge(sem("p_in"), 16 * (layer + 1))
                hi_lo(p_hi[:, :, :], p_lo[:, :, :], p_raw[:, :, :], "p_split")
                residual(f"mlp{layer}")

            def gated_projection(layer, n):
                norm_T(n, between=lambda: evac(f"ple{layer}", half(G2)))
                for b in range(5):
                    if b < 4:
                        dve.wait_ge(sem(f"ev_gate{layer}"), upto(f"ev_gate{layer}", b + 1))
                        t, c = b // 2, slice((b % 2) * 512, (b % 2 + 1) * 512)
                        go(v.tensor_tensor(G2[:, t, c], G2[:, t, c], GT[:, t, c], ALU.mult))
                    if b:
                        dve.wait_ge(sem("dve"), counts["dve"] - (b < 4))
                        t, c = (b - 1) // 2, slice(((b - 1) % 2) * 512, ((b - 1) % 2 + 1) * 512)
                        v.tensor_tensor(X[:, t, c], X[:, t, c], G2[:, t, c], ALU.add).then_inc(
                            sem(f"x_ple{layer}"), 1)

            norm_T(3)
            mlp(0)
            gated_projection(0, 4)

            norm_T(5)
            dve.wait_ge(sem("causal"), 6)
            dve.wait_ge(sem("iota"), 4)
            for h in range(C_H):
                then(v.scalar_tensor_tensor(out=ALIBI[:, h, :], in0=dist[:, :],
                                            scalar=-2.0 ** (-8.0 * (h + 1) / C_H), in1=causal1[:, :],
                                            op0=ALU.mult, op1=ALU.add))
            for n in range(2):
                lam = [rows[:, R_LAM + 64 * (2 * n + i):R_LAM + 64 * (2 * n + i + 1)]
                       for i in range(2)]
                then(v.tensor_tensor_reduce(SQ[:, 0, 0:64], lam[0], lam[1], 1.0, 0.0, ALU.mult,
                                            ALU.add, stat[:, n:n + 1]), "lam_dots")
            for m, (g, src, gain) in enumerate((("q1", Q1, R_QG), ("k1", K1, R_KG))):
                evac(g, half(src))
                x = src[:, :, :].rearrange("p t (n d) -> p (t n) d", d=C_DH)
                y = SQ[:, :, :].rearrange("p t (n d) -> p (t n) d", d=C_DH)
                then(v.tensor_tensor(y, x, x, ALU.mult))
                then(v.tensor_reduce(sq32[:, :], y, AX_X, ALU.add), "qk_ss")
                dve.wait_ge(sem("qk_root"), upto("qk_root", m + 1))
                then(v.reciprocal(sq32[:, :], sq32[:, :]))
                if m == 0:
                    then(v.tensor_scalar(sq32[:, :], sq32[:, :], C_DH ** -0.5, None, ALU.mult))
                then(v.tensor_tensor(x, x, over(sq32[:, :], [P, 32, C_DH], 2), ALU.mult))
                then(v.tensor_tensor(x, x, over(rows[:, gain:gain + C_DH], [P, 32, C_DH], 1),
                                     ALU.mult), "qk1")
            dve.wait_ge(sem("lam_exp"), upto("lam_exp", 1))
            then(v.tensor_scalar(stat[:, 4:5], stat[:, 2:3], stat[:, 3:4], LAM_INIT, ALU.subtract,
                                 ALU.add))
            evac("v1", half(V1))
            copies("qk1", [QKT[:, 2 * b:2 * b + 2, :].rearrange("p a s -> p (a s)")
                           for b in range(8)])

            def masked1(w):
                dve.wait_ge(sem("scores1"), w + 1)
                if w >= 2:
                    dve.wait_ge(sem("exp1"), w - 1)
                masked(S1[:, w % 2, :], col[w % 2], ALIBI[:, w // 2, :], mx1[:, w, :], 1.0,
                       "masked1")

            def heads_out1(part):
                for t in range(NT):
                    dve.wait_ge(sem("o1_r"), upto("o1_r", NT * part + t + 1))
                    for h in range(4):
                        i, c = 8 * part + 4 * t + h, (4 * part + h) * P
                        x = v.scalar_tensor_tensor(
                            out=O1[:, t, c:c + P], in0=acc[2 * t + part][:, h * P:(h + 1) * P],
                            scalar=sq16[:, i:i + 1], in1=rows[:, R_SG:R_SG + P], op0=ALU.mult,
                            op1=ALU.mult)
                then(x, "o1")

            masked1(0)
            masked1(1)
            for h in range(C_H):
                if h + 1 < C_H:
                    masked1(2 * h + 2)
                    masked1(2 * h + 3)
                dve.wait_ge(sem("exp1"), 2 * h + 2)
                s01 = sum1[:, 2 * h:2 * h + 2, :]
                then(v.reciprocal(s01, s01))
                then(v.tensor_scalar(sum1[:, 2 * h + 1, :], sum1[:, 2 * h + 1, :], stat[:, 4:5],
                                     None, ALU.mult))
                p0, p1 = PR1[:, (2 * h) % 4, :], PR1[:, (2 * h + 1) % 4, :]
                halves = ((0, P), (P, 3 * P))
                for t, (a, b) in enumerate(halves):
                    i = v.tensor_scalar(p1[:, a:b], p1[:, a:b], sum1[:, 2 * h + 1, t:t + 1], None,
                                        ALU.mult)
                    if t == 0:
                        go(i)
                then(i)
                for t, (a, b) in enumerate(halves):
                    i = v.scalar_tensor_tensor(out=p0[:, a:b], in0=p0[:, a:b],
                                               scalar=sum1[:, 2 * h, t:t + 1], in1=p1[:, a:b],
                                               op0=ALU.mult, op1=ALU.subtract)
                    if t == 0:
                        go(i)
                then(i, "attn1")
            heads_out1(0)
            heads_out1(1)
            stream_T("o1")
            residual("out_o")
            norm_T(6)
            mlp(1)
            gated_projection(1, 7)


def kernel(**inputs):
    import concourse.bacc as bacc
    from concourse.bass_utils import run_bass_kernel_spmd

    a = {k: np.ascontiguousarray(x) for k, x in inputs.items()}

    def col_form(w):
        k, n = w.shape
        return np.ascontiguousarray(w.reshape(k // P, P, n // P, P).transpose(2, 1, 0, 3)).reshape(
            n // P, P, k)

    def columns(v):
        return v.reshape(-1, P).T

    gains = [a["mix_norm_g"][0], a["ffn_norm_g"][0], a["ln_mix_e_2"][0], a["ln_mlp_2"][0],
             a["ln_ple_2"][0], a["ln_mix_o_2"][0], a["ln_mlp_2"][1], a["ln_ple_2"][1]]
    conv = a["gdn_conv_2"][0].reshape(4, 12, P).transpose(2, 1, 0).reshape(P, 48)
    w_in_e = a["w_in_e_2"][0]
    freqs = [np.float32(10000.0) ** (-np.arange(0, dim, 2, dtype=np.float32) / np.float32(dim))
             for dim in (A_DH, B_ROPE)]
    keys = np.stack([a["peer_sub_keys_1"][0], a["peer_sub_keys_2"][0]], 1)
    arrays = {
        "x": a["x"][0],
        "positions": a["positions"][0].reshape(NT, P).T,
        "freqs": np.concatenate(freqs).astype(np.float32)[None],
        "cols": np.concatenate([columns(g) for g in gains] + [
            columns(a["q_norm_g"][0]), columns(a["kv_norm_g"][0]), conv, a["gmlp_bs_2"][0].T], 1),
        "rows": np.concatenate([
            a["final_norm_g"], a["gmlp_v_gain_2"][0], a["gdn_out_gain_2"][0], a["attn_q_gain_2"][0],
            a["attn_k_gain_2"][0], a["attn_sub_gain_2"][0], a["diff_lambda_2"][0].reshape(-1),
            a["gdn_a_log_2"][0], a["gdn_dt_bias_2"][0]])[None],
        "w_in": a["w_in"][0],
        "w_q_up": a["w_q_up"][0],
        "w_kv_up": a["w_kv_up"][0],
        "w_branch_a": a["w_branch_a"][0],
        "w_branch_b": a["w_branch_b"][0],
        "w_out": a["w_out"][0],
        "w_query": col_form(a["w_peer_query"][0]),
        "sub_keys": keys.transpose(3, 0, 1, 2).reshape(P, 16, NKEYS),
        "expert_u": col_form(a["peer_expert_u"][0].T),
        "expert_v": a["peer_expert_v"][0],
        "w_in_e": w_in_e,
        "w_qkv_e": col_form(w_in_e[:, 1024:2560]),
        "gmlp_w": a["gmlp_ws_2"][0].transpose(2, 0, 1),
        "w_out_e": a["w_out_e_2"][0],
        "w_qkv_o": a["w_qkv_o_2"][0],
        "w_out_o": a["w_out_o_2"][0],
        "p": a["p_2"][:, 0].transpose(0, 2, 1).reshape(2, PLE // P, P, SEQ).transpose(0, 2, 1, 3),
    }
    for n in range(2):
        arrays[f"w_mlp1_{n}"] = col_form(a["w_mlp1_2"][n])
        arrays[f"w_mlp2_{n}"] = a["w_mlp2_2"][n]
        arrays[f"w_gate_{n}"] = a["w_ple_gate_2"][n]
        arrays[f"w_ple_{n}"] = a["w_ple_proj_2"][n]
    arrays = {k: np.ascontiguousarray(x) for k, x in arrays.items()}

    nc = bacc.Bacc("TRN2", target_bir_lowering=False, num_devices=1)
    feeds = {f"in_{k}": x for k, x in arrays.items()}
    ins = {k: nc.dram_tensor(f"in_{k}", x.shape, mybir.dt.from_np(x.dtype),
                             kind="ExternalInput").ap() for k, x in arrays.items()}
    out = nc.dram_tensor("out_x", [SEQ, D], F32, kind="ExternalOutput").ap()
    program(nc, ins, out)
    r = run_bass_kernel_spmd(nc, [feeds], core_ids=[0])
    return r.results[0]["out_x"].reshape(1, SEQ, D)
```
